# Optimizing a Trainium2 kernel written in Bass

```python
import math
import jax, jax.numpy as jnp
from jax import lax
import numpy as np

D_MODEL = 1024
BATCH = 1
SEQ = 256
DEPTH = 2

CHUNK = 64
Q_BLOCK = 128
EPS = 1e-6
MAX_OFFSET = 4096

HG_HEADS = 4
HG_DK = 128
HG_DV = 128
HG_WIDTH = HG_HEADS * HG_DV

MLA_HEADS = 8
MLA_NOPE = 64
MLA_ROPE = 32
MLA_V = 64
MLA_Q_LORA = 384
MLA_KV_LORA = 256
MLA_DQK = MLA_NOPE + MLA_ROPE
MLA_WIDTH = MLA_HEADS * MLA_V
ROPE_BASE = 10000.0

N_EXPERTS = 16
N_GROUPS = 4
EXPERTS_PER_GROUP = N_EXPERTS // N_GROUPS
TOPK_GROUPS = 1
TOP_K = 2
D_EXPERT = 512

IN_SIZES = (HG_HEADS * HG_DK,
            HG_HEADS * HG_DK,
            HG_HEADS * HG_DV,
            HG_WIDTH,
            MLA_Q_LORA,
            MLA_KV_LORA,
            MLA_ROPE,
            2 * D_MODEL)
IN_COLS = int(sum(IN_SIZES))
IN_SPLITS = tuple(int(v) for v in np.cumsum(IN_SIZES)[:-1])


def rmsnorm(x, g):
    xf = x.astype(jnp.float32)
    y = xf * lax.rsqrt(jnp.mean(xf * xf, axis=-1, keepdims=True) + EPS)
    return (y * g.astype(jnp.float32)).astype(x.dtype)

def rotary(x, pos):
    half = x.shape[-1] // 2
    inv = ROPE_BASE ** (-jnp.arange(half, dtype=jnp.float32) / half)
    ang = pos.astype(jnp.float32)[..., None] * inv
    cos = jnp.cos(ang)[:, :, None, :]
    sin = jnp.sin(ang)[:, :, None, :]
    xf = x.astype(jnp.float32)
    x1, x2 = xf[..., :half], xf[..., half:]
    return jnp.concatenate([x1 * cos - x2 * sin, x1 * sin + x2 * cos], -1).astype(x.dtype)

def hgrn2_mix(q, f_logit, v, lb):
    B, S = q.shape[0], q.shape[1]
    nc = S // CHUNK
    lbh = lb.astype(jnp.float32).reshape(HG_HEADS, HG_DK)
    f = lbh + (1.0 - lbh) * jax.nn.sigmoid(f_logit.astype(jnp.float32))
    log_f = jnp.log(f)
    k = 1.0 - f
    qf = jax.nn.silu(q.astype(jnp.float32)) * (HG_DK ** -0.5)
    vf = v.astype(jnp.float32)

    def to_chunks(t):
        return t.reshape(B, nc, CHUNK, HG_HEADS, t.shape[-1]).transpose(1, 0, 3, 2, 4)

    qc, kc, vc, gc = to_chunks(qf), to_chunks(k), to_chunks(vf), to_chunks(log_f)
    causal = jnp.tril(jnp.ones((CHUNK, CHUNK), dtype=bool))[:, :, None]

    def step(state, inp):
        qb, kb, vb, gb = inp
        b = jnp.cumsum(gb, axis=2)
        rel = b[:, :, :, None, :] - b[:, :, None, :, :]
        decay = jnp.exp(jnp.where(causal, rel, -jnp.inf))
        attn = jnp.einsum('bhtd,bhtsd,bhsd->bhts', qb, decay, kb)
        intra = jnp.einsum('bhts,bhsv->bhtv', attn, vb)
        inter = jnp.einsum('bhtd,bhdv->bhtv', qb * jnp.exp(b), state)
        b_last = b[:, :, -1:, :]
        k_dec = kb * jnp.exp(b_last - b)
        new_state = state * jnp.exp(b_last[:, :, 0, :, None]) + jnp.einsum('bhsd,bhsv->bhdv', k_dec, vb)
        return new_state, intra + inter

    state0 = jnp.zeros((B, HG_HEADS, HG_DK, HG_DV), jnp.float32)
    _, out = lax.scan(step, state0, (qc, kc, vc, gc))
    return out.transpose(1, 0, 3, 2, 4).reshape(B, S, HG_HEADS, HG_DV)

def mla_mix(c_q, c_kv, k_rope, pos, q_norm_g, w_q_up, kv_norm_g, w_kv_up):
    B, S = c_q.shape[0], c_q.shape[1]
    q = (rmsnorm(c_q, q_norm_g) @ w_q_up).reshape(B, S, MLA_HEADS, MLA_DQK)
    q = jnp.concatenate([q[..., :MLA_NOPE], rotary(q[..., MLA_NOPE:], pos)], -1)
    kv = (rmsnorm(c_kv, kv_norm_g) @ w_kv_up).reshape(B, S, MLA_HEADS, MLA_NOPE + MLA_V)
    k_nope, v = kv[..., :MLA_NOPE], kv[..., MLA_NOPE:]
    k_pe = rotary(k_rope[:, :, None, :], pos)
    k = jnp.concatenate([k_nope, jnp.broadcast_to(k_pe, (B, S, MLA_HEADS, MLA_ROPE)).astype(k_nope.dtype)], -1)
    scale = MLA_DQK ** -0.5
    nb = S // Q_BLOCK
    qb = q.reshape(B, nb, Q_BLOCK, MLA_HEADS, MLA_DQK).transpose(1, 0, 2, 3, 4)
    key_chunk = jnp.arange(S) // CHUNK

    def block(args):
        qblk, start = args
        q_chunk = (start + jnp.arange(Q_BLOCK)) // CHUNK
        s = jnp.einsum('bqhd,bkhd->bhqk', qblk, k, preferred_element_type=jnp.float32) * scale
        mask = key_chunk[None, :] <= q_chunk[:, None]
        p = jax.nn.softmax(jnp.where(mask, s, -jnp.inf), axis=-1).astype(v.dtype)
        return jnp.einsum('bhqk,bkhd->bqhd', p, v)

    out = lax.map(block, (qb, jnp.arange(nb, dtype=jnp.int32) * Q_BLOCK))
    return out.transpose(1, 0, 2, 3, 4).reshape(B, S, MLA_WIDTH)

def token_mix(h, pos, w_in, lb, hg_norm_g, q_norm_g, w_q_up, kv_norm_g, w_kv_up, w_br_a, w_br_b, w_out):
    B, S, D = h.shape
    proj = h @ w_in
    hq, hf, hi, hgate, cq, ckv, kr, gates = jnp.split(proj, IN_SPLITS, axis=-1)
    o_a = hgrn2_mix(hq.reshape(B, S, HG_HEADS, HG_DK), hf.reshape(B, S, HG_HEADS, HG_DK),
                    hi.reshape(B, S, HG_HEADS, HG_DV), lb)
    o_a = rmsnorm(o_a, hg_norm_g.reshape(HG_HEADS, HG_DV)).reshape(B, S, HG_WIDTH)
    o_a = (o_a * jax.nn.silu(hgate.astype(jnp.float32))).astype(h.dtype)
    y_a = o_a @ w_br_a
    y_b = mla_mix(cq, ckv, kr, pos, q_norm_g, w_q_up, kv_norm_g, w_kv_up) @ w_br_b
    g = jax.nn.sigmoid(gates.astype(jnp.float32))
    g_a, g_b = g[..., :D], g[..., D:]
    merged = (g_a * y_a.astype(jnp.float32) + g_b * y_b.astype(jnp.float32)).astype(h.dtype)
    return merged @ w_out

def grouped_moe(h, w_router, router_bias, w_gate, w_up, w_down):
    B, S, D = h.shape
    t = h.reshape(-1, D)
    scores = jax.nn.sigmoid((t @ w_router).astype(jnp.float32))
    biased = (scores + router_bias.astype(jnp.float32)).reshape(-1, N_GROUPS, EXPERTS_PER_GROUP)
    group_score = lax.top_k(biased, 2)[0].sum(-1)
    _, gidx = lax.top_k(group_score, TOPK_GROUPS)
    gmask = jax.nn.one_hot(gidx, N_GROUPS, dtype=jnp.float32).sum(-2) > 0
    masked = jnp.where(gmask[:, :, None], biased, -jnp.inf).reshape(-1, N_EXPERTS)
    _, eidx = lax.top_k(masked, TOP_K)
    sel = jnp.take_along_axis(scores, eidx, axis=-1)
    w = sel / sel.sum(-1, keepdims=True)
    combine = (jax.nn.one_hot(eidx, N_EXPERTS, dtype=jnp.float32) * w[..., None]).sum(-2)
    y = jnp.zeros(t.shape, jnp.float32)
    for e in range(N_EXPERTS):
        he = jax.nn.silu(t @ w_gate[e]) * (t @ w_up[e])
        y = y + combine[:, e:e + 1] * (he @ w_down[e]).astype(jnp.float32)
    return y.astype(h.dtype).reshape(B, S, D)

def first_inputs(seed: int = 0) -> dict:
    key = jax.random.key(seed)
    ks = jax.random.split(key, 24)
    f32 = jnp.float32
    D = D_MODEL

    def nrm(k, shape, scale):
        return jax.random.normal(k, shape, f32) * scale

    positions = (jax.random.randint(ks[2], (BATCH, 1), 0, MAX_OFFSET, dtype=jnp.int32)
                 + jnp.arange(SEQ, dtype=jnp.int32)[None, :]).astype(jnp.int32)
    return {
        "x": nrm(ks[0], (BATCH, SEQ, D), 1.0),
        "c": nrm(ks[1], (BATCH, D), 1.0),
        "positions": positions,
        "ada_w": nrm(ks[3], (DEPTH, D, 6 * D), 0.5 * D ** -0.5),
        "ada_b": nrm(ks[4], (DEPTH, 6 * D), 0.02),
        "norm1_g": 1.0 + nrm(ks[5], (DEPTH, D), 0.02),
        "w_in": nrm(ks[6], (DEPTH, D, IN_COLS), D ** -0.5),
        "hg_lb_logits": nrm(ks[7], (DEPTH, HG_HEADS * HG_DK), 1.0),
        "hg_norm_g": 1.0 + nrm(ks[8], (DEPTH, HG_WIDTH), 0.02),
        "q_norm_g": 1.0 + nrm(ks[9], (DEPTH, MLA_Q_LORA), 0.02),
        "w_q_up": nrm(ks[10], (DEPTH, MLA_Q_LORA, MLA_HEADS * MLA_DQK), MLA_Q_LORA ** -0.5),
        "kv_norm_g": 1.0 + nrm(ks[11], (DEPTH, MLA_KV_LORA), 0.02),
        "w_kv_up": nrm(ks[12], (DEPTH, MLA_KV_LORA, MLA_HEADS * (MLA_NOPE + MLA_V)), MLA_KV_LORA ** -0.5),
        "w_br_a": nrm(ks[13], (DEPTH, HG_WIDTH, D), HG_WIDTH ** -0.5),
        "w_br_b": nrm(ks[14], (DEPTH, MLA_WIDTH, D), MLA_WIDTH ** -0.5),
        "w_out": nrm(ks[15], (DEPTH, D, D), D ** -0.5),
        "norm2_g": 1.0 + nrm(ks[16], (DEPTH, D), 0.02),
        "w_router": nrm(ks[17], (D, N_EXPERTS), D ** -0.5),
        "router_bias": nrm(ks[18], (N_EXPERTS,), 0.01),
        "w_gate": nrm(ks[19], (DEPTH, N_EXPERTS, D, D_EXPERT), D ** -0.5),
        "w_up": nrm(ks[20], (DEPTH, N_EXPERTS, D, D_EXPERT), D ** -0.5),
        "w_down": nrm(ks[21], (DEPTH, N_EXPERTS, D_EXPERT, D), D_EXPERT ** -0.5),
        "final_g": 1.0 + nrm(ks[22], (D,), 0.02),
    }

def first_block(x, c, positions, ada_w, ada_b, norm1_g, w_in, hg_lb_logits, hg_norm_g,
              q_norm_g, w_q_up, kv_norm_g, w_kv_up, w_br_a, w_br_b, w_out, norm2_g,
              w_router, router_bias, w_gate, w_up, w_down, final_g):
    D = D_MODEL
    lb_soft = jax.nn.softmax(hg_lb_logits.astype(jnp.float32), axis=0)
    lb_all = jnp.cumsum(lb_soft, axis=0) - lb_soft[0:1]
    c_act = jax.nn.silu(c)
    for l in range(DEPTH):
        mod = c_act @ ada_w[l] + ada_b[l]
        sh1, sc1, g1 = mod[:, None, 0:D], mod[:, None, D:2 * D], mod[:, None, 2 * D:3 * D]
        sh2, sc2, g2 = mod[:, None, 3 * D:4 * D], mod[:, None, 4 * D:5 * D], mod[:, None, 5 * D:6 * D]
        h = rmsnorm(x, norm1_g[l]) * (1.0 + sc1) + sh1
        x = x + g1 * token_mix(h, positions, w_in[l], lb_all[l], hg_norm_g[l], q_norm_g[l], w_q_up[l],
                               kv_norm_g[l], w_kv_up[l], w_br_a[l], w_br_b[l], w_out[l])
        h = rmsnorm(x, norm2_g[l]) * (1.0 + sc2) + sh2
        x = x + g2 * grouped_moe(h, w_router, router_bias, w_gate[l], w_up[l], w_down[l])
    return rmsnorm(x, final_g)


LEFT_CHUNKS = 8
BAND_CHUNKS = LEFT_CHUNKS + 1
N_HEADS = 16
HEAD_DIM = D_MODEL // N_HEADS
REL_CLIP = 128
LRU_WIDTH = ((4 * D_MODEL // 3 + 127) // 128) * 128
N_LRU_BLOCKS = 16
LRU_BLOCK = LRU_WIDTH // N_LRU_BLOCKS
LRU_C = 8.0
CONV_WIDTH = 4
D_FF = 4 * D_MODEL
N_A_LAYERS = DEPTH // 2
N_B_LAYERS = DEPTH - N_A_LAYERS


def rms_norm(x, g):
    xf = x.astype(jnp.float32)
    y = xf * lax.rsqrt(jnp.mean(xf * xf, axis=-1, keepdims=True) + EPS)
    return (y * g.astype(jnp.float32)).astype(x.dtype)

def modulate(x, shift, scale):
    return x * (1 + scale[:, None, :]) + shift[:, None, :]

def causal_depthwise_conv(x, w, b):
    y = lax.conv_general_dilated(
        x, w[:, None, :].astype(x.dtype), window_strides=(1,),
        padding=[(CONV_WIDTH - 1, 0)],
        dimension_numbers=("NWC", "WIO", "NWC"),
        feature_group_count=x.shape[-1])
    return y + b

def rg_lru(x, w_a, b_a, w_x, b_x, lam):
    bsz, s, w = x.shape
    xb = x.reshape(bsz, s, N_LRU_BLOCKS, LRU_BLOCK)
    r = jax.nn.sigmoid(jnp.einsum("bsnd,nde->bsne", xb, w_a).reshape(bsz, s, w) + b_a)
    i = jax.nn.sigmoid(jnp.einsum("bsnd,nde->bsne", xb, w_x).reshape(bsz, s, w) + b_x)
    log_a = (-LRU_C * r.astype(jnp.float32)) * jax.nn.softplus(-lam.astype(jnp.float32))
    a = jnp.exp(log_a)
    mult = jnp.sqrt(-jnp.expm1(2.0 * log_a))
    u = mult * (i * x).astype(jnp.float32)

    def combine(left, right):
        a_l, b_l = left
        a_r, b_r = right
        return a_r * a_l, a_r * b_l + b_r

    _, h = lax.associative_scan(combine, (a, u), axis=1)
    return h.astype(x.dtype)

def recurrent_mixer(hn, w_in, conv_w, conv_b, gate_a_w, gate_a_b, gate_x_w, gate_x_b, lam, w_out):
    z = hn @ w_in
    gate, xr = jnp.split(z, 2, axis=-1)
    xr = causal_depthwise_conv(xr, conv_w, conv_b)
    y = rg_lru(xr, gate_a_w, gate_a_b, gate_x_w, gate_x_b, lam)
    return (y * jax.nn.gelu(gate)) @ w_out

def shared_kv(h, c_act, kv_norm_g, kv_ada_w, kv_ada_b, kv_w, k_norm_g):
    bsz, s, _ = h.shape
    shift, scale = jnp.split(c_act @ kv_ada_w + kv_ada_b, 2, axis=-1)
    hn = modulate(rms_norm(h, kv_norm_g), shift, scale)
    k, v = jnp.split(hn @ kv_w, 2, axis=-1)
    k = rms_norm(k.reshape(bsz, s, N_HEADS, HEAD_DIM), k_norm_g)
    v = v.reshape(bsz, s, N_HEADS, HEAD_DIM)
    pad = ((0, 0), (LEFT_CHUNKS * CHUNK, 0), (0, 0), (0, 0))
    return jnp.pad(k, pad), jnp.pad(v, pad)

def chunk_attention(hn, w_q, q_norm_g, rel_bias, w_o, k_pad, v_pad):
    bsz, s, d = hn.shape
    n_chunks = s // CHUNK
    band = BAND_CHUNKS * CHUNK
    left = LEFT_CHUNKS * CHUNK
    q = rms_norm((hn @ w_q).reshape(bsz, s, N_HEADS, HEAD_DIM), q_norm_g)
    q_chunks = q.reshape(bsz, n_chunks, CHUNK, N_HEADS, HEAD_DIM).transpose(1, 0, 2, 3, 4)
    rel = jnp.arange(CHUNK)[:, None] - (jnp.arange(band)[None, :] - left)
    rel_idx = jnp.clip(rel, -REL_CLIP, REL_CLIP) + REL_CLIP
    bias = rel_bias[:, rel_idx].astype(jnp.float32)
    scale = HEAD_DIM ** -0.5

    def one_chunk(args):
        qc, ci = args
        start = ci * CHUNK
        kc = lax.dynamic_slice_in_dim(k_pad, start, band, axis=1)
        vc = lax.dynamic_slice_in_dim(v_pad, start, band, axis=1)
        sc = jnp.einsum("bqhd,bkhd->bhqk", qc, kc,
                        preferred_element_type=jnp.float32) * scale + bias
        valid = (start - left + jnp.arange(band)) >= 0
        sc = jnp.where(valid[None, None, None, :], sc, -1e30)
        p = jax.nn.softmax(sc, axis=-1).astype(vc.dtype)
        return jnp.einsum("bhqk,bkhd->bqhd", p, vc)

    out = lax.map(one_chunk, (q_chunks, jnp.arange(n_chunks)))
    out = out.transpose(1, 0, 2, 3, 4).reshape(bsz, s, d)
    return out @ w_o

def sqrelu_mlp(hn, w1, w2):
    return jnp.square(jax.nn.relu(hn @ w1)) @ w2

def second_inputs(seed: int = 0) -> dict:
    key = jax.random.key(seed)
    ks = jax.random.split(key, 32)
    f32 = jnp.float32
    D, W = D_MODEL, LRU_WIDTH

    def nrm(k, shape, fan_in):
        return jax.random.normal(k, shape, f32) * (fan_in ** -0.5)

    u = jax.random.uniform(ks[10], (N_A_LAYERS, W), f32, 0.9, 0.999)
    a0 = u ** (1.0 / LRU_C)
    lru_lambda = jnp.log(a0) - jnp.log1p(-a0)
    return {
        "x": jax.random.normal(ks[0], (BATCH, SEQ, D), f32),
        "c": jax.random.normal(ks[1], (BATCH, D), f32),
        "ada_w": nrm(ks[2], (DEPTH, D, 6 * D), D),
        "ada_b": 0.02 * jax.random.normal(ks[3], (DEPTH, 6 * D), f32),
        "norm1_g": 1.0 + 0.05 * jax.random.normal(ks[4], (DEPTH, D), f32),
        "norm2_g": 1.0 + 0.05 * jax.random.normal(ks[5], (DEPTH, D), f32),
        "mlp_w1": nrm(ks[6], (DEPTH, D, D_FF), D),
        "mlp_w2": nrm(ks[7], (DEPTH, D_FF, D), D_FF),
        "lru_w_in": nrm(ks[8], (N_A_LAYERS, D, 2 * W), D),
        "lru_conv_w": nrm(ks[9], (N_A_LAYERS, CONV_WIDTH, W), CONV_WIDTH),
        "lru_conv_b": 0.02 * jax.random.normal(ks[11], (N_A_LAYERS, W), f32),
        "lru_gate_a_w": nrm(ks[12], (N_A_LAYERS, N_LRU_BLOCKS, LRU_BLOCK, LRU_BLOCK), LRU_BLOCK),
        "lru_gate_a_b": 0.02 * jax.random.normal(ks[13], (N_A_LAYERS, W), f32),
        "lru_gate_x_w": nrm(ks[14], (N_A_LAYERS, N_LRU_BLOCKS, LRU_BLOCK, LRU_BLOCK), LRU_BLOCK),
        "lru_gate_x_b": 0.02 * jax.random.normal(ks[15], (N_A_LAYERS, W), f32),
        "lru_lambda": lru_lambda,
        "lru_w_out": nrm(ks[16], (N_A_LAYERS, W, D), W),
        "kv_norm_g": 1.0 + 0.05 * jax.random.normal(ks[17], (D,), f32),
        "kv_ada_w": nrm(ks[18], (D, 2 * D), D),
        "kv_ada_b": 0.02 * jax.random.normal(ks[19], (2 * D,), f32),
        "kv_w": nrm(ks[20], (D, 2 * D), D),
        "k_norm_g": 1.0 + 0.05 * jax.random.normal(ks[21], (HEAD_DIM,), f32),
        "attn_w_q": nrm(ks[22], (N_B_LAYERS, D, D), D),
        "q_norm_g": 1.0 + 0.05 * jax.random.normal(ks[23], (N_B_LAYERS, HEAD_DIM), f32),
        "rel_bias": 0.5 * jax.random.normal(ks[24], (N_B_LAYERS, N_HEADS, 2 * REL_CLIP + 1), f32),
        "attn_w_o": nrm(ks[25], (N_B_LAYERS, D, D), D),
    }

def second_block(x, c, ada_w, ada_b, norm1_g, norm2_g, mlp_w1, mlp_w2,
              lru_w_in, lru_conv_w, lru_conv_b, lru_gate_a_w, lru_gate_a_b,
              lru_gate_x_w, lru_gate_x_b, lru_lambda, lru_w_out,
              kv_norm_g, kv_ada_w, kv_ada_b, kv_w, k_norm_g,
              attn_w_q, q_norm_g, rel_bias, attn_w_o):
    c_act = jax.nn.silu(c)
    h = x
    k_pad = None
    v_pad = None
    for layer in range(DEPTH):
        mod = c_act @ ada_w[layer] + ada_b[layer]
        sh1, sc1, g1, sh2, sc2, g2 = jnp.split(mod, 6, axis=-1)
        hn = modulate(rms_norm(h, norm1_g[layer]), sh1, sc1)
        if layer < N_A_LAYERS:
            y = recurrent_mixer(hn, lru_w_in[layer], lru_conv_w[layer], lru_conv_b[layer],
                                lru_gate_a_w[layer], lru_gate_a_b[layer],
                                lru_gate_x_w[layer], lru_gate_x_b[layer],
                                lru_lambda[layer], lru_w_out[layer])
        else:
            j = layer - N_A_LAYERS
            y = chunk_attention(hn, attn_w_q[j], q_norm_g[j], rel_bias[j], attn_w_o[j],
                                k_pad, v_pad)
        h = h + g1[:, None, :] * y
        hn = modulate(rms_norm(h, norm2_g[layer]), sh2, sc2)
        h = h + g2[:, None, :] * sqrelu_mlp(hn, mlp_w1[layer], mlp_w2[layer])
        if layer == N_A_LAYERS - 1:
            k_pad, v_pad = shared_kv(h, c_act, kv_norm_g, kv_ada_w, kv_ada_b, kv_w, k_norm_g)
    return h


def setup_inputs(seed=0):
    out = dict(first_inputs(seed))
    for name, value in second_inputs(seed + 1).items():
        if name != "x":
            out[name + "_2"] = value
    return out


def reference(
    x, c, positions, ada_w, ada_b, norm1_g, w_in, hg_lb_logits, hg_norm_g, q_norm_g, w_q_up,
    kv_norm_g, w_kv_up, w_br_a, w_br_b, w_out, norm2_g, w_router, router_bias, w_gate, w_up,
    w_down, final_g, c_2, ada_w_2, ada_b_2, norm1_g_2, norm2_g_2, mlp_w1_2, mlp_w2_2,
    lru_w_in_2, lru_conv_w_2, lru_conv_b_2, lru_gate_a_w_2, lru_gate_a_b_2, lru_gate_x_w_2,
    lru_gate_x_b_2, lru_lambda_2, lru_w_out_2, kv_norm_g_2, kv_ada_w_2, kv_ada_b_2, kv_w_2,
    k_norm_g_2, attn_w_q_2, q_norm_g_2, rel_bias_2, attn_w_o_2,
):
    x = first_block(
        x, c, positions, ada_w, ada_b, norm1_g, w_in, hg_lb_logits, hg_norm_g, q_norm_g, w_q_up,
        kv_norm_g, w_kv_up, w_br_a, w_br_b, w_out, norm2_g, w_router, router_bias, w_gate, w_up,
        w_down, final_g,
    )
    return second_block(
        x, c_2, ada_w_2, ada_b_2, norm1_g_2, norm2_g_2, mlp_w1_2, mlp_w2_2, lru_w_in_2,
        lru_conv_w_2, lru_conv_b_2, lru_gate_a_w_2, lru_gate_a_b_2, lru_gate_x_w_2,
        lru_gate_x_b_2, lru_lambda_2, lru_w_out_2, kv_norm_g_2, kv_ada_w_2, kv_ada_b_2, kv_w_2,
        k_norm_g_2, attn_w_q_2, q_norm_g_2, rel_bias_2, attn_w_o_2,
    )


_drawn_inputs = setup_inputs


def setup_inputs(seed=0):
    import zlib

    import numpy as np

    out = dict(_drawn_inputs(seed))
    spreads = {}
    factors = {'norm1_g': 4.376,
     'hg_lb_logits': 4.016,
     'hg_norm_g': 3.82,
     'q_norm_g': 4.455,
     'kv_norm_g': 5.911,
     'final_g': 2.854,
     'lru_gate_a_b_2': 8.0,
     'lru_gate_x_b_2': 8.0,
     'kv_norm_g_2': 6.421,
     'kv_ada_b_2': 8.0,
     'k_norm_g_2': 8.0,
     'q_norm_g_2': 8.0,
     'rel_bias_2': 3.052}
    for name, (base, spread) in spreads.items():
        noise = np.random.default_rng([zlib.crc32(name.encode()), seed]).standard_normal(out[name].shape)
        drawn = base * np.exp(spread * noise) if base else spread * noise
        out[name] = __import__('jax').numpy.asarray(drawn.astype(out[name].dtype))
    for name, factor in factors.items():
        out[name] = (out[name] * factor).astype(out[name].dtype)
    return out
```

```python
from contextlib import ExitStack

import numpy as np

import concourse.bass as bass
from concourse import mybir

ALU = mybir.AluOpType
ACT = mybir.ActivationFunctionType
AX = mybir.AxisListType.X
F32 = mybir.dt.float32
I32 = mybir.dt.int32

P = 128
D = 1024
T = 256
KT = D // P
TT = T // P
EPS = 1e-6
HH, DK = 4, 128
NH, NOPE, ROPE, VD = 8, 64, 32, 64
DQK = NOPE + ROPE
QL, KVL = 384, 256
NE, NG, DE = 16, 4, 512
EG = NE // NG
LW, LN = 1408, 16
LB = LW // LN
NH2, HD = 16, 64
FF = 4096
SLOTS, SLOT = 6, 4096
MODS = 6 * KT
CH = 384
LEVELS = [1, 2, 4, 8, 16, 32, 64]
NEG = -1e30
TWO_PI = 2 * np.pi
C1 = 6.28125
C2 = float(np.float32(np.round((TWO_PI - C1) * 2**22) / 2**22))
C3 = float(TWO_PI - C1 - C2)
MAGIC = 12582912.0

COLS = {}


def _cols():
    at = 0
    for name, n in [("layer", 2 * 25), ("lb", 2 * HH), ("ada_b", 4 * MODS), ("kv_ada_b", 2 * KT),
                    ("c", 2 * KT), ("final_g", KT), ("n1g2", 2 * KT), ("n2g2", 2 * KT),
                    ("kvng2", KT), ("kng", 1), ("qng", 1), ("conv_w", 4 * LN), ("conv_b", LN),
                    ("ba", LN), ("bx", LN), ("lam", LN)]:
        COLS[name] = (at, n)
        at += n
    return at


NCOLS = _cols()
N1G, HGN, QNG, KVNG, N2G, LP = 0, 8, 12, 15, 17, 25

CONST = {}


def _const():
    at = 0
    for name, n in [("ident", P), ("ones", P), ("heads", P), ("turn", DQK), ("pair", 8 * P),
                    ("future", 2 * P), ("freq", 1)]:
        CONST[name] = (at, n)
        at += n
    return at


NCONST = _const()


UNITS = [("w_in", D, 512, 512), ("w_in", D, 0, 512), ("w_in", D, 1024, 512), ("w_in", D, 1536, 512),
         ("w_in", D, 2048, QL), ("w_in", D, 2432, KVL + ROPE)]
UNITS += [("w_in", D, 2720 + 512 * i, 512) for i in range(4)]
UNITS += [("w_q_up", QL, 0, NH * DQK), ("w_kv_up", KVL, 0, NH * (NOPE + VD)),
          ("w_br_a", HH * DK, 0, D), ("w_br_b", NH * VD, 0, D),
          ("w_out", D, 0, 512), ("w_out", D, 512, 512)]
LAST_USE = ["f1", "q1", "v1", "hgate1", "cq1", "kr", "gates1", "gates3", "gates5", "gates7",
            "q up3", "v up1", "ya3", "yb3", "out1", "out3"]
STATIC_IN = [len(range(s, len(UNITS), SLOTS)) for s in range(SLOTS)]
PER_LAYER = [n + NE // 2 for n in STATIC_IN]
LAST_USE_OF_SLOT = [LAST_USE[s + SLOTS * (STATIC_IN[s] - 1)] for s in range(SLOTS)]


class Steps:

    def __init__(self, sem, names):
        assert len(set(names)) == len(names)
        self.sem, self.names, self.n, self.given = sem, names, len(names), 0

    def one(self, name):
        assert self.names[self.given] == name, (self.names[self.given], name)
        self.given += 1
        return 1

    def at(self, name, turn=0):
        return turn * self.n + self.names.index(name) + 1


class Turns(Steps):

    def __init__(self, sem, names, first):
        super().__init__(sem, names)
        self.first = first

    def one(self, name):
        assert self.names[self.given % self.n] == name, (self.names[self.given % self.n], name)
        self.given += 1
        return 1

    def at(self, name, turn=0):
        return turn * self.n + (self.first + self.names.index(name) + 1)


FILL = ["hgate0", "hgate1", "cq0", "cq1", "ckv", "kr", "gates0", "gates1", "gates2",
        "gates3", "gates4", "gates5", "gates6", "gates7"]
MASKED = ["diag"] + [f"L{n}" for n in LEVELS]


def pe_jobs():
    jobs = [("norm1", "act")] + [(n, "act") for n in ("f0", "f1", "q0", "q1", "v0", "v1")]
    fill = list(FILL)
    for name in MASKED:
        jobs += [(f"{name} t0", "dve"), (f"{name} t1", "dve"), (fill.pop(0), "act")]
    jobs += [("cross", "act")] + [(fill.pop(0), "act") for _ in range(2)]
    jobs += [("o0", "act"), ("o1", "act")]
    jobs += [(n, "act") for n in fill]
    jobs += [("cq norm", "act"), ("ckv norm", "act"), ("o norm0", "act"), ("o norm1", "act")]
    jobs += [(f"q up{i}", "act") for i in range(4)] + [(f"k up{i}", "act") for i in range(4)]
    jobs += [(f"v up{i}", "act") for i in range(2)]
    jobs += [(f"q turn{i}", "dve") for i in range(4)] + [("k turn", "dve")]
    jobs += attention_jobs()
    jobs += [(f"ya{i}", "dve") for i in range(4)] + [(f"yb{i}", "dve") for i in range(4)]
    jobs += [(f"out{i}", "dve") for i in range(4)]
    jobs += [("norm2", "act"), ("router", "act"), ("combine", "dve")]
    return jobs


def attention_pe(pe, job, PE, AC, DV, l, tag, q, k, v, p, pT, ident):
    for g in range(6):
        b = job(f"{tag}s{g}")
        t, nh, n = (0, 4, P) if g < 2 else (1, 2, T)
        h0 = 4 * g if g < 2 else 2 * (g - 2)
        for j in range(nh):
            ins = pe.matmul(b[:, n * j:n * j + n], q(h0 + j, t), k(h0 + j, n), start=True, stop=True)
        ins.then_inc(PE.sem, PE.one(f"{tag}s{g}"))
    for g in range(6):
        pe.wait_ge(DV.sem, DV.at(f"{tag}p{g}", l))
        b = job(f"{tag}pT{g}")
        for j in range(4):
            c = 512 * g + P * j
            ins = pe.transpose(b[:, P * j:P * j + P], p[:, c:c + P], ident)
        ins.then_inc(PE.sem, PE.one(f"{tag}pT{g}"))
    for g in range(4):
        pe.wait_ge(AC.sem, AC.at(f"{tag}pT{2 + g}", l))
        b = job(f"{tag}ov{g}")
        for h in (2 * g, 2 * g + 1):
            o = b[0:VD, T * (h % 2):T * (h % 2) + T]
            w = lambda i: pT[:, P * i:P * i + P]
            pe.matmul(o[:, 0:P], v(h, 0), w(h), start=True, stop=True)
            pe.matmul(o[:, P:T], v(h, 0), w(8 + 2 * h), start=True, stop=False)
            ins = pe.matmul(o[:, P:T], v(h, 1), w(9 + 2 * h), start=False, stop=True)
        ins.then_inc(PE.sem, PE.one(f"{tag}ov{g}"))


def attention_act(nc, act, bank, PE, AC, DV, l, tag, p, pT, o, nmax, sums):
    for g in range(6):
        nh, n = (4, P) if g < 2 else (2, T)
        act.wait_ge(DV.sem, DV.at(f"{tag}s{g}", l))
        for j in range(nh):
            s = p[:, 512 * g + n * j:512 * g + n * j + n]
            ins = nc.scalar.activation(s, s, ACT.Exp, bias=nmax[:, 4 * g + j:4 * g + j + 1],
                                       accum_out=sums[:, 4 * g + j:4 * g + j + 1])
        ins.then_inc(AC.sem, AC.one(f"{tag}e{g}"))
    for g in range(6):
        act.wait_ge(PE.sem, PE.at(f"{tag}pT{g}", l))
        nc.scalar.activation(pT[:, 512 * g:512 * g + 512], bank(f"{tag}pT{g}")[:, :], ACT.Copy)\
            .then_inc(AC.sem, AC.one(f"{tag}pT{g}"))
    for g in range(4):
        act.wait_ge(PE.sem, PE.at(f"{tag}ov{g}", l))
        for j in range(2):
            ins = nc.scalar.activation(o[VD * j:VD * j + VD, g, :],
                                       bank(f"{tag}ov{g}")[0:VD, T * j:T * j + T], ACT.Copy)
        ins.then_inc(AC.sem, AC.one(f"{tag}ov{g}"))


def attention_dve(nc, dve, bank, PE, AC, DV, l, tag, scale, bias, p, nmax, sums):
    for g in range(6):
        nh, n = (4, P) if g < 2 else (2, T)
        s = p[:, 512 * g:512 * g + 512].rearrange("p (h n) -> p h n", h=nh)
        dve.wait_ge(PE.sem, PE.at(f"{tag}s{g}", l))
        nc.vector.scalar_tensor_tensor(s, bank(f"{tag}s{g}")[:, :].rearrange("p (h n) -> p h n", h=nh),
                                       scale, bias(g, nh, n), ALU.mult, ALU.add)
        dve.drain()
        nc.vector.tensor_reduce(nmax[:, 4 * g:4 * g + nh], s, AX, ALU.max, negate=True)\
            .then_inc(DV.sem, DV.one(f"{tag}s{g}"))
    for g in range(6):
        nh, n = (4, P) if g < 2 else (2, T)
        dve.wait_ge(AC.sem, AC.at(f"{tag}e{g}", l))
        r = sums[:, 4 * g:4 * g + nh]
        nc.vector.reciprocal(r, r)
        dve.drain()
        for j in range(nh):
            s = p[:, 512 * g + n * j:512 * g + n * j + n]
            ins = nc.vector.tensor_scalar(s, s, r[:, j:j + 1], None, ALU.mult)
        ins.then_inc(DV.sem, DV.one(f"{tag}p{g}"))


def attention_jobs(tag=""):
    jobs = [(f"{tag}s{g}", "dve") for g in range(6)]
    jobs += [(f"{tag}pT{g}", "act") for g in range(6)]
    jobs += [(f"{tag}ov{g}", "act") for g in range(4)]
    return jobs


def act_soft(tag=""):
    return [x for g in range(6) for x in (f"{tag}e{g}",)]


def act_steps():
    s = ["sq1", "norm1", "f0", "f1", "q0", "q1", "v0", "v1"]
    fill = list(FILL)
    s += [fill.pop(0) for _ in MASKED] + ["cross", fill.pop(0), fill.pop(0), "o0", "o1", "o sq"]
    s += fill + ["c sq", "cq norm", "ckv norm", "o norm0", "o norm1"]
    s += [f"q up{i}" for i in range(4)] + [f"k up{i}" for i in range(4)] + ["v up0", "v up1"]
    s += act_attention() + ["sq2", "norm2", "router"]
    return s


def act_attention(tag=""):
    return [f"{tag}e{g}" for g in range(6)] + [f"{tag}pT{g}" for g in range(6)] + [f"{tag}ov{g}" for g in range(4)]


def dve_attention(tag=""):
    return [f"{tag}s{g}" for g in range(6)] + [f"{tag}p{g}" for g in range(6)]


def dve_steps():
    s = ["mods", "h1", "fk"]
    s += ["qk L1", "diag t0", "diag t1"]
    for i, n in enumerate(LEVELS):
        s += [f"qk L{2 * n}", f"L{n} t0", f"L{n} t1"]
    s += ["cn", "oa"]
    s += [f"q turn{i}" for i in range(4)] + ["k turn"]
    s += dve_attention() + [f"ya{i}" for i in range(4)] + [f"yb{i}" for i in range(4)]
    s += [f"out{i}" for i in range(4)] + ["h2", "comb", "combine", "x2"]
    return s


MOE_PE = ["pick", "gu0", "gu1", "mods", "gu2", "gu3", "down"]
MOE_ACT = ["sg0", "sg1", "sg2", "sg3"]
MOE_DVE = ["acc", "he0", "he1", "mods", "he2", "he3", "next"]

R_JOBS = ([("final norm", "act"), ("norm1", "act")] + [(f"xr{i}", "act") for i in range(8)]
          + [(f"gelu{i}", "act") for i in range(8)] + [(f"ri{n}", "act") for n in range(LN)]
          + [(f"out{i}", "dve") for i in range(4)] + [("norm2", "act")])
R_ACT = (["sq0", "final norm", "sq1", "norm1", "softplus"] + [f"xr{i}" for i in range(8)]
         + [f"gelu{i}" for i in range(8)] + [f"ri{n}" for n in range(LN)]
         + ["tanh", "decay", "root", "sq2", "norm2"])
R_DVE = ["lambda", "x", "h1", "conv", "ix", "u", "y"] + [f"out{i}" for i in range(4)] + ["h2"]
R_UNITS = [("lru_w_in_2", P, KT, 0, LW + 352 * i, 352) for i in range(4)]
R_UNITS += [("lru_w_in_2", P, KT, 0, 352 * i, 352) for i in range(4)]
R_UNITS += [("lru_gates", LB, 2, 0, 0, LN * LB)]
R_UNITS += [("lru_w_out_2", LB, 4, 4 * LB * i, 0, D) for i in range(4)]
R_LAST = ["xr1", "xr3", "xr5", "xr7", "gelu1", "gelu3", "gelu5", "gelu7", f"ri{LN - 1}", "out3", "out3", "out3", "out3"]
A_JOBS = ([("norm", "act")] + [(f"k{i}", "act") for i in range(4)] + [(f"v{i}", "act") for i in range(4)]
          + [(f"kn{i}", "act") for i in range(4)] + [(f"q{i}", "act") for i in range(4)]
          + [(f"qn{i}", "act") for i in range(4)] + attention_jobs("A ") + attention_jobs("B ")
          + [(f"out{i}", "dve") for i in range(4)] + [("norm2", "act")])
A_ACT = (["sq", "norm"] + [f"k{i}" for i in range(4)] + ["k sq"] + [f"v{i}" for i in range(4)]
         + [f"kn{i}" for i in range(4)] + [f"q{i}" for i in range(4)] + ["q sq"]
         + [f"qn{i}" for i in range(4)] + act_attention("A ") + act_attention("B ") + ["sq2", "norm2"])
A_DVE = (["mods", "h", "hq", "bias", "k", "q"] + dve_attention("A ") + dve_attention("B ")
         + [f"out{i}" for i in range(4)] + ["h2", "x"])
A_UNITS = [("kv_w_2", P, KT, 0, 512 * i, 512) for i in range(4)]
A_UNITS += [("attn_w_q_2", P, KT, 0, 512 * i, 512) for i in range(2)]
A_UNITS += [("bias a",), ("bias b",)]
A_UNITS += [("attn_w_o_2", P, KT, 0, 512 * i, 512) for i in range(2)]
A_LAST = ["k1", "k3", "v1", "v3", "q1", "q3", None, None, "out1", "out3"]
MLP_TURNS = FF // 512
MLP_BANK = [4, 5, 6, 4]
MLP_SLOTS = [[0, 1, 2, 3], [4, 5, 0, 1]]
MLP_STEPS = [(["g0", "g1", "g2", "g3", "down", "mods"], ["mul0", "g0", "mul1", "g1", "mul2", "g2", "g3"],
              ["acc0", "he0", "acc1", "he1", "acc2", "he2", "he3", "mods"]),
             (["g0", "g1", "g2", "g3", "down"], ["g0", "g1", "g2", "g3"], ["he0", "he1", "he2", "he3"])]
MLP_CHUNKS = [CH, CH, 2 * D // MLP_TURNS]


def program(nc, xT, positions, cols, consts, ext, w):
    pe1, act1, dve1 = pe_jobs(), act_steps(), dve_steps()
    with ExitStack() as ctx:
        sem = lambda name: ctx.enter_context(nc.semaphore(name))
        ring = ctx.enter_context(nc.sbuf_tensor("ring", [P, SLOTS * SLOT], F32))
        sizes = {}

        def sb(name, *shape, dt=F32, parts=P):
            n = int(np.prod(shape))
            sizes[name] = n
            t = ctx.enter_context(nc.sbuf_tensor(name, [parts, n], dt))
            return t

        def view(t, off, *shape):
            n = int(np.prod(shape))
            ap = t[:, off:off + n]
            if len(shape) == 2:
                return ap.rearrange("p (a b) -> p a b", a=shape[0])
            if len(shape) == 3:
                return ap.rearrange("p (a b c) -> p a b c", a=shape[0], b=shape[1])
            return ap

        x_t = view(sb("x_t", KT * T), 0, KT, T)
        h_t = view(sb("h_t", KT * T), 0, KT, T)
        par = sb("par", NCOLS)
        con = sb("con", NCONST)
        posi = sb("posi", T, dt=I32)
        trig = sb("trig", 2 * T)
        lp = sb("lp", LP)
        modn = sb("modn", MODS + 2 * KT)
        mod = sb("mod", MODS)
        amod = sb("amod", 2 * KT)
        lbs = sb("lbs", 4 * HH)
        cact = sb("cact", 2 * KT)
        rs = view(sb("rs", 2 * T), 0, 2, T)
        small = sb("small", 640)
        epsb = sb("epsb", 2)
        zeros = ctx.enter_context(nc.sbuf_tensor("zeros", [P, 512], mybir.dt.bfloat16))
        lbl = sb("lbl", 2 * HH)
        wr_sb = sb("w_router", KT * NE)
        oa = view(sb("oa", HH * T), 0, HH, T)
        cqkv = sb("cqkv", 5 * T)
        krs = sb("krs", T)
        mix = sb("mix", 11264 + 16 * T + 4 * T)

        def col(name, i=0, n=1):
            a = COLS[name][0] + i
            return par[:, a:a + n]

        def const(name):
            a, n = CONST[name]
            return con[:, a:a + n]

        ident, ones, heads_ones = const("ident"), const("ones"), const("heads")
        cos, sin = trig[:, 0:T], trig[:, T:2 * T]

        def slot(u, *shape, parts=P):
            ap = ring[0:parts, (u % SLOTS) * SLOT:(u % SLOTS) * SLOT + int(np.prod(shape))]
            return ap.rearrange("p (a b) -> p a b", a=shape[0])

        banks = [ctx.enter_context(nc.psum_tensor(f"bank{i}", [P, 512], F32)) for i in range(8)]

        qf = view(mix, 0, HH, T)
        kf = view(mix, 1024, HH, T)
        fwd = view(mix, 2048, HH, T)
        bwd = view(mix, 3072, HH, T)
        qd = [view(mix, 4096 + 1024 * i, HH, T) for i in range(2)]
        kd = [view(mix, 6144 + 1024 * i, HH, T) for i in range(2)]
        vt = view(mix, 8192, TT, HH * DK)
        pairs = [view(mix, 9216 + 512 * i, HH, P) for i in range(2)]
        cross = view(mix, 10240, HH, P)
        tmp = view(mix, 10752, HH, P)
        osq = view(mix, 1024, HH, T)
        oraw = view(mix, 0, HH, T)
        ors = view(mix, 2048, HH, T)
        gates = view(mix, 11264, 16, T)
        hgate = view(mix, 11264 + 16 * T, HH, T)
        cq, ckv = view(cqkv, 0, 3, T), view(cqkv, 3 * T, 2, T)
        csq = view(mix, 3072, 5, T)
        q_a = view(mix, 0, NH, T)
        k_a = view(mix, 2048, NH, T)
        v_a = view(mix, 4096, TT, NH * VD)
        p_a = view(mix, 5120, 3072)
        pT_a = view(mix, 8192, 3072)
        ob = view(cqkv, 0, 4, T)
        he = view(mix, 0, 4, T)
        sg = view(mix, 1024, 4, T)
        tg = view(mix, 2048, 4, T)
        chunk = mix[:, 11264:11264 + KT * CH]
        accs = view(mix, 4096, 3, CH)
        combt = mix[0:NE, 5376:5376 + T]
        pick = mix[0:NE, 5632:5632 + T]
        ones16 = ones[0:NE, :]
        tmps = [tmp, oa[:, 0:2, :].rearrange("p a (b c) -> p (a b) c", c=P)]
        wr = view(wr_sb, 0, KT, NE)
        rbias = sb("router_bias", NE)[:, :]
        scores, biased = small[:, 0:32], small[:, 32:64]
        combw = small[:, 64:96]
        sm = small[:, 96:640]
        nmax, sums = small[:, 96:120], small[:, 120:144]

        loaded = sem("inputs_loaded")
        ring_full = [sem(f"ring_full{i}") for i in range(SLOTS)]
        chunk_full = sem("chunk_full")
        gate_half = sem("lru_gate_a_loaded")
        P0 = Steps(sem("prologue_pe"), ["mods"])
        A0 = Steps(sem("prologue_act"), ["c", "trig", "lb"])
        V0 = Steps(sem("prologue_dve"), ["zeros", "angles", "lb", "mods"])
        P0U = Steps(sem("prologue_unit_used"), [f"u{i}" for i in range(12)])
        PE = Steps(sem("pe_done"), [n for n, _ in pe1])
        AC = Steps(sem("act_done"), act1)
        DV = Steps(sem("dve_done"), dve1)
        MP = Turns(sem("moe_pe_done"), MOE_PE, 2 * len(MOE_PE))
        MA = Turns(sem("moe_act_done"), MOE_ACT, 0)
        MV = Turns(sem("moe_dve_done"), MOE_DVE, len(MOE_DVE))
        bank_of = {n: banks[i % 8] for i, (n, _) in enumerate(pe1)}
        before = {n: pe1[i - 8] for i, (n, _) in enumerate(pe1) if i >= 8}
        LBS = slice(0, LB)
        xc = view(mix, 0, LN, T)
        gelu = view(mix, 4096, LN, T)
        rg = view(mix, 8192, LN, T)
        ig = view(mix, 12288, LN, T)
        xr = view(mix, 12240, LN, T + 3)
        lam = [small[:, 144 + 16 * i:160 + 16 * i] for i in range(5)]
        q2_ = view(mix, 0, KT, 2, T)
        own = [(slice(HD * i, HD * i + HD), i) for i in range(2)]
        k2_ = view(mix, 4096, KT, T)
        v2_ = view(mix, 6144, TT, D)
        p2_, pT2 = view(mix, 8192, 3072), view(mix, 11264, 3072)
        o2_ = view(mix, 14336, KT, T)
        hq = view(mix, 14336, KT, T)
        ksq = view(mix, 11264, KT, T)
        krs2, qrs2 = view(mix, 8192, KT, T), view(mix, 11264, KT, T)
        akv = small[:, 240:240 + KT]
        chunks2 = [mix[:, 2048 + 3072 * i:2048 + 3072 * i + KT * n].rearrange("p (k n) -> p k n", k=KT)
                   for i, n in enumerate(MLP_CHUNKS)]
        accs2 = [mix[:, 11264 + CH * i:11264 + CH * i + n] for i, n in enumerate(MLP_CHUNKS)]
        chunk2_full = [sem(f"mlp_chunk_full{i}") for i in range(3)]
        PR, AR, VR = Steps(sem("lru_pe_done"), [n for n, _ in R_JOBS]), Steps(sem("lru_act_done"), R_ACT), Steps(sem("lru_dve_done"), R_DVE)
        PA, AA, VA = Steps(sem("attn_pe_done"), [n for n, _ in A_JOBS]), Steps(sem("attn_act_done"), A_ACT), Steps(sem("attn_dve_done"), A_DVE)
        MLP = [(Turns(sem(f"mlp{i}_pe_done"), p, 2 * len(p)), Turns(sem(f"mlp{i}_act_done"), a, 2 * len(a)),
                Turns(sem(f"mlp{i}_dve_done"), v, 2 * len(v))) for i, (p, a, v) in enumerate(MLP_STEPS)]
        stored = sem("output_stored")
        rows_stored = sem("bias_rows_stored")
        rows = nc.dram_tensor("bias_rows", (NH2, P, 512), F32, kind="Internal").ap()
        R_BASE = [2 + 2 * PER_LAYER[i] for i in range(SLOTS)]
        M0_BASE = [R_BASE[i] + len(range(i, len(R_UNITS), SLOTS)) for i in range(SLOTS)]
        A_BASE = [M0_BASE[i] + (MLP_TURNS // 2 if i in MLP_SLOTS[0] else 0) for i in range(SLOTS)]
        M1_BASE = [A_BASE[i] + len(range(i, len(A_UNITS), SLOTS)) for i in range(SLOTS)]

        def banks_of(jobs):
            at = {n: banks[i % 8] for i, (n, _) in enumerate(jobs)}
            old = {n: jobs[i - 8] for i, (n, _) in enumerate(jobs) if i >= 8}
            return at, old

        r_bank, r_old = banks_of(R_JOBS)
        a_bank, a_old = banks_of(A_JOBS)

        def heads(ap, n):
            return ap.unsqueeze(1).broadcast_to([ap.shape[0], n, ap.shape[1]])

        block = ctx.enter_context(nc.Block())

        @block.sync
        def _(sp):
            sp.dma_start(par[:, :], cols).then_inc(loaded, 16)
            sp.dma_start(con[:, :], consts).then_inc(loaded, 16)
            sp.dma_start(wr, w["w_router"].rearrange("(k p) n -> p k n", p=P)).then_inc(loaded, 16)
            sp.dma_start(rbias, w["router_bias"].rearrange("(a n) -> a n", a=1).to_broadcast([P, NE]))\
                .then_inc(loaded, 16)
            sp.dma_start(posi[:, :], positions.to_broadcast([P, T])).then_inc(loaded, 16)
            ada = w["ada"]
            for u in range(12):
                if u >= SLOTS:
                    sp.wait_ge(P0U.sem, P0U.at(f"u{u - SLOTS}"))
                sp.dma_start(slot(u, KT, 512), ada[0, :, 512 * u:512 * u + 512].rearrange(
                    "(k p) n -> p k n", p=P)).then_inc(ring_full[u % SLOTS], 16)
                if u == 1:
                    sp.dma_start(x_t, xT).then_inc(loaded, 16)
            sp.dma_start(rows, ext.unsqueeze(1).broadcast_to([NH2, P, 512])).then_inc(rows_stored, 16)
            sp.wait_ge(P0.sem, P0.at("mods"))
            with sp.Fori(0, 2) as l:
                for u, (name, height, c0, n) in enumerate(UNITS):
                    if u < SLOTS:
                        k = "down" if u % 3 == 2 else "gu3"
                        if u != 1:
                            sp.wait_ge(MP.sem, MP.at(k, (l * NE) + (u // 3 - 2)))
                    else:
                        sp.wait_ge(PE.sem, PE.at(LAST_USE[u - SLOTS], l))
                    src = w[name][bass.ds(l, 1), :, c0:c0 + n].rearrange(
                        "a (k p) n -> p (a k) n", p=P)
                    sp.dma_start(slot(u, height // P, n), src).then_inc(ring_full[u % SLOTS], 16)

                def expert(e, s0, waits, l=l):
                    for i, (name, nk, n) in enumerate([("w_gate", KT, DE), ("w_up", KT, DE), ("w_down", DE // P, D)]):
                        waits(i)
                        src = w[name][bass.ds(l, 1), bass.ds(e, 1)].rearrange(
                            "a b (k p) n -> p (a b k) n", p=P)
                        sp.dma_start(slot(s0 + i, nk, n), src).then_inc(ring_full[s0 + i], 16)

                def mod_chunk(e, l=l):
                    src = w["ada"][bass.ds(l + 1, 1), :, bass.ds(e * CH, CH)].rearrange(
                        "a (k p) n -> p (a k) n", p=P)
                    sp.dma_start(chunk.rearrange("p (k n) -> p k n", k=KT), src).then_inc(chunk_full, 16)

                for e in range(2):
                    expert(e, 3 * e, lambda i: sp.wait_ge(PE.sem, PE.at(LAST_USE_OF_SLOT[3 * e + i], l)))
                    if e == 0:
                        sp.wait_ge(DV.sem, DV.at("yb3", l))
                    else:
                        sp.wait_ge(MV.sem, MV.at("acc", l * NE))
                    mod_chunk(e)
                with sp.Fori(1, NE // 2) as it:
                    for j in range(2):
                        def used(i):
                            sp.wait_ge(MP.sem, MP.at("down" if i == 2 else "gu3",
                                                     l * NE + it * 2 + (j - 2)))
                        expert(it * 2 + j, 3 * j, used)
                        sp.wait_ge(MV.sem, MV.at("acc", l * NE + it * 2 + (j - 1)))
                        mod_chunk(it * 2 + j)

            for u, (name, height, nk, r0, c0, n) in enumerate(R_UNITS):
                s = u % SLOTS
                if u < SLOTS:
                    sp.wait_ge(MP.sem, MP.at("down" if s % 3 == 2 else "gu3", 2 * NE - 2 + s // 3))
                else:
                    sp.wait_ge(PR.sem, PR.at(R_LAST[u - SLOTS]))
                if name == "lru_gates":
                    for i, part in enumerate(("lru_gate_a_w_2", "lru_gate_x_w_2")):
                        sp.dma_start(slot(u, 2 * LN, LB, parts=LB)[:, LN * i:LN * i + LN, :],
                                     w[part][0].rearrange("n d e -> d n e")).then_inc(
                                         ring_full[s] if i else gate_half, 16)
                else:
                    sp.dma_start(slot(u, nk, n, parts=height),
                                 w[name][0][r0:r0 + height * nk, c0:c0 + n].rearrange(
                                     "(k p) n -> p k n", p=height)).then_inc(ring_full[s], 16)

            def mlp_units(layer, j, pair, waits):
                s1, s2 = MLP_SLOTS[layer][2 * pair:2 * pair + 2]
                waits(0)
                sp.dma_start(slot(s1, KT, 512), w["mlp_w1_2"][layer, :, bass.ds(j * 512, 512)].rearrange(
                    "(k p) n -> p k n", p=P)).then_inc(ring_full[s1], 16)
                waits(1)
                sp.dma_start(slot(s2, 4, D), w["mlp_w2_2"][layer, bass.ds(j * 512, 512), :].rearrange(
                    "(k p) n -> p k n", p=P)).then_inc(ring_full[s2], 16)

            def mlp_chunks(j, waits):
                for i, n in enumerate(MLP_CHUNKS):
                    waits(i)
                    src = w["ada"][3, :, bass.ds(j * (2 * CH) + CH * i, CH)] if i < 2 else \
                        w["kv_ada_w_2"][:, bass.ds(j * n, n)]
                    sp.dma_start(chunks2[i], src.rearrange("(k p) n -> p k n", p=P))\
                        .then_inc(chunk2_full[i], 16)

            def mlp_sync(layer, first_waits):
                pe_steps, _, dve_steps_ = MLP[layer]
                for j in range(2):
                    mlp_units(layer, j, j, lambda i: first_waits(2 * j + i))
                    if layer == 0:
                        if j == 0:
                            sp.wait_ge(VR.sem, VR.at("h2"))
                            mlp_chunks(j, lambda i: None)
                        else:
                            mlp_chunks(j, lambda i: sp.wait_ge(dve_steps_.sem, dve_steps_.at(f"acc{i}", 0)))
                with sp.Fori(1, MLP_TURNS // 2) as it:
                    for j in range(2):
                        mlp_units(layer, it * 2 + j, j, lambda i: sp.wait_ge(
                            pe_steps.sem, pe_steps.at("down" if i else "g3", it * 2 + (j - 2))))
                        if layer == 0:
                            mlp_chunks(it * 2 + j, lambda i: sp.wait_ge(
                                dve_steps_.sem, dve_steps_.at(f"acc{i}", it * 2 + (j - 1))))

            r_last = [R_LAST[max(range(i, len(R_UNITS), SLOTS))] for i in range(SLOTS)]
            mlp_sync(0, lambda i: sp.wait_ge(PR.sem, PR.at(r_last[MLP_SLOTS[0][i]])))
            for u, unit in enumerate(A_UNITS):
                s = u % SLOTS
                if u >= SLOTS:
                    sp.wait_ge(PA.sem, PA.at(A_LAST[u - SLOTS]))
                elif s in MLP_SLOTS[0]:
                    sp.wait_ge(MLP[0][0].sem, MLP[0][0].at("down" if s % 2 else "g3", MLP_TURNS - 2 + s // 2))
                else:
                    sp.wait_ge(PR.sem, PR.at(r_last[s]))
                if len(unit) == 1:
                    n, off = (P, 255) if unit[0] == "bias a" else (T, 127)
                    if unit[0] == "bias a":
                        sp.wait_ge(rows_stored, 16)
                    src = bass.AP(rows.tensor, off, [[511, P], [P * 512, NH2], [1, n]])
                    sp.dma_start(slot(u, NH2, n), src).then_inc(ring_full[s], 16)
                else:
                    name, _, nk, _, c0, n = unit
                    m = w[name] if name == "kv_w_2" else w[name][0]
                    sp.dma_start(slot(u, nk, n), m[:, c0:c0 + n].rearrange("(k p) n -> p k n", p=P))\
                        .then_inc(ring_full[s], 16)

            def before_mlp1(i):
                s = MLP_SLOTS[1][i]
                if s in (0, 1):
                    sp.wait_ge(VA.sem, VA.at("B s1" if s == 0 else "B s5"))
                else:
                    sp.wait_ge(PA.sem, PA.at(A_LAST[s]))
            mlp_sync(1, before_mlp1)
            sp.wait_ge(VA.sem, VA.at("x"))
            sp.dma_start(w["out"], x_t).then_inc(stored, 16)
            sp.wait_ge(stored, 16)

        def clear_sums(pe):
            for i in range(4):
                pe.matmul(banks[i][:, :], zeros[:, 0:P], zeros[:, :], start=True, stop=True,
                          skip_group_check=True)

        def mods_pe(pe, counts, steps, acc, done, e, sums, n, off=0):
            pe.wait_ge(counts.sem, counts.at(acc, e))
            for i in range(n):
                ins = pe.matmul(banks[7][:, off + i:off + i + 1], sums[:, P * i:P * i + P], ones[:, 0:1],
                                start=True, stop=True)
            if done:
                ins.then_inc(steps.sem, steps.one(done))

        @block.tensor
        def _(pe):
            pe.wait_ge(V0.sem, V0.at("zeros"))
            def full(u, l):
                s = u % SLOTS
                turn = u // SLOTS
                pe.wait_ge(ring_full[s], l * (16 * PER_LAYER[s]) + 16 * (2 + turn + 1))

            def tiles(bank, place, w_ap, c0, nk, rhs, m, width=P):
                for k in range(nk):
                    ins = pe.matmul(bank[0:width, place * T:place * T + T], w_ap[:, k, c0:c0 + width],
                                    rhs[:, k, :], start=(k == 0), stop=(k == nk - 1))
                return ins

            pe.wait_ge(loaded, 16 * 6)
            pe.wait_ge(A0.sem, A0.at("c"))
            for u in range(12):
                pe.wait_ge(ring_full[u % SLOTS], 16 * (u // SLOTS + 1))
                for m in range(4):
                    for k in range(KT):
                        ins = pe.matmul(banks[7][:, 4 * u + m:4 * u + m + 1],
                                        slot(u, KT, 512)[:, k, P * m:P * m + P],
                                        cact[:, k:k + 1], start=(k == 0), stop=(k == KT - 1))
                ins.then_inc(P0U.sem, P0U.one(f"u{u}"))
            pe.drain().then_inc(P0.sem, P0.one("mods"))
            pe.drain().then_inc(MP.sem, MP.first)
            with pe.Fori(0, 2) as l:
                def job(name):
                    if name in before:
                        old, by = before[name]
                        who = AC if by == "act" else DV
                        pe.wait_ge(who.sem, who.at(old, l))
                    return bank_of[name]

                def mean_squares(name, sq, n, lhs=ones, width=T, off=0):
                    b = job(name)
                    for k in range(n):
                        ins = pe.matmul(b[:, 0:width], lhs, sq[:, k, :], start=(k == 0), stop=(k == n - 1))
                    ins.then_inc(PE.sem, PE.one(name))

                def pair_tiles(name, u, j0, rhs, nk, n=2):
                    b = job(name)
                    for i in range(n):
                        ins = tiles(b, i, slot(u, nk, UNITS[u][3]), P * (j0 + i), nk, rhs, P)
                    ins.then_inc(PE.sem, PE.one(name))

                pe.wait_ge(AC.sem, AC.at("sq1", l))
                mean_squares("norm1", h_t, KT)
                pe.wait_ge(DV.sem, DV.at("h1", l))
                full(0, l)
                pair_tiles("f0", 0, 0, h_t, KT)
                pair_tiles("f1", 0, 2, h_t, KT)
                full(1, l)
                pair_tiles("q0", 1, 0, h_t, KT)
                pair_tiles("q1", 1, 2, h_t, KT)
                full(2, l)
                for t in range(TT):
                    b = job(f"v{t}")
                    for k in range(KT):
                        ins = pe.matmul(b[:, :], h_t[:, k, P * t:P * t + P], slot(2, KT, 512)[:, k, :],
                                        start=(k == 0), stop=(k == KT - 1))
                    ins.then_inc(PE.sem, PE.one(f"v{t}"))

                def fill(name):
                    if name.startswith("hgate"):
                        i = int(name[-1])
                        if i == 0:
                            full(3, l)
                        pair_tiles(name, 3, 2 * i, h_t, KT)
                    elif name.startswith("gates"):
                        i = int(name[-1])
                        if i % 2 == 0:
                            full(6 + i // 2, l)
                        pair_tiles(name, 6 + i // 2, 2 * (i % 2), h_t, KT)
                    elif name == "cq0":
                        full(4, l)
                        pair_tiles(name, 4, 0, h_t, KT)
                    elif name == "cq1":
                        pair_tiles(name, 4, 2, h_t, KT, n=1)
                    elif name == "ckv":
                        full(5, l)
                        pair_tiles(name, 5, 0, h_t, KT)
                    else:
                        b = job("kr")
                        tiles(b, 0, slot(5, KT, KVL + ROPE), KVL, KT, h_t, P, width=ROPE)\
                            .then_inc(PE.sem, PE.one("kr"))

                fills = list(FILL)
                for i, name in enumerate(MASKED):
                    if i == 0:
                        pe.wait_ge(DV.sem, DV.at("fk", l))
                        pe.wait_ge(AC.sem, AC.at("q1", l))
                    else:
                        pe.wait_ge(DV.sem, DV.at(f"qk {name}", l))
                    qs, ks = (qf, kf) if i == 0 else (qd[i % 2], kd[i % 2])
                    for t in range(TT):
                        b = job(f"{name} t{t}")
                        for h in range(HH):
                            ins = pe.matmul(b[:, P * h:P * h + P], ks[:, h, P * t:P * t + P],
                                            qs[:, h, P * t:P * t + P], start=True, stop=True)
                        ins.then_inc(PE.sem, PE.one(f"{name} t{t}"))
                    fill(fills.pop(0))
                pe.wait_ge(DV.sem, DV.at(f"qk L{P}", l))
                b = job("cross")
                for h in range(HH):
                    ins = pe.matmul(b[:, P * h:P * h + P], kd[0][:, h, 0:P], qd[0][:, h, P:T],
                                    start=True, stop=True)
                ins.then_inc(PE.sem, PE.one("cross"))
                fill(fills.pop(0))
                fill(fills.pop(0))
                pe.wait_ge(DV.sem, DV.at("L64 t1", l))
                pe.wait_ge(AC.sem, AC.at("cross", l))
                for i in range(2):
                    b = job(f"o{i}")
                    for h in (2 * i, 2 * i + 1):
                        o = b[:, T * (h % 2):T * (h % 2) + T]
                        v = lambda t: vt[:, t, DK * h:DK * h + DK]
                        pe.matmul(o[:, 0:P], v(0), pairs[0][:, h, :], start=True, stop=True)
                        pe.matmul(o[:, P:T], v(0), cross[:, h, :], start=True, stop=False)
                        ins = pe.matmul(o[:, P:T], v(1), pairs[1][:, h, :], start=False, stop=True)
                    ins.then_inc(PE.sem, PE.one(f"o{i}"))
                for name in fills:
                    fill(name)
                pe.wait_ge(AC.sem, AC.at("c sq", l))
                mean_squares("cq norm", csq[:, 0:3, :], 3)
                mean_squares("ckv norm", csq[:, 3:5, :], 2)
                for i in range(2):
                    b = job(f"o norm{i}")
                    pe.matmul(b[:, :], ones, osq[:, 2 * i:2 * i + 2, :], start=True, stop=True)\
                        .then_inc(PE.sem, PE.one(f"o norm{i}"))
                pe.wait_ge(DV.sem, DV.at("cn", l))
                full(10, l)
                wq = slot(10, 3, NH * DQK)
                for i in range(4):
                    b = job(f"q up{i}")
                    for j in range(2):
                        ins = tiles(b, j, wq, DQK * (2 * i + j), 3, cq, P, width=DQK)
                    ins.then_inc(PE.sem, PE.one(f"q up{i}"))
                full(11, l)
                wkv = slot(11, 2, NH * (NOPE + VD))
                for i in range(4):
                    b = job(f"k up{i}")
                    for j in range(2):
                        ins = tiles(b, j, wkv, (NOPE + VD) * (2 * i + j), 2, ckv, P, width=NOPE)
                    ins.then_inc(PE.sem, PE.one(f"k up{i}"))
                for t in range(TT):
                    b = job(f"v up{t}")
                    for k in range(2):
                        ins = pe.matmul(b[:, :], ckv[:, k, P * t:P * t + P],
                                        wkv[:, k, :].rearrange("p (h c) -> p h c", h=NH)[:, :, NOPE:NOPE + VD],
                                        start=(k == 0), stop=(k == 1))
                    ins.then_inc(PE.sem, PE.one(f"v up{t}"))
                turn = const("turn")[NOPE:DQK, :]
                for i in range(4):
                    pe.wait_ge(AC.sem, AC.at(f"q up{i}", l))
                    b = job(f"q turn{i}")
                    pe.matmul(b[0:DQK, :], turn, q_a[NOPE:DQK, 2 * i:2 * i + 2, :], start=True, stop=True)\
                        .then_inc(PE.sem, PE.one(f"q turn{i}"))
                pe.wait_ge(AC.sem, AC.at("kr", l))
                b = job("k turn")
                pe.matmul(b[0:DQK, 0:T], turn, krs[NOPE:DQK, :], start=True, stop=True)\
                    .then_inc(PE.sem, PE.one("k turn"))
                pe.wait_ge(DV.sem, DV.at("k turn", l))
                pe.wait_ge(AC.sem, AC.at("v up1", l))
                attention_pe(pe, job, PE, AC, DV, l, "",
                             lambda h, t: q_a[0:DQK, h, P * t:P * t + P],
                             lambda h, n: k_a[0:DQK, h, 0:n],
                             lambda h, t: v_a[:, t, VD * h:VD * h + VD], p_a, pT_a, ident)
                pe.wait_ge(DV.sem, DV.at("oa", l))
                full(12, l)
                for i in range(4):
                    pair_tiles(f"ya{i}", 12, 2 * i, oa, 4)
                pe.wait_ge(AC.sem, AC.at("ov3", l))
                full(13, l)
                for i in range(4):
                    pair_tiles(f"yb{i}", 13, 2 * i, ob, 4)
                pe.wait_ge(DV.sem, DV.at("yb3", l))
                for i in range(4):
                    if i % 2 == 0:
                        full(14 + i // 2, l)
                    pair_tiles(f"out{i}", 14 + i // 2, 2 * (i % 2), h_t, KT)
                pe.wait_ge(AC.sem, AC.at("sq2", l))
                mean_squares("norm2", h_t, KT)
                pe.wait_ge(DV.sem, DV.at("h2", l))
                b = job("router")
                for t in range(TT):
                    for k in range(KT):
                        ins = pe.matmul(b[:, NE * t:NE * t + NE], h_t[:, k, P * t:P * t + P],
                                        wr[:, k, :], start=(k == 0), stop=(k == KT - 1))
                ins.then_inc(PE.sem, PE.one("router"))
                pe.wait_ge(DV.sem, DV.at("comb", l))
                b = job("combine")
                for t in range(TT):
                    ins = pe.transpose(b[0:NE, P * t:P * t + P], combw[:, NE * t:NE * t + NE], ident)
                ins.then_inc(PE.sem, PE.one("combine"))
                pe.wait_ge(DV.sem, DV.at("combine", l))

                clear_sums(pe)
                with pe.Fori(0, NE // 2) as it:
                    for j in range(2):
                        e = l * NE + it * 2 + j
                        gate, up, down = slot(3 * j, KT, DE), slot(3 * j + 1, KT, DE), slot(3 * j + 2, 4, D)

                        def expert_full(s):
                            pe.wait_ge(ring_full[s], l * (16 * PER_LAYER[s]) + it * 16
                                       + 16 * (2 + STATIC_IN[s] + 1))

                        pe.wait_ge(MV.sem, MV.at("next", e - 1))
                        pe.matmul(banks[6][:, 0:T], ones16, pick, start=True, stop=True)\
                            .then_inc(MP.sem, MP.one("pick"))
                        expert_full(3 * j)
                        for m in range(4):
                            if m < 2:
                                pe.wait_ge(MV.sem, MV.at(f"he{m + 2}", e - 1))
                            else:
                                pe.wait_ge(MV.sem, MV.at(f"he{m - 2}", e))
                            b = banks[4 + m % 2]
                            tiles(b, 0, gate, P * m, KT, h_t, P)
                            if m == 0:
                                expert_full(3 * j + 1)
                            tiles(b, 1, up, P * m, KT, h_t, P).then_inc(MP.sem, MP.one(f"gu{m}"))
                            if m == 1:
                                mods_pe(pe, MV, MP, "acc", "mods", e, accs[:, 0, :], 3)
                        expert_full(3 * j + 2)
                        for k in range(4):
                            pe.wait_ge(MV.sem, MV.at(f"he{k}", e))
                            for o in range(KT):
                                ins = pe.matmul(banks[o // 2][:, T * (o % 2):T * (o % 2) + T],
                                                down[:, k, P * o:P * o + P], he[:, k, :],
                                                start=False, stop=False, skip_group_check=True)
                        ins.then_inc(MP.sem, MP.one("down"))
            def unit(u, base):
                pe.wait_ge(ring_full[u % SLOTS], 16 * (base[u % SLOTS] + u // SLOTS + 1))

            def r_job(name):
                if name in r_old:
                    old, by = r_old[name]
                    who = AR if by == "act" else VR
                    pe.wait_ge(who.sem, who.at(old))
                return r_bank[name]

            def sum_squares(b, sq, n):
                for k in range(n):
                    ins = pe.matmul(b[:, 0:T], ones, sq[:, k, :], start=(k == 0), stop=(k == n - 1))
                return ins

            pe.wait_ge(AR.sem, AR.at("sq0"))
            sum_squares(r_job("final norm"), h_t, KT).then_inc(PR.sem, PR.one("final norm"))
            pe.wait_ge(AR.sem, AR.at("sq1"))
            sum_squares(r_job("norm1"), h_t, KT).then_inc(PR.sem, PR.one("norm1"))
            pe.wait_ge(VR.sem, VR.at("h1"))
            for i in range(16):
                name = f"xr{i}" if i < 8 else f"gelu{i - 8}"
                if i % 2 == 0:
                    unit(i // 2, R_BASE)
                b = r_job(name)
                for j in range(2):
                    ins = tiles(b, j, slot(i // 2, KT, 352), LB * (2 * (i % 2) + j), KT, h_t, P, width=LB)
                ins.then_inc(PR.sem, PR.one(name))
            pe.wait_ge(VR.sem, VR.at("conv"))
            unit(8, R_BASE)
            pe.wait_ge(gate_half, 16)
            wg = slot(8, 2 * LN, LB, parts=LB)
            for n in range(LN):
                b = r_job(f"ri{n}")
                pe.matmul(b[LBS, 0:T], wg[:, n, :], xc[LBS, n, :], start=True, stop=True)
                pe.matmul(b[LBS, T:2 * T], wg[:, LN + n, :], xc[LBS, n, :], start=True, stop=True)\
                    .then_inc(PR.sem, PR.one(f"ri{n}"))
            outs = [r_job(f"out{i}") for i in range(4)]
            for b in outs:
                pe.matmul(b[:, :], zeros[:, 0:P], zeros[:, :], start=True, stop=True, skip_group_check=True)
            pe.wait_ge(VR.sem, VR.at("y"))
            for u in range(4):
                unit(9 + u, R_BASE)
                wo = slot(9 + u, 4, D, parts=LB)
                for o in range(KT):
                    for k in range(4):
                        ins = pe.matmul(outs[o // 2][:, T * (o % 2):T * (o % 2) + T], wo[:, k, P * o:P * o + P],
                                        gelu[LBS, 4 * u + k, :], start=False, stop=False, skip_group_check=True)
                    if u == 3 and o % 2:
                        ins.then_inc(PR.sem, PR.one(f"out{o // 2}"))
            pe.wait_ge(AR.sem, AR.at("sq2"))
            sum_squares(r_job("norm2"), h_t, KT).then_inc(PR.sem, PR.one("norm2"))

            def mlp_pe(layer, base, h2):
                pe_steps, act_steps_, dve_steps_ = MLP[layer]
                pe.wait_ge(h2[0].sem, h2[0].at("h2"))
                pe.drain().then_inc(pe_steps.sem, pe_steps.first)
                clear_sums(pe)
                with pe.Fori(0, MLP_TURNS // 2) as it:
                    for j in range(2):
                        e = it * 2 + j
                        s1, s2 = MLP_SLOTS[layer][2 * j:2 * j + 2]
                        pe.wait_ge(ring_full[s1], it * 16 + 16 * (base[s1] + 1))
                        for m in range(4):
                            pe.wait_ge(act_steps_.sem, act_steps_.at(*[("g3", e - 1), ("g1", e - 1),
                                                                       ("g2", e - 1), ("g0", e)][m]))
                            tiles(banks[MLP_BANK[m]], 0, slot(s1, KT, 512), P * m, KT, h_t, P)\
                                .then_inc(pe_steps.sem, pe_steps.one(f"g{m}"))
                        pe.wait_ge(ring_full[s2], it * 16 + 16 * (base[s2] + 1))
                        for k in range(4):
                            pe.wait_ge(dve_steps_.sem, dve_steps_.at(f"he{k}", e))
                            for o in range(KT):
                                ins = pe.matmul(banks[o // 2][:, T * (o % 2):T * (o % 2) + T],
                                                slot(s2, 4, D)[:, k, P * o:P * o + P], he[:, k, :],
                                                start=False, stop=False, skip_group_check=True)
                        ins.then_inc(pe_steps.sem, pe_steps.one("down"))
                        if layer == 0:
                            pe.wait_ge(dve_steps_.sem, dve_steps_.at("acc2", e))
                            at = 0
                            for i, n in enumerate(MLP_CHUNKS):
                                for c in range(n // P):
                                    ins = pe.matmul(banks[7][:, at:at + 1], accs2[i][:, P * c:P * c + P],
                                                    ones[:, 0:1], start=True, stop=True)
                                    at += 1
                            ins.then_inc(pe_steps.sem, pe_steps.one("mods"))

            mlp_pe(0, M0_BASE, (VR,))

            def a_job(name):
                if name in a_old:
                    old, by = a_old[name]
                    who = AA if by == "act" else VA
                    pe.wait_ge(who.sem, who.at(old))
                return a_bank[name]

            pe.wait_ge(AA.sem, AA.at("sq"))
            sum_squares(a_job("norm"), h_t, KT).then_inc(PA.sem, PA.one("norm"))
            pe.wait_ge(VA.sem, VA.at("h"))

            def projected(name, u0, rhs):
                for i in range(4):
                    u = u0 + i // 2
                    if i % 2 == 0:
                        unit(u, A_BASE)
                    b = a_job(f"{name}{i}")
                    for j in range(2):
                        ins = tiles(b, j, slot(u, KT, 512), P * (2 * (i % 2) + j), KT, rhs, P)
                    ins.then_inc(PA.sem, PA.one(f"{name}{i}"))

            def head_squares(name, sq):
                for i in range(4):
                    b = a_job(f"{name}{i}")
                    pe.matmul(b[:, :], heads_ones, sq[:, 2 * i:2 * i + 2, :], start=True, stop=True)\
                        .then_inc(PA.sem, PA.one(f"{name}{i}"))

            projected("k", 0, h_t)
            for i in range(4):
                u, t = 2 + i // 2, i % 2
                if t == 0:
                    unit(u, A_BASE)
                b = a_job(f"v{i}")
                for k in range(KT):
                    ins = pe.matmul(b[:, :], h_t[:, k, P * t:P * t + P], slot(u, KT, 512)[:, k, :],
                                    start=(k == 0), stop=(k == KT - 1))
                ins.then_inc(PA.sem, PA.one(f"v{i}"))
            pe.wait_ge(AA.sem, AA.at("k sq"))
            head_squares("kn", ksq)
            pe.wait_ge(VA.sem, VA.at("hq"))
            projected("q", 4, hq)
            pe.wait_ge(AA.sem, AA.at("q sq"))
            head_squares("qn", h_t)
            pe.wait_ge(VA.sem, VA.at("q"))
            for half, tag in enumerate(("A ", "B ")):
                attention_pe(pe, a_job, PA, AA, VA, 0, tag,
                             lambda h, t: q2_[:, 4 * half + h // 2, h % 2, P * t:P * t + P],
                             lambda h, n: k2_[:, 4 * half + h // 2, 0:n],
                             lambda h, t: v2_[:, t, HD * (8 * half + h):HD * (8 * half + h) + HD],
                             p2_, pT2, ident)
            pe.wait_ge(AA.sem, AA.at("B ov3"))
            projected("out", 8, o2_)
            pe.wait_ge(AA.sem, AA.at("sq2"))
            sum_squares(a_job("norm2"), h_t, KT).then_inc(PA.sem, PA.one("norm2"))
            mlp_pe(1, M1_BASE, (VA,))

        def rstd(act, bank, out, n, width=T):
            act.activation(out, bank[:, 0:width], ACT.Ln, scale=1.0 / n, bias=epsb[:, 0:1])
            act.drain()
            return act.activation(out, out, ACT.Exp, scale=-0.5)

        @block.scalar
        def _(act):
            act.wait_ge(V0.sem, V0.at("zeros"))
            act.wait_ge(loaded, 16 * 6)
            act.activation(cact[:, :], col("c", 0, 2 * KT), ACT.Silu).then_inc(A0.sem, A0.one("c"))
            act.wait_ge(V0.sem, V0.at("angles"))
            act.activation(trig[:, :], mix[:, 0:2 * T], ACT.Sin).then_inc(A0.sem, A0.one("trig"))
            act.wait_ge(V0.sem, V0.at("lb"))
            act.activation(lbs[:, 0:2 * HH], lbs[:, 0:2 * HH], ACT.Exp).then_inc(A0.sem, A0.one("lb"))
            with act.Fori(0, 2) as l:
                def emptied(name, out, func, rows=P, width=512, **kw):
                    act.wait_ge(PE.sem, PE.at(name, l))
                    src = bank_of[name][0:rows, 0:width]
                    if len(out.shape) == 3:
                        src = src.rearrange("p (a b) -> p a b", a=out.shape[1])
                    act.activation(out, src, func, **kw).then_inc(AC.sem, AC.one(name))

                def two(t, i, n=2):
                    return t[:, 2 * i:2 * i + n, :]

                act.wait_ge(DV.sem, DV.at("mods", l))
                act.activation(h_t, x_t, ACT.Square).then_inc(AC.sem, AC.one("sq1"))
                act.wait_ge(PE.sem, PE.at("norm1", l))
                rstd(act, bank_of["norm1"], rs[:, 0, :], D).then_inc(AC.sem, AC.one("norm1"))
                for i in range(2):
                    emptied(f"f{i}", two(fwd, i), ACT.Sigmoid)
                for i in range(2):
                    emptied(f"q{i}", two(qf, i), ACT.Silu)
                for i in range(2):
                    emptied(f"v{i}", vt[:, i, :], ACT.Copy)

                def fill(name):
                    if name.startswith("hgate"):
                        emptied(name, two(hgate, int(name[-1])), ACT.Silu)
                    elif name.startswith("gates"):
                        emptied(name, two(gates, int(name[-1])), ACT.Sigmoid)
                    elif name == "kr":
                        act.wait_ge(PE.sem, PE.at(name, l))
                        act.activation(krs[NOPE:DQK, :], bank_of[name][0:ROPE, 0:T], ACT.Copy)\
                            .then_inc(AC.sem, AC.one(name))
                    elif name == "cq1":
                        emptied(name, cq[:, 2:3, :], ACT.Copy, width=T)
                    elif name == "cq0":
                        emptied(name, cq[:, 0:2, :], ACT.Copy)
                    else:
                        emptied(name, ckv, ACT.Copy)

                fills = list(FILL)
                for _ in MASKED:
                    fill(fills.pop(0))
                emptied("cross", cross, ACT.Copy, scale=DK ** -0.5)
                fill(fills.pop(0))
                fill(fills.pop(0))
                emptied("o0", two(oraw, 0), ACT.Copy)
                emptied("o1", two(oraw, 1), ACT.Copy)
                act.drain()
                act.activation(osq, oraw, ACT.Square).then_inc(AC.sem, AC.one("o sq"))
                for name in fills:
                    fill(name)
                act.activation(csq, view(cqkv, 0, 5, T), ACT.Square).then_inc(AC.sem, AC.one("c sq"))
                act.wait_ge(PE.sem, PE.at("cq norm", l))
                rstd(act, bank_of["cq norm"], rs[:, 0, :], QL).then_inc(AC.sem, AC.one("cq norm"))
                act.wait_ge(PE.sem, PE.at("ckv norm", l))
                rstd(act, bank_of["ckv norm"], rs[:, 1, :], KVL).then_inc(AC.sem, AC.one("ckv norm"))
                for i in range(2):
                    act.wait_ge(PE.sem, PE.at(f"o norm{i}", l))
                    rstd(act, bank_of[f"o norm{i}"], mix[:, 2048 + 512 * i:2560 + 512 * i], DK, 512)\
                        .then_inc(AC.sem, AC.one(f"o norm{i}"))
                act.wait_ge(DV.sem, DV.at("oa", l))
                for i in range(4):
                    emptied(f"q up{i}", q_a[0:DQK, 2 * i:2 * i + 2, :], ACT.Copy, rows=DQK)
                for i in range(4):
                    emptied(f"k up{i}", k_a[0:NOPE, 2 * i:2 * i + 2, :], ACT.Copy, rows=NOPE)
                for i in range(2):
                    emptied(f"v up{i}", v_a[:, i, :], ACT.Copy)
                attention_act(nc, act, lambda n: bank_of[n], PE, AC, DV, l, "", p_a, pT_a, ob, nmax, sums)
                act.wait_ge(DV.sem, DV.at("out3", l))
                act.activation(h_t, x_t, ACT.Square).then_inc(AC.sem, AC.one("sq2"))
                act.wait_ge(PE.sem, PE.at("norm2", l))
                rstd(act, bank_of["norm2"], rs[:, 0, :], D).then_inc(AC.sem, AC.one("norm2"))
                emptied("router", scores, ACT.Sigmoid, width=TT * NE)
                with act.Fori(0, NE) as e:
                    for m in range(4):
                        act.wait_ge(MP.sem, MP.at(f"gu{m}", l * NE + e))
                        act.activation(sg[:, m, :], banks[4 + m % 2][:, 0:T], ACT.Silu)\
                            .then_inc(MA.sem, MA.one(f"sg{m}"))
            def norm_act(A, V, Pj, bank, sq, name, ready):
                act.wait_ge(V.sem, ready)
                act.activation(h_t, x_t, ACT.Square).then_inc(A.sem, A.one(sq))
                act.wait_ge(Pj.sem, Pj.at(name))
                rstd(act, bank[name], rs[:, 0, :], D).then_inc(A.sem, A.one(name))

            norm_act(AR, DV, PR, r_bank, "sq0", "final norm", DV.at("x2", 1))
            norm_act(AR, VR, PR, r_bank, "sq1", "norm1", VR.at("x"))
            act.activation(lam[2][LBS, :], lam[1][LBS, :], ACT.Exp, scale=-1.0)
            act.drain()
            act.activation(lam[2][LBS, :], lam[2][LBS, :], ACT.Ln, bias=epsb[LBS, 1:2])\
                .then_inc(AR.sem, AR.one("softplus"))
            for i in range(8):
                act.wait_ge(PR.sem, PR.at(f"xr{i}"))
                act.activation(xr[LBS, 2 * i:2 * i + 2, 3:T + 3],
                               r_bank[f"xr{i}"][LBS, :].rearrange("p (a b) -> p a b", a=2), ACT.Copy)\
                    .then_inc(AR.sem, AR.one(f"xr{i}"))
            for i in range(8):
                act.wait_ge(PR.sem, PR.at(f"gelu{i}"))
                act.activation(gelu[LBS, 2 * i:2 * i + 2, :],
                               r_bank[f"gelu{i}"][LBS, :].rearrange("p (a b) -> p a b", a=2),
                               ACT.Gelu_apprx_tanh).then_inc(AR.sem, AR.one(f"gelu{i}"))
            for n in range(LN):
                act.wait_ge(PR.sem, PR.at(f"ri{n}"))
                b = r_bank[f"ri{n}"]
                act.activation(rg[LBS, n, :], b[LBS, 0:T], ACT.Sigmoid, bias=col("ba", n)[LBS, :])
                act.activation(ig[LBS, n, :], b[LBS, T:2 * T], ACT.Sigmoid, bias=col("bx", n)[LBS, :])\
                    .then_inc(AR.sem, AR.one(f"ri{n}"))
            act.wait_ge(VR.sem, VR.at("ix"))
            act.drain()
            for n in range(LN):
                ins = act.activation(xc[LBS, n, :], rg[LBS, n, :], ACT.Tanh, scale=lam[3][LBS, n:n + 1])
            ins.then_inc(AR.sem, AR.one("tanh"))
            for n in range(LN):
                ins = act.activation(rg[LBS, n, :], rg[LBS, n, :], ACT.Exp, scale=lam[4][LBS, n:n + 1])
            ins.then_inc(AR.sem, AR.one("decay"))
            act.wait_ge(VR.sem, VR.at("u"))
            act.activation(xc[LBS, :, :], xc[LBS, :, :], ACT.Sqrt).then_inc(AR.sem, AR.one("root"))
            norm_act(AR, VR, PR, r_bank, "sq2", "norm2", VR.at("out3"))

            def mlp_act(layer):
                pe_steps, act_steps_, dve_steps_ = MLP[layer]
                act.drain().then_inc(act_steps_.sem, act_steps_.first)
                with act.Fori(0, MLP_TURNS) as e:
                    for m in range(4):
                        if layer == 0 and m < 3:
                            act.wait_ge(chunk2_full[m], e * 16 + 16)
                            for k in range(KT):
                                ins = act.activation(chunks2[m][:, k, :], chunks2[m][:, k, :], ACT.Copy,
                                                     scale=cact[:, KT + k:KT + k + 1])
                            ins.then_inc(act_steps_.sem, act_steps_.one(f"mul{m}"))
                        act.wait_ge(pe_steps.sem, pe_steps.at(f"g{m}", e))
                        act.activation(sg[:, m, :], banks[MLP_BANK[m]][:, 0:T], ACT.Relu)\
                            .then_inc(act_steps_.sem, act_steps_.one(f"g{m}"))

            mlp_act(0)
            norm_act(AA, VA, PA, a_bank, "sq", "norm", VA.at("mods"))

            def taken(name, out):
                act.wait_ge(PA.sem, PA.at(name))
                src = a_bank[name][:, :]
                if len(out.shape) == 3:
                    src = src.rearrange("p (a b) -> p a b", a=2)
                act.activation(out, src, ACT.Copy).then_inc(AA.sem, AA.one(name))

            def head_norm(name, out):
                for i in range(4):
                    act.wait_ge(PA.sem, PA.at(f"{name}{i}"))
                    rstd(act, a_bank[f"{name}{i}"], out[:, 512 * i:512 * i + 512], HD, 512)\
                        .then_inc(AA.sem, AA.one(f"{name}{i}"))

            for i in range(4):
                taken(f"k{i}", k2_[:, 2 * i:2 * i + 2, :])
            act.drain()
            act.activation(ksq, k2_, ACT.Square).then_inc(AA.sem, AA.one("k sq"))
            for i in range(4):
                taken(f"v{i}", v2_[:, i % 2, 512 * (i // 2):512 * (i // 2) + 512])
            head_norm("kn", mix[:, 8192:10240])
            for i in range(4):
                act.wait_ge(PA.sem, PA.at(f"q{i}"))
                for rows, j in own:
                    ins = act.activation(q2_[rows, 2 * i:2 * i + 2, j, :],
                                         a_bank[f"q{i}"][rows, :].rearrange("p (a b) -> p a b", a=2), ACT.Copy)
                ins.then_inc(AA.sem, AA.one(f"q{i}"))
            act.drain()
            for rows, j in own:
                ins = act.activation(h_t[rows, :, :], q2_[rows, :, j, :], ACT.Square)
            ins.then_inc(AA.sem, AA.one("q sq"))
            head_norm("qn", mix[:, 11264:13312])
            for half, tag in enumerate(("A ", "B ")):
                attention_act(nc, act, lambda n: a_bank[n], PA, AA, VA, 0, tag, p2_, pT2,
                              o2_[:, 4 * half:4 * half + 4, :], nmax, sums)
            norm_act(AA, VA, PA, a_bank, "sq2", "norm2", VA.at("out3"))
            mlp_act(1)

        def routing():
            tt, ts = nc.vector.tensor_tensor, nc.vector.tensor_scalar
            wait = nc.vector.drain
            at = [0]

            def cols(*shape):
                n = int(np.prod(shape))
                ap = sm[:, at[0]:at[0] + n]
                at[0] += n
                if len(shape) == 3:
                    return ap.rearrange("p (a b c) -> p a b c", a=shape[0], b=shape[1])
                return ap.rearrange("p (a b) -> p a b", a=shape[0])

            s = scores.rearrange("p (t e) -> p t e", t=TT)
            v = biased.rearrange("p (t e) -> p t e", t=TT)
            tt(v, s, heads(rbias, TT), ALU.add)
            wait()
            g = biased.rearrange("p (g e) -> p g e", g=TT * NG)
            sums6 = cols(TT * NG, 6)
            tt(sums6[:, :, 0:3], g[:, :, 0:3], g[:, :, 1:4], ALU.add)
            tt(sums6[:, :, 3:5], g[:, :, 0:2], g[:, :, 2:4], ALU.add)
            tt(sums6[:, :, 5:6], g[:, :, 0:1], g[:, :, 3:4], ALU.add)
            wait()
            score = cols(TT, NG)
            nc.vector.tensor_reduce(score.rearrange("p t g -> p (t g)"), sums6, AX, ALU.max)

            def first_best(x, n, order):
                top = cols(TT, 1)
                wait()
                nc.vector.tensor_reduce(top.rearrange("p t a -> p (t a)"), x, AX, ALU.max)
                wait()
                is_top = cols(TT, n)
                tt(is_top, x, top.broadcast_to([P, TT, n]), ALU.is_equal)
                wait()
                tt(is_top, is_top, heads(order, TT), ALU.mult)
                wait()
                lowest = cols(TT, 1)
                nc.vector.tensor_reduce(lowest.rearrange("p t a -> p (t a)"), is_top, AX, ALU.max)
                wait()
                tt(is_top, is_top, lowest.broadcast_to([P, TT, n]), ALU.is_equal)
                wait()
                return is_top

            order = cols(1, NE)[:, 0, :]
            for i in range(NE):
                nc.vector.memset(order[:, i:i + 1], float(NE - i))
            best = first_best(score, NG, order[:, 0:NG])
            inside = cols(TT * NG, EG)
            nc.vector.tensor_copy(inside, best.rearrange("p t g -> p (t g)").unsqueeze(2)
                                  .broadcast_to([P, TT * NG, EG]))
            wait()
            left = cols(TT * NG, EG)
            out = cols(TT * NG, EG)
            tt(left, g, inside, ALU.mult)
            ts(out, inside, -NEG, NEG, ALU.mult, ALU.add)
            wait()
            tt(left, left, out, ALU.add)
            wait()
            flat = lambda ap: ap.rearrange("p g e -> p (g e)").rearrange("p (t e) -> p t e", t=TT)
            one = first_best(flat(left), NE, order)
            ts(out, one.rearrange("p t e -> p (t e)").rearrange("p (g e) -> p g e", e=EG), 2 * NEG, None, ALU.mult)
            wait()
            tt(left, left, out, ALU.add)
            two = first_best(flat(left), NE, order)
            tt(one, one, two, ALU.add)
            wait()
            tt(one, one, s, ALU.mult)
            wait()
            total = cols(TT, 1)
            nc.vector.tensor_reduce(total.rearrange("p t a -> p (t a)"), one, AX, ALU.add)
            wait()
            nc.vector.reciprocal(total, total)
            wait()
            tt(combw.rearrange("p (t e) -> p t e", t=TT), one, total.broadcast_to([P, TT, NE]), ALU.mult)

        @block.vector
        def _(dve):
            tt, ts, stt = nc.vector.tensor_tensor, nc.vector.tensor_scalar, nc.vector.scalar_tensor_tensor
            nc.vector.memset(zeros[:, :], 0.0)
            nc.vector.memset(epsb[:, 0:1], EPS)
            nc.vector.memset(epsb[:, 1:2], 1.0)
            dve.drain().then_inc(V0.sem, V0.one("zeros"))
            dve.drain().then_inc(MV.sem, MV.first)
            dve.wait_ge(loaded, 16 * 6)
            ang, n = mix[:, 2 * T:3 * T], mix[:, 3 * T:4 * T]
            nc.vector.tensor_copy(ang, posi[:, :])
            dve.drain()
            ts(ang, ang, const("freq"), None, ALU.mult)
            dve.drain()
            for out, quarter in ((mix[:, 0:T], 0.25), (mix[:, T:2 * T], 0.0)):
                ts(n, ang, 1.0 / TWO_PI, quarter, ALU.mult, ALU.add)
                dve.drain()
                ts(n, n, MAGIC, None, ALU.add)
                dve.drain()
                ts(n, n, -MAGIC, None, ALU.add)
                dve.drain()
                stt(out, n, -C1, ang, ALU.mult, ALU.add)
                dve.drain()
                stt(out, n, -C2, out, ALU.mult, ALU.add)
                dve.drain()
                stt(out, n, -C3, out, ALU.mult, ALU.add)
                dve.drain()
                if quarter:
                    ts(out, out, float(np.pi / 2), None, ALU.add)
                    dve.drain()
                ts(out, out, 3.1415925, -3.1415925, ALU.min, ALU.max)
            dve.drain().then_inc(V0.sem, V0.one("angles"))
            a0, a1 = col("lb", 0, HH), col("lb", HH, HH)
            top = small[:, 0:HH]
            tt(top, a0, a1, ALU.max)
            dve.drain()
            tt(lbs[:, 0:HH], a0, top, ALU.subtract)
            tt(lbs[:, HH:2 * HH], a1, top, ALU.subtract).then_inc(V0.sem, V0.one("lb"))
            dve.wait_ge(A0.sem, A0.at("lb"))
            e0, e1, total = small[:, 4:8], small[:, 8:12], small[:, 12:16]
            tt(total, lbs[:, 0:HH], lbs[:, HH:2 * HH], ALU.add)
            dve.drain()
            nc.vector.reciprocal(total, total)
            dve.drain()
            tt(e0, lbs[:, 0:HH], total, ALU.mult)
            tt(e1, lbs[:, HH:2 * HH], total, ALU.mult)
            dve.drain()
            tt(lbs[:, 0:HH], e0, e0, ALU.subtract)
            tt(total, e0, e1, ALU.add)
            dve.drain()
            tt(lbs[:, 2 * HH:3 * HH], total, e0, ALU.subtract)
            dve.drain()
            for i in range(2):
                ts(lbs[:, (2 * i + 1) * HH:(2 * i + 2) * HH], lbs[:, 2 * i * HH:(2 * i + 1) * HH], -1.0, 1.0,
                   ALU.mult, ALU.add)
            dve.wait_ge(P0.sem, P0.at("mods"))
            tt(modn[:, 0:MODS], banks[7][:, 0:MODS], col("ada_b", 0, MODS), ALU.add)
            dve.drain().then_inc(V0.sem, V0.one("mods"))

            def modulated(src, gain_scale, shift, r):
                tt(h_t, src, heads(r, KT), ALU.mult)
                dve.drain()
                for k in range(KT):
                    ins = ts(h_t[:, k, :], h_t[:, k, :], gain_scale[:, k:k + 1], shift[:, k:k + 1],
                             ALU.mult, ALU.add)
                return ins

            with dve.Fori(0, 2) as l:
                bank = lambda name: bank_of[name]
                nc.vector.tensor_copy(lp[:, :], par[:, bass.ds(l * LP, LP)])
                nc.vector.tensor_copy(lbl[:, :], lbs[:, bass.ds(l * (2 * HH), 2 * HH)])
                nc.vector.tensor_copy(mod[:, :], modn[:, 0:MODS])
                dve.drain()
                stt(amod[:, 0:KT], mod[:, KT:2 * KT], 1.0, lp[:, N1G:N1G + KT], ALU.add, ALU.mult)
                stt(amod[:, KT:2 * KT], mod[:, 4 * KT:5 * KT], 1.0, lp[:, N2G:N2G + KT], ALU.add, ALU.mult)
                dve.drain().then_inc(DV.sem, DV.one("mods"))
                dve.wait_ge(AC.sem, AC.at("norm1", l))
                modulated(x_t, amod[:, 0:KT], mod[:, 0:KT], rs[:, 0, :]).then_inc(DV.sem, DV.one("h1"))
                dve.wait_ge(AC.sem, AC.at("f1", l))
                nc.vector.memset(bwd, 1.0)
                for h in range(HH):
                    ts(fwd[:, h, :], fwd[:, h, :], lbl[:, HH + h:HH + h + 1], lbl[:, h:h + 1], ALU.mult, ALU.add)
                dve.drain()
                ts(kf, fwd, -1.0, 1.0, ALU.mult, ALU.add).then_inc(DV.sem, DV.one("fk"))

                def halves(t, n):
                    return t.rearrange("p h t -> p (h t)").rearrange("p (b two n) -> p b two n", two=2, n=n)

                def weigh(n, i):
                    if n <= 2:
                        tt(qd[i], qf, fwd, ALU.mult)
                        return tt(kd[i], kf, bwd, ALU.mult)
                    s = lambda t, half: halves(t, n)[:, :, half, :]
                    tt(s(qd[i], 1), s(qf, 1), s(fwd, 1), ALU.mult)
                    return tt(s(kd[i], 0), s(kf, 0), s(bwd, 0), ALU.mult)

                def pair_sums(i, first):
                    name = MASKED[i]
                    mask = heads(const("pair")[:, P * i:P * i + P], HH)
                    for t in range(TT):
                        dve.wait_ge(PE.sem, PE.at(f"{name} t{t}", l))
                        out = pairs[t] if first else tmps[t]
                        ins = tt(out, bank(f"{name} t{t}")[:, :].rearrange("p (h n) -> p h n", h=HH),
                                 mask, ALU.mult)
                        if t == 0 or first:
                            ins.then_inc(DV.sem, DV.one(f"{name} t{t}"))
                    dve.drain()
                    if not first:
                        for t in range(TT):
                            ins = tt(pairs[t], pairs[t], tmps[t], ALU.add)
                        ins.then_inc(DV.sem, DV.one(f"{name} t1"))

                dve.drain()
                dve.wait_ge(AC.sem, AC.at("q1", l))
                weigh(1, 1).then_inc(DV.sem, DV.one("qk L1"))
                pair_sums(0, True)
                for i, n in enumerate(LEVELS):
                    f, b = halves(fwd, n), halves(bwd, n)
                    nb = HH * T // (2 * n)
                    wide = lambda ap: ap.broadcast_to([P, nb, n])
                    tt(b[:, :, 0, :], b[:, :, 0, :], wide(f[:, :, 1, n - 1:n]), ALU.mult)
                    dve.drain()
                    tt(f[:, :, 1, :], f[:, :, 1, :], wide(f[:, :, 0, n - 1:n]), ALU.mult)
                    dve.drain()
                    weigh(2 * n, i % 2).then_inc(DV.sem, DV.one(f"qk L{2 * n}"))
                    pair_sums(i + 1, False)
                dve.wait_ge(AC.sem, AC.at("ckv norm", l))
                tt(cq, cq, heads(rs[:, 0, :], 3), ALU.mult)
                tt(ckv, ckv, heads(rs[:, 1, :], 2), ALU.mult)
                dve.drain()
                for k in range(3):
                    ts(cq[:, k, :], cq[:, k, :], lp[:, QNG + k:QNG + k + 1], None, ALU.mult)
                for k in range(2):
                    ins = ts(ckv[:, k, :], ckv[:, k, :], lp[:, KVNG + k:KVNG + k + 1], None, ALU.mult)
                ins.then_inc(DV.sem, DV.one("cn"))
                dve.wait_ge(AC.sem, AC.at("o norm1", l))
                tt(oa, oraw, ors, ALU.mult)
                dve.drain()
                for h in range(HH):
                    ins = stt(oa[:, h, :], oa[:, h, :], lp[:, HGN + h:HGN + h + 1], hgate[:, h, :],
                              ALU.mult, ALU.mult)
                ins.then_inc(DV.sem, DV.one("oa"))
                rows = slice(NOPE, DQK)
                for i in range(4):
                    dve.wait_ge(PE.sem, PE.at(f"q turn{i}", l))
                    q2 = q_a[rows, 2 * i:2 * i + 2, :]
                    t2 = mix[rows, 8192 + 512 * i:8704 + 512 * i].rearrange("p (a b) -> p a b", a=2)
                    tt(t2, bank(f"q turn{i}")[rows, :].rearrange("p (a b) -> p a b", a=2),
                       heads(sin[rows, :], 2), ALU.mult)
                    tt(q2, q2, heads(cos[rows, :], 2), ALU.mult)
                    dve.drain()
                    tt(q2, q2, t2, ALU.add).then_inc(DV.sem, DV.one(f"q turn{i}"))
                dve.wait_ge(PE.sem, PE.at("k turn", l))
                t1 = mix[rows, 8192 + 2048:8192 + 2048 + T]
                tt(t1, bank("k turn")[rows, 0:T], sin[rows, :], ALU.mult)
                tt(krs[rows, :], krs[rows, :], cos[rows, :], ALU.mult)
                dve.drain()
                tt(krs[rows, :], krs[rows, :], t1, ALU.add)
                dve.drain()
                nc.vector.tensor_copy(k_a[rows, :, :], heads(krs[rows, :], NH)).then_inc(DV.sem, DV.one("k turn"))
                future = const("future")
                attention_dve(nc, dve, bank, PE, AC, DV, l, "", DQK ** -0.5,
                              lambda g, nh, n: heads(future[:, 2 * P - n:2 * P], nh), p_a, nmax, sums)
                two = lambda t, i: t[:, 2 * i:2 * i + 2, :]
                half = lambda name: bank(name)[:, :].rearrange("p (a b) -> p a b", a=2)
                for i in range(4):
                    dve.wait_ge(PE.sem, PE.at(f"ya{i}", l))
                    tt(two(h_t, i), half(f"ya{i}"), two(gates, i), ALU.mult).then_inc(DV.sem, DV.one(f"ya{i}"))
                for i in range(4):
                    dve.wait_ge(PE.sem, PE.at(f"yb{i}", l))
                    t2 = view(mix, 5120 + 512 * i, 2, T)
                    tt(t2, half(f"yb{i}"), two(gates, 4 + i), ALU.mult)
                    dve.drain()
                    tt(two(h_t, i), two(h_t, i), t2, ALU.add).then_inc(DV.sem, DV.one(f"yb{i}"))
                for i in range(4):
                    dve.wait_ge(PE.sem, PE.at(f"out{i}", l))
                    for k in (2 * i, 2 * i + 1):
                        ins = stt(x_t[:, k, :], bank(f"out{i}")[:, T * (k % 2):T * (k % 2) + T],
                                  mod[:, 2 * KT + k:2 * KT + k + 1], x_t[:, k, :], ALU.mult, ALU.add)
                    ins.then_inc(DV.sem, DV.one(f"out{i}"))
                dve.wait_ge(AC.sem, AC.at("norm2", l))
                modulated(x_t, amod[:, KT:2 * KT], mod[:, 3 * KT:4 * KT], rs[:, 0, :])\
                    .then_inc(DV.sem, DV.one("h2"))
                dve.wait_ge(AC.sem, AC.at("router", l))
                routing()
                dve.drain().then_inc(DV.sem, DV.one("comb"))
                dve.wait_ge(PE.sem, PE.at("combine", l))
                nc.vector.tensor_copy(combt, bank("combine")[0:NE, 0:T])
                dve.drain()
                ts(pick, combt, ident[0:NE, 0:1], None, ALU.mult)
                dve.drain().then_inc(DV.sem, DV.one("combine"))
                with dve.Fori(0, NE) as it:
                    e = l * NE + it
                    dve.wait_ge(chunk_full, (l * NE + it) * 16 + 16)
                    ck = chunk.rearrange("p (k n) -> p k n", k=KT)
                    cs = cact[:, bass.ds(l * KT, KT)].unsqueeze(2).broadcast_to([P, KT, CH])
                    tt(ck, ck, cs, ALU.mult)
                    dve.drain()
                    nc.vector.tensor_reduce(accs[:, 0, :], chunk.rearrange("p (k n) -> p n k", k=KT), AX, ALU.add)\
                        .then_inc(MV.sem, MV.one("acc"))
                    for m in range(4):
                        u = banks[4 + m % 2][:, T:2 * T]
                        if m == 2:
                            dve.wait_ge(MP.sem, MP.at("mods", e))
                            tt(modn[:, bass.ds(it * 3, 3)], banks[7][:, 0:3],
                               par[:, bass.ds(l * MODS + it * 3 + (COLS["ada_b"][0] + MODS), 3)], ALU.add)\
                                .then_inc(MV.sem, MV.one("mods"))
                        dve.wait_ge(MA.sem, MA.at(f"sg{m}", e))
                        tt(tg[:, m, :], sg[:, m, :], banks[6][:, 0:T], ALU.mult)
                        dve.drain()
                        tt(he[:, m, :], tg[:, m, :], u, ALU.mult).then_inc(MV.sem, MV.one(f"he{m}"))
                    ts(pick, combt, ident[0:NE, bass.ds(it + 1, 1)], None, ALU.mult)\
                        .then_inc(MV.sem, MV.one("next"))
                dve.wait_ge(MP.sem, MP.at("down", l * NE + (NE - 1)))
                for k in range(KT):
                    stt(x_t[:, k, :], banks[k // 2][:, T * (k % 2):T * (k % 2) + T],
                        mod[:, 5 * KT + k:5 * KT + k + 1], x_t[:, k, :], ALU.mult, ALU.add)
                dve.drain().then_inc(DV.sem, DV.one("x2"))
            def modulation(n1, n2, done=None):
                nc.vector.tensor_copy(mod[:, :], modn[:, 0:MODS])
                dve.drain()
                stt(amod[:, 0:KT], mod[:, KT:2 * KT], 1.0, n1, ALU.add, ALU.mult)
                stt(amod[:, KT:2 * KT], mod[:, 4 * KT:5 * KT], 1.0, n2, ALU.add, ALU.mult)
                dve.drain()

            lam0 = col("lam", 0, LN)[LBS, :]
            ts(lam[0][LBS, :], lam0, -1.0, None, ALU.mult)
            dve.drain()
            tt(lam[1][LBS, :], lam[0][LBS, :], lam0, ALU.max).then_inc(VR.sem, VR.one("lambda"))
            modulation(col("n1g2", 0, KT), col("n2g2", 0, KT))
            dve.wait_ge(AR.sem, AR.at("final norm"))
            tt(h_t, x_t, heads(rs[:, 0, :], KT), ALU.mult)
            dve.drain()
            for k in range(KT):
                ins = ts(x_t[:, k, :], h_t[:, k, :], col("final_g", k), None, ALU.mult)
            ins.then_inc(VR.sem, VR.one("x"))
            dve.wait_ge(AR.sem, AR.at("norm1"))
            modulated(x_t, amod[:, 0:KT], mod[:, 0:KT], rs[:, 0, :]).then_inc(VR.sem, VR.one("h1"))
            nc.vector.memset(xr[LBS, :, 0:3], 0.0)
            dve.wait_ge(AR.sem, AR.at("softplus"))
            stt(lam[2][LBS, :], lam[0][LBS, :], 0.0, lam[2][LBS, :], ALU.max, ALU.add)
            dve.drain()
            ts(lam[3][LBS, :], lam[2][LBS, :], 8.0, None, ALU.mult)
            ts(lam[4][LBS, :], lam[2][LBS, :], -8.0, None, ALU.mult)
            for i in range(8):
                dve.wait_ge(AR.sem, AR.at(f"xr{i}"))
                for n in (2 * i, 2 * i + 1):
                    ts(xc[LBS, n, :], xr[LBS, n, 3:T + 3], col("conv_w", 3 * LN + n)[LBS, :],
                       col("conv_b", n)[LBS, :], ALU.mult, ALU.add)
            for tap in (2, 1, 0):
                dve.drain()
                for n in range(LN):
                    ins = stt(xc[LBS, n, :], xr[LBS, n, tap:tap + T], col("conv_w", tap * LN + n)[LBS, :],
                              xc[LBS, n, :], ALU.mult, ALU.add)
            ins.then_inc(VR.sem, VR.one("conv"))
            dve.wait_ge(AR.sem, AR.at(f"ri{LN - 1}"))
            tt(ig[LBS, :, :], ig[LBS, :, :], xc[LBS, :, :], ALU.mult).then_inc(VR.sem, VR.one("ix"))
            dve.wait_ge(AR.sem, AR.at("decay"))
            for i in range(2):
                part = slice(8 * i, 8 * i + 8)
                dve.drain()
                tt(h_t[LBS, :, :], rg[LBS, part, :], rg[LBS, part, :], ALU.mult)
                dve.drain()
                ins = stt(xc[LBS, part, :], h_t[LBS, :, :], 1.0, xc[LBS, part, :], ALU.add, ALU.mult)
            ins.then_inc(VR.sem, VR.one("u"))
            dve.wait_ge(AR.sem, AR.at("root"))
            tt(xc[LBS, :, :], xc[LBS, :, :], ig[LBS, :, :], ALU.mult)
            dve.drain()
            for n in range(LN):
                nc.vector.tensor_tensor_scan(ig[LBS, n, :], rg[LBS, n, :], xc[LBS, n, :], 0.0, ALU.mult, ALU.add)
            dve.drain()
            tt(gelu[LBS, :, :], gelu[LBS, :, :], ig[LBS, :, :], ALU.mult).then_inc(VR.sem, VR.one("y"))

            def into_x(V, Pj, bank, g1):
                for i in range(4):
                    dve.wait_ge(Pj.sem, Pj.at(f"out{i}"))
                    for k in (2 * i, 2 * i + 1):
                        ins = stt(x_t[:, k, :], bank[f"out{i}"][:, T * (k % 2):T * (k % 2) + T],
                                  g1[:, k:k + 1], x_t[:, k, :], ALU.mult, ALU.add)
                    ins.then_inc(V.sem, V.one(f"out{i}"))

            into_x(VR, PR, r_bank, mod[:, 2 * KT:3 * KT])
            dve.wait_ge(AR.sem, AR.at("norm2"))
            modulated(x_t, amod[:, KT:2 * KT], mod[:, 3 * KT:4 * KT], rs[:, 0, :]).then_inc(VR.sem, VR.one("h2"))

            def mlp_dve(layer):
                pe_steps, act_steps_, dve_steps_ = MLP[layer]
                dve.drain().then_inc(dve_steps_.sem, dve_steps_.first)
                with dve.Fori(0, MLP_TURNS) as e:
                    for m in range(4):
                        if layer == 0 and m < 3:
                            dve.wait_ge(act_steps_.sem, act_steps_.at(f"mul{m}", e))
                            nc.vector.tensor_reduce(accs2[m], chunks2[m].rearrange("p k n -> p n k"), AX, ALU.add)\
                                .then_inc(dve_steps_.sem, dve_steps_.one(f"acc{m}"))
                        dve.wait_ge(act_steps_.sem, act_steps_.at(f"g{m}", e))
                        tt(he[:, m, :], sg[:, m, :], sg[:, m, :], ALU.mult)\
                            .then_inc(dve_steps_.sem, dve_steps_.one(f"he{m}"))
                    if layer == 0:
                        dve.wait_ge(pe_steps.sem, pe_steps.at("mods", e))
                        tt(modn[:, bass.ds(e * 6, 6)], banks[7][:, 0:6],
                           par[:, bass.ds(e * 6 + (COLS["ada_b"][0] + 3 * MODS), 6)], ALU.add)
                        tt(modn[:, bass.ds(e * 2 + MODS, 2)], banks[7][:, 6:8],
                           par[:, bass.ds(e * 2 + COLS["kv_ada_b"][0], 2)], ALU.add)\
                            .then_inc(dve_steps_.sem, dve_steps_.one("mods"))
                dve.wait_ge(pe_steps.sem, pe_steps.at("down", MLP_TURNS - 1))
                for k in range(KT):
                    ins = stt(x_t[:, k, :], banks[k // 2][:, T * (k % 2):T * (k % 2) + T],
                              mod[:, 5 * KT + k:5 * KT + k + 1], x_t[:, k, :], ALU.mult, ALU.add)
                return ins

            mlp_dve(0)
            dve.drain()
            modulation(col("n1g2", KT, KT), col("n2g2", KT, KT))
            stt(akv, modn[:, MODS + KT:MODS + 2 * KT], 1.0, col("kvng2", 0, KT), ALU.add, ALU.mult)
            dve.drain().then_inc(VA.sem, VA.one("mods"))
            dve.wait_ge(AA.sem, AA.at("norm"))
            modulated(x_t, akv, modn[:, MODS:MODS + KT], rs[:, 0, :]).then_inc(VA.sem, VA.one("h"))
            tt(hq, x_t, heads(rs[:, 0, :], KT), ALU.mult)
            dve.drain()
            for k in range(KT):
                ins = ts(hq[:, k, :], hq[:, k, :], amod[:, k:k + 1], mod[:, k:k + 1], ALU.mult, ALU.add)
            ins.then_inc(VA.sem, VA.one("hq"))
            bias_a, bias_b = slot(6, NH2, P), slot(7, NH2, T)
            for u, ap in ((6, bias_a[0:64, :, 64:P]), (7, bias_b[0:64, :, T - 64:T])):
                dve.wait_ge(ring_full[u % SLOTS], 16 * (A_BASE[u % SLOTS] + u // SLOTS + 1))
                nc.vector.memset(ap, NEG)
            dve.drain().then_inc(VA.sem, VA.one("bias"))

            for rows, j in own:
                nc.vector.memset(q2_[rows, :, 1 - j, :], 0.0)
            dve.wait_ge(AA.sem, AA.at("kn3"))
            stt(k2_, k2_, col("kng"), krs2, ALU.mult, ALU.mult).then_inc(VA.sem, VA.one("k"))
            dve.wait_ge(AA.sem, AA.at("qn3"))
            for rows, j in own:
                ins = stt(q2_[rows, :, j, :], q2_[rows, :, j, :], col("qng")[rows, :], qrs2[rows, :, :],
                          ALU.mult, ALU.mult)
            ins.then_inc(VA.sem, VA.one("q"))
            for half, tag in enumerate(("A ", "B ")):
                def bias(g, nh, n):
                    h0 = 8 * half + (4 * g if g < 2 else 2 * (g - 2))
                    return (bias_a if g < 2 else bias_b)[:, h0:h0 + nh, :]
                attention_dve(nc, dve, lambda n: a_bank[n], PA, AA, VA, 0, tag, HD ** -0.5, bias, p2_, nmax, sums)
            into_x(VA, PA, a_bank, mod[:, 2 * KT:3 * KT])
            dve.wait_ge(AA.sem, AA.at("norm2"))
            modulated(x_t, amod[:, KT:2 * KT], mod[:, 3 * KT:4 * KT], rs[:, 0, :]).then_inc(VA.sem, VA.one("h2"))
            mlp_dve(1).then_inc(VA.sem, VA.one("x"))


def shape_constants():
    con = np.zeros((P, NCONST), np.float32)
    def put(name, v):
        con[:v.shape[0], CONST[name][0]:CONST[name][0] + v.shape[1]] = v

    put("ident", np.eye(P, dtype=np.float32))
    put("ones", np.ones((P, P), np.float32))
    put("heads", np.kron(np.eye(2, dtype=np.float32), np.ones((HD, HD), np.float32)))
    turn = np.zeros((P, DQK), np.float32)
    half = ROPE // 2
    for i in range(half):
        turn[NOPE + half + i, NOPE + i] = -1.0
        turn[NOPE + i, NOPE + half + i] = 1.0
    put("turn", turn)
    s, t = np.arange(P)[:, None], np.arange(P)[None, :]
    masks = [s == t] + [(s // (2 * n) == t // (2 * n)) & (s // n % 2 == 0) & (t // n % 2 == 1) for n in LEVELS]
    put("pair", np.concatenate([m.astype(np.float32) * np.float32(DK ** -0.5) for m in masks], 1))
    future = np.zeros((P, 2 * P), np.float32)
    future[:64, P + 64:] = NEG
    put("future", future)
    freq = (np.float32(10000.0) ** (-np.arange(half, dtype=np.float32) / np.float32(half))).astype(np.float32)
    put("freq", np.tile(freq, P // half)[:, None])
    return con


def columns(v):
    return v.reshape(-1, P).T


def kernel(**inputs):
    import concourse.bacc as bacc
    from concourse.bass_utils import run_bass_kernel_spmd

    a = {k: np.asarray(v) for k, v in inputs.items()}
    cols = np.zeros((P, NCOLS), np.float32)

    def put(name, v):
        cols[:v.shape[0], COLS[name][0]:COLS[name][0] + v.shape[1]] = v

    put("layer", np.concatenate([columns(a[n][l]) for l in range(2) for n in
                                 ("norm1_g", "hg_norm_g", "q_norm_g", "kv_norm_g", "norm2_g")], 1))
    put("lb", columns(a["hg_lb_logits"]))
    put("ada_b", np.concatenate([columns(a["ada_b"]), columns(a["ada_b_2"])], 1))
    put("kv_ada_b", columns(a["kv_ada_b_2"]))
    put("c", np.concatenate([columns(a["c"]), columns(a["c_2"])], 1))
    put("final_g", columns(a["final_g"]))
    put("n1g2", columns(a["norm1_g_2"]))
    put("n2g2", columns(a["norm2_g_2"]))
    put("kvng2", columns(a["kv_norm_g_2"]))
    put("kng", columns(np.tile(a["k_norm_g_2"], 2)))
    put("qng", columns(np.tile(a["q_norm_g_2"][0], 2)))
    put("conv_w", a["lru_conv_w_2"][0].reshape(4 * LN, LB).T)
    for name, v in (("conv_b", "lru_conv_b_2"), ("ba", "lru_gate_a_b_2"), ("bx", "lru_gate_x_b_2"), ("lam", "lru_lambda_2")):
        put(name, a[v][0].reshape(LN, LB).T)
    rb = a["rel_bias_2"][0]
    ext = np.concatenate([np.repeat(rb[:, 256:257], 127, 1), rb[:, ::-1], np.repeat(rb[:, 0:1], 128, 1)], 1)
    arrays = {
        "x": np.ascontiguousarray(a["x"][0].T.reshape(KT, P, T).transpose(1, 0, 2)),
        "positions": a["positions"],
        "cols": cols,
        "consts": shape_constants(),
        "ext": np.ascontiguousarray(ext),
        "ada": np.concatenate([a["ada_w"], a["ada_w_2"]], 0),
        "w_router": a["w_router"], "router_bias": a["router_bias"],
    }
    for n in ("w_in", "w_q_up", "w_kv_up", "w_br_a", "w_br_b", "w_out", "w_gate", "w_up", "w_down",
              "mlp_w1_2", "mlp_w2_2", "lru_w_in_2", "lru_gate_a_w_2", "lru_gate_x_w_2", "lru_w_out_2",
              "kv_ada_w_2", "kv_w_2", "attn_w_q_2", "attn_w_o_2"):
        arrays[n] = np.ascontiguousarray(a[n])
    nc = bacc.Bacc("TRN2", target_bir_lowering=False, num_devices=1)
    w = {n: nc.dram_tensor("in_" + n, v.shape, mybir.dt.from_np(v.dtype), kind="ExternalInput").ap()
         for n, v in arrays.items()}
    w["out"] = nc.dram_tensor("out", (P, KT, T), F32, kind="ExternalOutput").ap()
    program(nc, w["x"], w["positions"], w["cols"], w["consts"], w["ext"], w)
    r = run_bass_kernel_spmd(nc, [{"in_" + n: v for n, v in arrays.items()}], core_ids=[0])
    out = np.asarray(r.results[0]["out"])
    return out.transpose(2, 1, 0).reshape(1, T, D)
```

```python
from contextlib import ExitStack

import numpy as np

import concourse.bass as bass
from concourse import mybir

ALU = mybir.AluOpType
ACT = mybir.ActivationFunctionType
AX = mybir.AxisListType.X
F32 = mybir.dt.float32
F32R = mybir.dt.float32r
I32 = mybir.dt.int32

P = 128
D = 1024
T = 256
KT = D // P
TT = T // P
EPS = 1e-6
HH, DK = 4, 128
NH, NOPE, ROPE, VD = 8, 64, 32, 64
DQK = NOPE + ROPE
QL, KVL = 384, 256
NE, NG, DE = 16, 4, 512
EG = NE // NG
LW, LN = 1408, 16
LB = LW // LN
NH2, HD = 16, 64
FF = 4096
SLOTS, SLOT = 6, 4096
PARTS, PART = 4, 1024
MODS = 6 * KT
CH = 384
LEVELS = [1, 2, 4, 8, 16, 32, 64]
NEG = -1e30
TWO_PI = 2 * np.pi
C1 = 6.28125
C2 = float(np.float32(np.round((TWO_PI - C1) * 2**22) / 2**22))
C3 = float(TWO_PI - C1 - C2)
MAGIC = 12582912.0

COLS = {}


def _cols():
    at = 0
    for name, n in [("layer", 2 * 25), ("lb", 2 * HH), ("ada_b", 4 * MODS), ("kv_ada_b", 2 * KT),
                    ("c", 2 * KT), ("final_g", KT), ("n1g2", 2 * KT), ("n2g2", 2 * KT),
                    ("kvng2", KT), ("kng", 1), ("qng", 1), ("conv_w", 4 * LN), ("conv_b", LN),
                    ("ba", LN), ("bx", LN), ("lam", LN)]:
        COLS[name] = (at, n)
        at += n
    return at


NCOLS = _cols()
N1G, HGN, QNG, KVNG, N2G, LP = 0, 8, 12, 15, 17, 25

CONST = {}


def _const():
    at = 0
    for name, n in [("ident", P), ("ones", P), ("heads", P), ("turn", DQK), ("pair", 8 * P),
                    ("future", 2 * P), ("freq", 1)]:
        CONST[name] = (at, n)
        at += n
    return at


NCONST = _const()


UNITS = [("w_in", D, 512, 512), ("w_in", D, 0, 512), ("w_in", D, 1024, 512), ("w_in", D, 1536, 512),
         ("w_in", D, 2048, QL), ("w_in", D, 2432, KVL + ROPE)]
UNITS += [("w_in", D, 2720 + 512 * i, 512) for i in range(4)]
UNITS += [("w_q_up", QL, 0, NH * DQK), ("w_kv_up", KVL, 0, NH * (NOPE + VD)),
          ("w_br_a", HH * DK, 0, D), ("w_br_b", NH * VD, 0, D),
          ("w_out", D, 0, 512), ("w_out", D, 512, 512)]
LAST_USE = ["f1", "q1", "v1", "hgate1", "cq1", "kr", "gates1", "gates3", "gates5", "gates7",
            "q up3", "v up1", "ya3", "yb3", "out1", "out3"]
STATIC_IN = [len(range(s, len(UNITS), SLOTS)) for s in range(SLOTS)]
PER_LAYER = STATIC_IN
LAST_USE_OF_SLOT = [LAST_USE[s + SLOTS * (STATIC_IN[s] - 1)] for s in range(SLOTS)]
FREED_BY_LO = ["lo7", "lo7", "lo11"]


class Steps:

    def __init__(self, sem, names):
        assert len(set(names)) == len(names)
        self.sem, self.names, self.n, self.given = sem, names, len(names), 0

    def one(self, name):
        assert self.names[self.given] == name, (self.names[self.given], name)
        self.given += 1
        return 1

    def at(self, name, turn=0):
        return turn * self.n + self.names.index(name) + 1


class Turns(Steps):

    def __init__(self, sem, names, first):
        super().__init__(sem, names)
        self.first = first

    def one(self, name):
        assert self.names[self.given % self.n] == name, (self.names[self.given % self.n], name)
        self.given += 1
        return 1

    def at(self, name, turn=0):
        return turn * self.n + (self.first + self.names.index(name) + 1)


FILL = ["hgate0", "hgate1", "cq0", "cq1", "ckv", "kr", "gates0", "gates1", "gates2",
        "gates3", "gates4", "gates5", "gates6", "gates7"]
MASKED = ["diag"] + [f"L{n}" for n in LEVELS]


def pe_jobs():
    jobs = [("norm1", "act")] + [(n, "act") for n in ("f0", "f1", "q0", "q1", "v0", "v1")]
    fill = list(FILL)
    for name in MASKED:
        jobs += [(f"{name} t0", "dve"), (f"{name} t1", "dve"), (fill.pop(0), "act")]
    jobs += [("cross", "act")] + [(fill.pop(0), "act") for _ in range(2)]
    jobs += [("o0", "act"), ("o1", "act")]
    jobs += [(n, "act") for n in fill]
    jobs += [("cq norm", "act"), ("ckv norm", "act"), ("o norm0", "act"), ("o norm1", "act")]
    jobs += [(f"q up{i}", "act") for i in range(4)] + [(f"k up{i}", "act") for i in range(4)]
    jobs += [(f"v up{i}", "act") for i in range(2)]
    jobs += [(f"q turn{i}", "dve") for i in range(4)] + [("k turn", "dve")]
    jobs += attention_jobs()
    jobs += [(f"ya{i}", "dve") for i in range(4)] + [(f"yb{i}", "dve") for i in range(4)]
    jobs += [(f"out{i}", "dve") for i in range(4)]
    jobs += [("norm2", "act"), ("router", "act"), ("combine", "dve")]
    return jobs


def attention_pe(pe, job, PE, AC, DV, l, tag, q, k, v, p, pT, ident):
    for g in range(6):
        b = job(f"{tag}s{g}")
        t, nh, n = (0, 4, P) if g < 2 else (1, 2, T)
        h0 = 4 * g if g < 2 else 2 * (g - 2)
        for j in range(nh):
            ins = pe.matmul(b[:, n * j:n * j + n], q(h0 + j, t), k(h0 + j, n), start=True, stop=True)
        ins.then_inc(PE.sem, PE.one(f"{tag}s{g}"))
    for g in range(6):
        pe.wait_ge(DV.sem, DV.at(f"{tag}p{g}", l))
        b = job(f"{tag}pT{g}")
        for j in range(4):
            c = 512 * g + P * j
            ins = pe.transpose(b[:, P * j:P * j + P], p[:, c:c + P], ident)
        ins.then_inc(PE.sem, PE.one(f"{tag}pT{g}"))
    for g in range(4):
        pe.wait_ge(AC.sem, AC.at(f"{tag}pT{2 + g}", l))
        b = job(f"{tag}ov{g}")
        for h in (2 * g, 2 * g + 1):
            o = b[0:VD, T * (h % 2):T * (h % 2) + T]
            w = lambda i: pT[:, P * i:P * i + P]
            pe.matmul(o[:, 0:P], v(h, 0), w(h), start=True, stop=True)
            pe.matmul(o[:, P:T], v(h, 0), w(8 + 2 * h), start=True, stop=False)
            ins = pe.matmul(o[:, P:T], v(h, 1), w(9 + 2 * h), start=False, stop=True)
        ins.then_inc(PE.sem, PE.one(f"{tag}ov{g}"))


def attention_act(nc, act, bank, PE, AC, DV, l, tag, p, pT, o, nmax, sums):
    for g in range(6):
        nh, n = (4, P) if g < 2 else (2, T)
        act.wait_ge(DV.sem, DV.at(f"{tag}s{g}", l))
        for j in range(nh):
            s = p[:, 512 * g + n * j:512 * g + n * j + n]
            ins = nc.scalar.activation(s, s, ACT.Exp, bias=nmax[:, 4 * g + j:4 * g + j + 1],
                                       accum_out=sums[:, 4 * g + j:4 * g + j + 1])
        ins.then_inc(AC.sem, AC.one(f"{tag}e{g}"))
    for g in range(6):
        act.wait_ge(PE.sem, PE.at(f"{tag}pT{g}", l))
        nc.scalar.activation(pT[:, 512 * g:512 * g + 512], bank(f"{tag}pT{g}")[:, :], ACT.Copy)\
            .then_inc(AC.sem, AC.one(f"{tag}pT{g}"))
    for g in range(4):
        act.wait_ge(PE.sem, PE.at(f"{tag}ov{g}", l))
        for j in range(2):
            ins = nc.scalar.activation(o[VD * j:VD * j + VD, g, :],
                                       bank(f"{tag}ov{g}")[0:VD, T * j:T * j + T], ACT.Copy)
        ins.then_inc(AC.sem, AC.one(f"{tag}ov{g}"))


def attention_dve(nc, dve, bank, PE, AC, DV, l, tag, scale, bias, p, nmax, sums):
    for g in range(6):
        nh, n = (4, P) if g < 2 else (2, T)
        s = p[:, 512 * g:512 * g + 512].rearrange("p (h n) -> p h n", h=nh)
        dve.wait_ge(PE.sem, PE.at(f"{tag}s{g}", l))
        nc.vector.scalar_tensor_tensor(s, bank(f"{tag}s{g}")[:, :].rearrange("p (h n) -> p h n", h=nh),
                                       scale, bias(g, nh, n), ALU.mult, ALU.add)
        dve.drain()
        nc.vector.tensor_reduce(nmax[:, 4 * g:4 * g + nh], s, AX, ALU.max, negate=True)\
            .then_inc(DV.sem, DV.one(f"{tag}s{g}"))
    for g in range(6):
        nh, n = (4, P) if g < 2 else (2, T)
        dve.wait_ge(AC.sem, AC.at(f"{tag}e{g}", l))
        r = sums[:, 4 * g:4 * g + nh]
        nc.vector.reciprocal(r, r)
        dve.drain()
        for j in range(nh):
            s = p[:, 512 * g + n * j:512 * g + n * j + n]
            ins = nc.vector.tensor_scalar(s, s, r[:, j:j + 1], None, ALU.mult)
        ins.then_inc(DV.sem, DV.one(f"{tag}p{g}"))


def attention_jobs(tag=""):
    jobs = [(f"{tag}s{g}", "dve") for g in range(6)]
    jobs += [(f"{tag}pT{g}", "act") for g in range(6)]
    jobs += [(f"{tag}ov{g}", "act") for g in range(4)]
    return jobs


def act_steps():
    s = ["sq1", "norm1", "f0", "f1", "q0", "q1", "v0", "v1"]
    fill = list(FILL)
    s += [fill.pop(0) for _ in MASKED] + ["cross", fill.pop(0), fill.pop(0), "o0", "o1", "o sq"]
    s += fill + ["c sq", "cq norm", "ckv norm", "o norm0", "o norm1"]
    s += [f"q up{i}" for i in range(4)] + [f"k up{i}" for i in range(4)] + ["v up0", "v up1"]
    s += act_attention() + ["sq2", "norm2", "h hi", "router"]
    return s


def act_attention(tag=""):
    return [f"{tag}e{g}" for g in range(6)] + [f"{tag}pT{g}" for g in range(6)] + [f"{tag}ov{g}" for g in range(4)]


def dve_attention(tag=""):
    return [f"{tag}s{g}" for g in range(6)] + [f"{tag}p{g}" for g in range(6)]


def dve_steps():
    s = ["mods", "h1", "fk"]
    s += ["qk L1", "diag t0", "diag t1"]
    for i, n in enumerate(LEVELS):
        s += [f"qk L{2 * n}", f"L{n} t0", f"L{n} t1"]
    s += ["cn", "oa"]
    s += [f"q turn{i}" for i in range(4)] + ["k turn"]
    s += dve_attention() + [f"ya{i}" for i in range(4)] + [f"yb{i}" for i in range(4)]
    s += [f"out{i}" for i in range(4)] + ["h2", "h lo", "comb", "combine", "x2"]
    return s


MOE_PE = ["pick"] + [f"part{j}" for j in range(8)] + ["mods"] + [f"part{j}" for j in range(8, 12)]
MOE_ACT = (["hi0", "hi1", "hi2", "hi3", "hi4", "sg0", "hi5", "hi6", "sg1", "hi7", "hi8", "sg2", "hi9",
            "hi10", "sg3", "hi11"])
MOE_DVE = ["lo0", "lo1", "lo2", "acc", "lo3", "lo4", "he0", "lo5", "lo6", "he1", "lo7", "lo8", "he2", "lo9",
           "lo10", "he3", "next", "mods", "lo11"]

R_JOBS = ([("final norm", "act"), ("norm1", "act")] + [(f"xr{i}", "act") for i in range(8)]
          + [(f"gelu{i}", "act") for i in range(4)] + [(f"ri{n}", "act") for n in range(LN)]
          + [(f"gelu{i}", "act") for i in range(4, 8)]
          + [(f"out{i}", "dve") for i in range(4)] + [("norm2", "act")])
R_ACT = (["sq0", "final norm", "sq1", "norm1", "softplus"] + [f"xr{i}" for i in range(8)]
         + [f"gelu{i}" for i in range(4)] + [f"ri{n}" for n in range(LN)]
         + ["tanh", "decay"] + [f"gelu{i}" for i in range(4, 8)] + ["root", "sq2", "norm2", "h hi"])
R_DVE = ["lambda", "x", "h1", "conv", "ix0", "ix1", "ix2", "ix3", "u", "y"] + [f"out{i}" for i in range(4)] + ["h2", "h lo"]
R_UNITS = [("lru_w_in_2", P, KT, 0, LW + 352 * i, 352) for i in range(4)]
R_UNITS += [("lru_w_in_2", P, KT, 0, 352 * i, 352) for i in range(4)]
R_UNITS += [("lru_gates", LB, 2, 0, 0, LN * LB)]
R_UNITS += [("lru_w_out_2", LB, 4, 4 * LB * i, 0, D) for i in range(4)]
R_LAST = ["xr1", "xr3", "xr5", "xr7", "gelu1", "gelu3", "gelu5", "gelu7", f"ri{LN - 1}", "out3", "out3", "out3", "out3"]
A_JOBS = ([("norm", "act")] + [(f"k{i}", "act") for i in range(4)] + [(f"v{i}", "act") for i in range(4)]
          + [(f"kn{i}", "act") for i in range(4)] + [(f"q{i}", "act") for i in range(4)]
          + [(f"qn{i}", "act") for i in range(4)] + attention_jobs("A ") + attention_jobs("B ")
          + [(f"out{i}", "dve") for i in range(4)] + [("norm2", "act")])
A_ACT = (["sq", "norm"] + [f"k{i}" for i in range(4)] + ["k sq"] + [f"v{i}" for i in range(4)]
         + [f"kn{i}" for i in range(4)] + [f"q{i}" for i in range(4)] + ["q sq"]
         + [f"qn{i}" for i in range(4)] + act_attention("A ") + act_attention("B ") + ["sq2", "norm2", "h hi"])
A_DVE = (["mods", "h", "hq", "bias", "k", "q"] + dve_attention("A ") + dve_attention("B ")
         + [f"out{i}" for i in range(4)] + ["h2", "h lo", "x"])
A_UNITS = [("kv_w_2", P, KT, 0, 512 * i, 512) for i in range(4)]
A_UNITS += [("attn_w_q_2", P, KT, 0, 512 * i, 512) for i in range(2)]
A_UNITS += [("bias a",), ("bias b",)]
A_UNITS += [("attn_w_o_2", P, KT, 0, 512 * i, 512) for i in range(2)]
A_SLOT = [0, 1, 2, 3, 4, 5, 0, 1, 4, 5]
A_LAST = ["k1", "k3", "v1", "v3", "q1", "q3", None, None, "out1", "out3"]
MLP_TURNS = FF // 512
MLP_BANK = [4, 5, 6, 4]
MLP_SLOTS = [[0, 1, 2, 3], [2, 3, 0, 1]]
MLP_PARTS = [f"part{j}" for j in range(8)]
MLP_SPLIT = [f"hi{j}" for j in range(4)], [f"lo{j}" for j in range(4)]
MLP_STEPS = [(MLP_PARTS[:6] + ["mods"] + MLP_PARTS[6:],
              ["hi0", "mul0", "hi1", "hi2", "mul1", "hi3"] + [x for j in range(4) for x in (f"g{j}", f"hi{j + 4}")],
              ["lo0", "lo1", "acc0", "lo2", "lo3", "acc1"]
              + [x for j in range(4) for x in (f"he{j}", f"lo{j + 4}")] + ["mods"]),
             (MLP_PARTS, MLP_SPLIT[0] + [x for j in range(4) for x in (f"g{j}", f"hi{j + 4}")],
              MLP_SPLIT[1] + [x for j in range(4) for x in (f"he{j}", f"lo{j + 4}")])]
MLP_CHUNKS = [CH, CH, 2 * D // MLP_TURNS]


def program(nc, xT, positions, cols, consts, ext, w):
    pe1, act1, dve1 = pe_jobs(), act_steps(), dve_steps()
    with ExitStack() as ctx:
        sem = lambda name: ctx.enter_context(nc.semaphore(name))

        def next_offset():
            return (nc.sbuf_base + 31) // 32 * 32

        ring_at = next_offset()
        ring = ctx.enter_context(nc.sbuf_tensor("ring", [P, SLOTS * SLOT], F32))
        def sb(name, *shape, dt=F32, parts=P):
            n = int(np.prod(shape))
            t = ctx.enter_context(nc.sbuf_tensor(name, [parts, n], dt))
            return t

        def view(t, off, *shape):
            n = int(np.prod(shape))
            ap = t[:, off:off + n]
            if len(shape) == 2:
                return ap.rearrange("p (a b) -> p a b", a=shape[0])
            if len(shape) == 3:
                return ap.rearrange("p (a b c) -> p a b c", a=shape[0], b=shape[1])
            return ap

        x_t = view(sb("x_t", KT * T), 0, KT, T)
        h_t = view(sb("h_t", KT * T), 0, KT, T)
        par = sb("par", NCOLS)
        con = sb("con", NCONST)
        posi = sb("posi", T, dt=I32)
        trig = sb("trig", 2 * T)
        lp = sb("lp", LP)
        modn = sb("modn", MODS + 2 * KT)
        mod = sb("mod", MODS)
        amod = sb("amod", 2 * KT)
        lbs = sb("lbs", 4 * HH)
        cact = sb("cact", 2 * KT)
        rs = view(sb("rs", 2 * T), 0, 2, T)
        small = sb("small", 640)
        epsb = sb("epsb", 2)
        zeros = ctx.enter_context(nc.sbuf_tensor("zeros", [P, 512], mybir.dt.bfloat16))
        lbl = sb("lbl", 2 * HH)
        wr_sb = sb("w_router", KT * NE)
        oa = view(sb("oa", HH * T), 0, HH, T)
        cqkv = sb("cqkv", 5 * T)
        krs = sb("krs", T)
        mix_at = next_offset()
        mix = sb("mix", 11264 + 16 * T + 4 * T)
        split_w = nc.alloc_sbuf_tensor_at("split_w", [P, 2 * PARTS * PART], F32R, offset=ring_at + 4 * SLOT * 4)
        split_x = nc.alloc_sbuf_tensor_at("split_x", [P, 2 * (KT + 4) * T], F32R,
                                          offset=mix_at + 4 * (11264 + 20 * T - 2 * (KT + 4) * T))

        def col(name, i=0, n=1):
            a = COLS[name][0] + i
            return par[:, a:a + n]

        def const(name):
            a, n = CONST[name]
            return con[:, a:a + n]

        ident, ones, heads_ones = const("ident"), const("ones"), const("heads")
        cos, sin = trig[:, 0:T], trig[:, T:2 * T]

        def slot(u, *shape, parts=P):
            ap = ring[0:parts, (u % SLOTS) * SLOT:(u % SLOTS) * SLOT + int(np.prod(shape))]
            return ap.rearrange("p (a b) -> p a b", a=shape[0])

        banks = [ctx.enter_context(nc.psum_tensor(f"bank{i}", [P, 512], F32)) for i in range(8)]

        qf = view(mix, 0, HH, T)
        kf = view(mix, 1024, HH, T)
        fwd = view(mix, 2048, HH, T)
        bwd = view(mix, 3072, HH, T)
        qd = [view(mix, 4096 + 1024 * i, HH, T) for i in range(2)]
        kd = [view(mix, 6144 + 1024 * i, HH, T) for i in range(2)]
        vt = view(mix, 8192, TT, HH * DK)
        pairs = [view(mix, 9216 + 512 * i, HH, P) for i in range(2)]
        cross = view(mix, 10240, HH, P)
        tmp = view(mix, 10752, HH, P)
        osq = view(mix, 1024, HH, T)
        oraw = view(mix, 0, HH, T)
        ors = view(mix, 2048, HH, T)
        gates = view(mix, 11264, 16, T)
        hgate = view(mix, 11264 + 16 * T, HH, T)
        cq, ckv = view(cqkv, 0, 3, T), view(cqkv, 3 * T, 2, T)
        csq = view(mix, 3072, 5, T)
        q_a = view(mix, 0, NH, T)
        k_a = view(mix, 2048, NH, T)
        v_a = view(mix, 4096, TT, NH * VD)
        p_a = view(mix, 5120, 3072)
        pT_a = view(mix, 8192, 3072)
        ob = view(cqkv, 0, 4, T)
        he = oa
        sg = view(mix, 0, 4, T)
        tg = view(mix, 1024, 4, T)
        chunk = mix[:, 2048:2048 + KT * CH]
        accs = mix[:, 5120:5120 + CH]
        combt = mix[0:NE, 5632:5632 + T]
        pick = mix[0:NE, 5888:5888 + T]
        h_hi, h_lo = view(split_x, 0, KT, T), view(split_x, KT * T, KT, T)
        he_hi, he_lo = view(split_x, 2 * KT * T, 4, T), view(split_x, (2 * KT + 4) * T, 4, T)

        def part_hi(j):
            return view(split_w, 2 * PART * (j % PARTS), KT, P)

        def part_lo(j):
            return view(split_w, 2 * PART * (j % PARTS) + PART, KT, P)

        def moe_raw(j):
            if j < 8:
                return slot(j % 2, KT, DE)[:, :, P * (j // 2):P * (j // 2) + P]
            return slot(2, 4, D)[:, j - 8, :].rearrange("p (o n) -> p o n", n=P)

        def mlp_raw(slots, j):
            if j < 4:
                return slot(slots[0], KT, 512)[:, :, P * j:P * j + P]
            return slot(slots[1], 4, D)[:, j - 4, :].rearrange("p (o n) -> p o n", n=P)
        ones16 = ones[0:NE, :]
        tmps = [tmp, oa[:, 0:2, :].rearrange("p a (b c) -> p (a b) c", c=P)]
        wr = view(wr_sb, 0, KT, NE)
        rbias = sb("router_bias", NE)[:, :]
        scores, biased = small[:, 0:32], small[:, 32:64]
        combw = small[:, 64:96]
        sm = small[:, 96:640]
        nmax, sums = small[:, 96:120], small[:, 120:144]

        def as_f32(ap):
            return ap.bitcast(F32)

        loaded = sem("inputs_loaded")
        x_loaded = sem("x_loaded")
        ring_full = [sem(f"ring_full{i}") for i in range(SLOTS)]
        chunk_full = sem("chunk_full")
        gu_full = [sem(f"expert_gate_up_half{i}_full") for i in range(2)]
        down_full = sem("expert_down_full")
        gate_half = sem("lru_gate_a_loaded")
        P0 = Steps(sem("prologue_pe"), ["mods"])
        A0 = Steps(sem("prologue_act"), ["c"] + [f"mul{u}" for u in range(6)] + ["trig", "lb"]
                   + [f"mul{u}" for u in range(6, 12)])
        V0 = Steps(sem("prologue_dve"), ["zeros", "angles", "lb"] + [f"sum{u}" for u in range(12)] + ["mods"])
        unit_sums = [mix[:, 4096 + 512 * u:4608 + 512 * u] for u in range(12)]
        PE = Steps(sem("pe_done"), [n for n, _ in pe1])
        AC = Steps(sem("act_done"), act1)
        DV = Steps(sem("dve_done"), dve1)
        MP = Turns(sem("moe_pe_done"), MOE_PE, len(MOE_PE))
        MA = Turns(sem("moe_act_done"), MOE_ACT, 0)
        MV = Turns(sem("moe_dve_done"), MOE_DVE, len(MOE_DVE))
        bank_of = {n: banks[i % 8] for i, (n, _) in enumerate(pe1)}
        before = {n: pe1[i - 8] for i, (n, _) in enumerate(pe1) if i >= 8}
        LBS = slice(0, LB)
        xc = view(mix, 0, LN, T)
        gelu = view(mix, 4096, LN, T)
        rg = view(mix, 8192, LN, T)
        ig = view(mix, 12288, LN, T)
        xr = view(mix, 12240, LN, T + 3)
        lam = [small[:, 144 + 16 * i:160 + 16 * i] for i in range(5)]
        q2_ = view(mix, 0, KT, 2, T)
        own = [(slice(HD * i, HD * i + HD), i) for i in range(2)]
        k2_ = view(mix, 4096, KT, T)
        v2_ = view(mix, 6144, TT, D)
        p2_, pT2 = view(mix, 8192, 3072), view(mix, 11264, 3072)
        o2_ = view(mix, 14336, KT, T)
        hq = view(mix, 14336, KT, T)
        ksq = view(mix, 11264, KT, T)
        krs2, qrs2 = view(mix, 8192, KT, T), view(mix, 11264, KT, T)
        akv = small[:, 240:240 + KT]
        chunks2 = [mix[:, 1024 + 3072 * i:1024 + 3072 * i + KT * n].rearrange("p (k n) -> p k n", k=KT)
                   for i, n in enumerate(MLP_CHUNKS)]
        accs2 = [mix[:, 9216 + CH * i:9216 + CH * i + n] for i, n in enumerate(MLP_CHUNKS)]
        chunk2_full = [sem(f"mlp_chunk_full{i}") for i in range(3)]
        PR, AR, VR = Steps(sem("lru_pe_done"), [n for n, _ in R_JOBS]), Steps(sem("lru_act_done"), R_ACT), Steps(sem("lru_dve_done"), R_DVE)
        PA, AA, VA = Steps(sem("attn_pe_done"), [n for n, _ in A_JOBS]), Steps(sem("attn_act_done"), A_ACT), Steps(sem("attn_dve_done"), A_DVE)
        MLP = [(Turns(sem(f"mlp{i}_pe_done"), p, 2 * len(p)), Turns(sem(f"mlp{i}_act_done"), a, 2 * len(a)),
                Turns(sem(f"mlp{i}_dve_done"), v, 2 * len(v))) for i, (p, a, v) in enumerate(MLP_STEPS)]
        kv_summed = sem("kv_chunk_summed")
        stored = sem("output_stored")
        rows_stored = sem("bias_rows_stored")
        rows = nc.dram_tensor("bias_rows", (NH2, P, 512), F32, kind="Internal").ap()
        R_BASE = [2 + 2 * PER_LAYER[i] for i in range(SLOTS)]
        M0_BASE = [R_BASE[i] + len(range(i, len(R_UNITS), SLOTS)) for i in range(SLOTS)]
        A_BASE = [M0_BASE[i] + (MLP_TURNS // 2 if i in MLP_SLOTS[0] else 0) for i in range(SLOTS)]
        M1_BASE = [A_BASE[i] + A_SLOT.count(i) for i in range(SLOTS)]

        def banks_of(jobs):
            at = {n: banks[i % 8] for i, (n, _) in enumerate(jobs)}
            old = {n: jobs[i - 8] for i, (n, _) in enumerate(jobs) if i >= 8}
            return at, old

        r_bank, r_old = banks_of(R_JOBS)
        a_bank, a_old = banks_of(A_JOBS)

        def heads(ap, n):
            return ap.unsqueeze(1).broadcast_to([ap.shape[0], n, ap.shape[1]])

        block = ctx.enter_context(nc.Block())

        @block.sync
        def _(sp):
            sp.dma_start(par[:, :], cols).then_inc(loaded, 16)
            sp.dma_start(con[:, :], consts).then_inc(loaded, 16)
            sp.dma_start(wr, w["w_router"].rearrange("(k p) n -> p k n", p=P)).then_inc(loaded, 16)
            sp.dma_start(rbias, w["router_bias"].rearrange("(a n) -> a n", a=1).to_broadcast([P, NE]))\
                .then_inc(loaded, 16)
            sp.dma_start(posi[:, :], positions.to_broadcast([P, T])).then_inc(loaded, 16)
            ada = w["ada"]
            for u in range(12):
                if u >= SLOTS:
                    sp.wait_ge(V0.sem, V0.at(f"sum{u - SLOTS}"))
                sp.dma_start(slot(u, KT, 512), ada[0, :, 512 * u:512 * u + 512].rearrange(
                    "(k p) n -> p k n", p=P)).then_inc(ring_full[u % SLOTS], 16)
                if u == 1:
                    sp.dma_start(x_t, xT).then_inc(x_loaded, 16)
            sp.dma_start(rows, ext.unsqueeze(1).broadcast_to([NH2, P, 512])).then_inc(rows_stored, 16)
            sp.wait_ge(P0.sem, P0.at("mods"))
            with sp.Fori(0, 2) as l:
                for u, (name, height, c0, n) in enumerate(UNITS):
                    if u < SLOTS:
                        if u == 0:
                            sp.wait_ge(MV.sem, MV.at("lo7", l * NE - 1))
                        elif u == 2:
                            sp.wait_ge(MV.sem, MV.at("lo11", l * NE - 1))
                        elif u == 4:
                            sp.wait_ge(MP.sem, MP.at("part11", l * NE - 1))
                    else:
                        sp.wait_ge(PE.sem, PE.at(LAST_USE[u - SLOTS], l))
                    src = w[name][bass.ds(l, 1), :, c0:c0 + n].rearrange(
                        "a (k p) n -> p (a k) n", p=P)
                    sp.dma_start(slot(u, height // P, n), src).then_inc(ring_full[u % SLOTS], 16)

                def expert(e, waits):
                    waits("chunk", None)
                    src = w["ada"][bass.ds(l + 1, 1), :, bass.ds(e * CH, CH)].rearrange(
                        "a (k p) n -> p (a k) n", p=P)
                    sp.dma_start(chunk.rearrange("p (k n) -> p k n", k=KT), src).then_inc(chunk_full, 16)
                    for half in range(2):
                        for s, name in enumerate(("w_gate", "w_up")):
                            waits(f"gate up {half}", s)
                            src = w[name][bass.ds(l, 1), bass.ds(e, 1), :, 256 * half:256 * half + 256]
                            sp.dma_start(slot(s, KT, DE)[:, :, 256 * half:256 * half + 256],
                                         src.rearrange("a b (k p) n -> p (a b k) n", p=P))\
                                .then_inc(gu_full[half], 16)
                    waits("down", 2)
                    sp.dma_start(slot(2, 4, D), w["w_down"][bass.ds(l, 1), bass.ds(e, 1)].rearrange(
                        "a b (k p) n -> p (a b k) n", p=P)).then_inc(down_full, 16)

                def statics_used(what, s):
                    if what == "gate up 0" or what == "down":
                        sp.wait_ge(PE.sem, PE.at(LAST_USE_OF_SLOT[s], l))
                    elif what == "chunk":
                        sp.wait_ge(DV.sem, DV.at("yb3", l))

                expert(0, statics_used)
                with sp.Fori(1, NE) as e:
                    def used(what, s):
                        if s != 1:
                            k = {"gate up 0": "lo3", "gate up 1": "lo7", "down": "lo11", "chunk": "acc"}[what]
                            sp.wait_ge(MV.sem, MV.at(k, l * NE + (e - 1)))
                    expert(e, used)

            for u, (name, height, nk, r0, c0, n) in enumerate(R_UNITS):
                s = u % SLOTS
                if u < SLOTS:
                    if s < 4:
                        sp.wait_ge(MV.sem, MV.at("lo7" if s < 2 else "lo11", 2 * NE - 1))
                    else:
                        sp.wait_ge(MP.sem, MP.at("part11", 2 * NE - 1))
                else:
                    sp.wait_ge(PR.sem, PR.at(R_LAST[u - SLOTS]))
                if name == "lru_gates":
                    for i, part in enumerate(("lru_gate_a_w_2", "lru_gate_x_w_2")):
                        sp.dma_start(slot(u, 2 * LN, LB, parts=LB)[:, LN * i:LN * i + LN, :],
                                     w[part][0].rearrange("n d e -> d n e")).then_inc(
                                         ring_full[s] if i else gate_half, 16)
                else:
                    sp.dma_start(slot(u, nk, n, parts=height),
                                 w[name][0][r0:r0 + height * nk, c0:c0 + n].rearrange(
                                     "(k p) n -> p k n", p=height)).then_inc(ring_full[s], 16)

            def mlp_units(layer, j, pair, waits):
                s1, s2 = MLP_SLOTS[layer][2 * pair:2 * pair + 2]
                waits(0)
                sp.dma_start(slot(s1, KT, 512), w["mlp_w1_2"][layer, :, bass.ds(j * 512, 512)].rearrange(
                    "(k p) n -> p k n", p=P)).then_inc(ring_full[s1], 16)
                waits(1)
                sp.dma_start(slot(s2, 4, D), w["mlp_w2_2"][layer, bass.ds(j * 512, 512), :].rearrange(
                    "(k p) n -> p k n", p=P)).then_inc(ring_full[s2], 16)

            def mlp_chunks(j, waits):
                for i, n in enumerate(MLP_CHUNKS):
                    waits(i)
                    src = w["ada"][3, :, bass.ds(j * (2 * CH) + CH * i, CH)] if i < 2 else \
                        w["kv_ada_w_2"][:, bass.ds(j * n, n)]
                    sp.dma_start(chunks2[i], src.rearrange("(k p) n -> p k n", p=P))\
                        .then_inc(chunk2_full[i], 16)

            def mlp_sync(layer, first_waits):
                dve_steps_ = MLP[layer][2]
                for j in range(2):
                    mlp_units(layer, j, j, lambda i: first_waits(2 * j + i))
                    if layer == 0:
                        if j == 0:
                            sp.wait_ge(VR.sem, VR.at("h2"))
                            mlp_chunks(j, lambda i: None)
                        else:
                            mlp_chunks(j, lambda i: sp.wait_ge(dve_steps_.sem, dve_steps_.at(f"acc{i}", 0)) if i < 2
                                       else sp.wait_ge(kv_summed, 1))
                with sp.Fori(1, MLP_TURNS // 2) as it:
                    for j in range(2):
                        mlp_units(layer, it * 2 + j, j, lambda i: sp.wait_ge(
                            dve_steps_.sem, dve_steps_.at("lo7" if i else "lo3", it * 2 + (j - 2))))
                        if layer == 0:
                            mlp_chunks(it * 2 + j, lambda i: sp.wait_ge(
                                dve_steps_.sem, dve_steps_.at(f"acc{i}", it * 2 + (j - 1))) if i < 2
                                       else sp.wait_ge(kv_summed, it * 2 + j))

            r_last = [R_LAST[max(range(i, len(R_UNITS), SLOTS))] for i in range(SLOTS)]
            mlp_sync(0, lambda i: sp.wait_ge(PR.sem, PR.at(r_last[MLP_SLOTS[0][i]])))
            for u, unit in enumerate(A_UNITS):
                s = A_SLOT[u]
                if u >= SLOTS:
                    sp.wait_ge(PA.sem, PA.at(A_LAST[A_SLOT.index(s)]))
                elif s in MLP_SLOTS[0]:
                    sp.wait_ge(MLP[0][2].sem, MLP[0][2].at("lo7" if s % 2 else "lo3", MLP_TURNS - 2 + s // 2))
                elif s == 4:
                    sp.wait_ge(MLP[0][0].sem, MLP[0][0].at("part7", MLP_TURNS - 1))
                if len(unit) == 1:
                    n, off = (P, 255) if unit[0] == "bias a" else (T, 127)
                    if unit[0] == "bias a":
                        sp.wait_ge(rows_stored, 16)
                    src = bass.AP(rows.tensor, off, [[511, P], [P * 512, NH2], [1, n]])
                    sp.dma_start(slot(s, NH2, n), src).then_inc(ring_full[s], 16)
                else:
                    name, _, nk, _, c0, n = unit
                    m = w[name] if name == "kv_w_2" else w[name][0]
                    sp.dma_start(slot(s, nk, n), m[:, c0:c0 + n].rearrange("(k p) n -> p k n", p=P))\
                        .then_inc(ring_full[s], 16)

            def before_mlp1(i):
                s = MLP_SLOTS[1][i]
                if s in (0, 1):
                    sp.wait_ge(VA.sem, VA.at("B s1" if s == 0 else "B s5"))
                else:
                    sp.wait_ge(PA.sem, PA.at(A_LAST[s]))
            mlp_sync(1, before_mlp1)
            sp.wait_ge(VA.sem, VA.at("x"))
            sp.dma_start(w["out"], x_t).then_inc(stored, 16)
            sp.wait_ge(stored, 16)

        def clear_sums(pe):
            for i in range(4):
                pe.matmul(banks[i][:, :], zeros[:, 0:P], zeros[:, :], start=True, stop=True,
                          skip_group_check=True)

        def split_products(pe, out, hi, lo, x_hi, x_lo, start=False, stop=False, **kw):
            pe.matmul(out, hi, x_hi, start=start, stop=False, **kw)
            pe.matmul(out, hi, x_lo, start=False, stop=False, **kw)
            return pe.matmul(out, lo, x_hi, start=False, stop=stop, **kw)

        def column_part(pe, j, out):
            for k in range(KT):
                ins = split_products(pe, out, part_hi(j)[:, k, :], part_lo(j)[:, k, :],
                                     h_hi[:, k, :], h_lo[:, k, :], start=(k == 0), stop=(k == KT - 1))
            return ins

        def row_part(pe, j, k):
            for o in range(KT):
                ins = split_products(pe, banks[o // 2][:, T * (o % 2):T * (o % 2) + T], part_hi(j)[:, o, :],
                                     part_lo(j)[:, o, :], he_hi[:, k, :], he_lo[:, k, :],
                                     skip_group_check=True)
            return ins

        @block.tensor
        def _(pe):
            pe.wait_ge(V0.sem, V0.at("zeros"))
            def full(u, l):
                s = u % SLOTS
                turn = u // SLOTS
                pe.wait_ge(ring_full[s], l * (16 * PER_LAYER[s]) + 16 * (2 + turn + 1))

            def tiles(bank, place, w_ap, c0, nk, rhs, m, width=P):
                for k in range(nk):
                    ins = pe.matmul(bank[0:width, place * T:place * T + T], w_ap[:, k, c0:c0 + width],
                                    rhs[:, k, :], start=(k == 0), stop=(k == nk - 1))
                return ins

            pe.wait_ge(loaded, 16 * 5)
            for u in range(12):
                pe.wait_ge(V0.sem, V0.at(f"sum{u}"))
                for m in range(4):
                    pe.matmul(banks[7][:, 4 * u + m:4 * u + m + 1], unit_sums[u][:, P * m:P * m + P],
                              ones[:, 0:1], start=True, stop=True)
            pe.drain().then_inc(P0.sem, P0.one("mods"))
            pe.drain().then_inc(MP.sem, MP.first)
            with pe.Fori(0, 2) as l:
                def job(name):
                    if name in before:
                        old, by = before[name]
                        who = AC if by == "act" else DV
                        pe.wait_ge(who.sem, who.at(old, l))
                    return bank_of[name]

                def mean_squares(name, sq, n, lhs=ones, width=T, off=0):
                    b = job(name)
                    for k in range(n):
                        ins = pe.matmul(b[:, 0:width], lhs, sq[:, k, :], start=(k == 0), stop=(k == n - 1))
                    ins.then_inc(PE.sem, PE.one(name))

                def pair_tiles(name, u, j0, rhs, nk, n=2):
                    b = job(name)
                    for i in range(n):
                        ins = tiles(b, i, slot(u, nk, UNITS[u][3]), P * (j0 + i), nk, rhs, P)
                    ins.then_inc(PE.sem, PE.one(name))

                pe.wait_ge(AC.sem, AC.at("sq1", l))
                mean_squares("norm1", h_t, KT)
                pe.wait_ge(DV.sem, DV.at("h1", l))
                full(0, l)
                pair_tiles("f0", 0, 0, h_t, KT)
                pair_tiles("f1", 0, 2, h_t, KT)
                full(1, l)
                pair_tiles("q0", 1, 0, h_t, KT)
                pair_tiles("q1", 1, 2, h_t, KT)
                full(2, l)
                for t in range(TT):
                    b = job(f"v{t}")
                    for k in range(KT):
                        ins = pe.matmul(b[:, :], h_t[:, k, P * t:P * t + P], slot(2, KT, 512)[:, k, :],
                                        start=(k == 0), stop=(k == KT - 1))
                    ins.then_inc(PE.sem, PE.one(f"v{t}"))

                def fill(name):
                    if name.startswith("hgate"):
                        i = int(name[-1])
                        if i == 0:
                            full(3, l)
                        pair_tiles(name, 3, 2 * i, h_t, KT)
                    elif name.startswith("gates"):
                        i = int(name[-1])
                        if i % 2 == 0:
                            full(6 + i // 2, l)
                        pair_tiles(name, 6 + i // 2, 2 * (i % 2), h_t, KT)
                    elif name == "cq0":
                        full(4, l)
                        pair_tiles(name, 4, 0, h_t, KT)
                    elif name == "cq1":
                        pair_tiles(name, 4, 2, h_t, KT, n=1)
                    elif name == "ckv":
                        full(5, l)
                        pair_tiles(name, 5, 0, h_t, KT)
                    else:
                        b = job("kr")
                        tiles(b, 0, slot(5, KT, KVL + ROPE), KVL, KT, h_t, P, width=ROPE)\
                            .then_inc(PE.sem, PE.one("kr"))

                fills = list(FILL)
                for i, name in enumerate(MASKED):
                    if i == 0:
                        pe.wait_ge(DV.sem, DV.at("fk", l))
                        pe.wait_ge(AC.sem, AC.at("q1", l))
                    else:
                        pe.wait_ge(DV.sem, DV.at(f"qk {name}", l))
                    qs, ks = (qf, kf) if i == 0 else (qd[i % 2], kd[i % 2])
                    for t in range(TT):
                        b = job(f"{name} t{t}")
                        for h in range(HH):
                            ins = pe.matmul(b[:, P * h:P * h + P], ks[:, h, P * t:P * t + P],
                                            qs[:, h, P * t:P * t + P], start=True, stop=True)
                        ins.then_inc(PE.sem, PE.one(f"{name} t{t}"))
                    fill(fills.pop(0))
                pe.wait_ge(DV.sem, DV.at(f"qk L{P}", l))
                b = job("cross")
                for h in range(HH):
                    ins = pe.matmul(b[:, P * h:P * h + P], kd[0][:, h, 0:P], qd[0][:, h, P:T],
                                    start=True, stop=True)
                ins.then_inc(PE.sem, PE.one("cross"))
                fill(fills.pop(0))
                fill(fills.pop(0))
                pe.wait_ge(DV.sem, DV.at("L64 t1", l))
                pe.wait_ge(AC.sem, AC.at("cross", l))
                for i in range(2):
                    b = job(f"o{i}")
                    for h in (2 * i, 2 * i + 1):
                        o = b[:, T * (h % 2):T * (h % 2) + T]
                        v = lambda t: vt[:, t, DK * h:DK * h + DK]
                        pe.matmul(o[:, 0:P], v(0), pairs[0][:, h, :], start=True, stop=True)
                        pe.matmul(o[:, P:T], v(0), cross[:, h, :], start=True, stop=False)
                        ins = pe.matmul(o[:, P:T], v(1), pairs[1][:, h, :], start=False, stop=True)
                    ins.then_inc(PE.sem, PE.one(f"o{i}"))
                for name in fills:
                    fill(name)
                pe.wait_ge(AC.sem, AC.at("c sq", l))
                mean_squares("cq norm", csq[:, 0:3, :], 3)
                mean_squares("ckv norm", csq[:, 3:5, :], 2)
                for i in range(2):
                    b = job(f"o norm{i}")
                    pe.matmul(b[:, :], ones, osq[:, 2 * i:2 * i + 2, :], start=True, stop=True)\
                        .then_inc(PE.sem, PE.one(f"o norm{i}"))
                pe.wait_ge(DV.sem, DV.at("cn", l))
                full(10, l)
                wq = slot(10, 3, NH * DQK)
                for i in range(4):
                    b = job(f"q up{i}")
                    for j in range(2):
                        ins = tiles(b, j, wq, DQK * (2 * i + j), 3, cq, P, width=DQK)
                    ins.then_inc(PE.sem, PE.one(f"q up{i}"))
                full(11, l)
                wkv = slot(11, 2, NH * (NOPE + VD))
                for i in range(4):
                    b = job(f"k up{i}")
                    for j in range(2):
                        ins = tiles(b, j, wkv, (NOPE + VD) * (2 * i + j), 2, ckv, P, width=NOPE)
                    ins.then_inc(PE.sem, PE.one(f"k up{i}"))
                for t in range(TT):
                    b = job(f"v up{t}")
                    for k in range(2):
                        ins = pe.matmul(b[:, :], ckv[:, k, P * t:P * t + P],
                                        wkv[:, k, :].rearrange("p (h c) -> p h c", h=NH)[:, :, NOPE:NOPE + VD],
                                        start=(k == 0), stop=(k == 1))
                    ins.then_inc(PE.sem, PE.one(f"v up{t}"))
                turn = const("turn")[NOPE:DQK, :]
                for i in range(4):
                    pe.wait_ge(AC.sem, AC.at(f"q up{i}", l))
                    b = job(f"q turn{i}")
                    pe.matmul(b[0:DQK, :], turn, q_a[NOPE:DQK, 2 * i:2 * i + 2, :], start=True, stop=True)\
                        .then_inc(PE.sem, PE.one(f"q turn{i}"))
                pe.wait_ge(AC.sem, AC.at("kr", l))
                b = job("k turn")
                pe.matmul(b[0:DQK, 0:T], turn, krs[NOPE:DQK, :], start=True, stop=True)\
                    .then_inc(PE.sem, PE.one("k turn"))
                pe.wait_ge(DV.sem, DV.at("k turn", l))
                pe.wait_ge(AC.sem, AC.at("v up1", l))
                attention_pe(pe, job, PE, AC, DV, l, "",
                             lambda h, t: q_a[0:DQK, h, P * t:P * t + P],
                             lambda h, n: k_a[0:DQK, h, 0:n],
                             lambda h, t: v_a[:, t, VD * h:VD * h + VD], p_a, pT_a, ident)
                pe.wait_ge(DV.sem, DV.at("oa", l))
                full(12, l)
                for i in range(4):
                    pair_tiles(f"ya{i}", 12, 2 * i, oa, 4)
                pe.wait_ge(AC.sem, AC.at("ov3", l))
                full(13, l)
                for i in range(4):
                    pair_tiles(f"yb{i}", 13, 2 * i, ob, 4)
                pe.wait_ge(DV.sem, DV.at("yb3", l))
                for i in range(4):
                    if i % 2 == 0:
                        full(14 + i // 2, l)
                    pair_tiles(f"out{i}", 14 + i // 2, 2 * (i % 2), h_t, KT)
                pe.wait_ge(AC.sem, AC.at("sq2", l))
                mean_squares("norm2", h_t, KT)
                pe.wait_ge(DV.sem, DV.at("h2", l))
                b = job("router")
                for t in range(TT):
                    for k in range(KT):
                        ins = pe.matmul(b[:, NE * t:NE * t + NE], h_t[:, k, P * t:P * t + P],
                                        wr[:, k, :], start=(k == 0), stop=(k == KT - 1))
                ins.then_inc(PE.sem, PE.one("router"))
                pe.wait_ge(DV.sem, DV.at("comb", l))
                b = job("combine")
                for t in range(TT):
                    ins = pe.transpose(b[0:NE, P * t:P * t + P], combw[:, NE * t:NE * t + NE], ident)
                ins.then_inc(PE.sem, PE.one("combine"))
                pe.wait_ge(DV.sem, DV.at("combine", l))

                clear_sums(pe)
                with pe.Fori(0, NE) as it:
                    e = l * NE + it
                    pe.wait_ge(MV.sem, MV.at("next", e - 1))
                    pe.matmul(banks[6][:, 0:T], ones16, pick, start=True, stop=True)\
                        .then_inc(MP.sem, MP.one("pick"))
                    for j in range(8):
                        m = j // 2
                        if j % 2 == 0:
                            pe.wait_ge(MV.sem, MV.at(f"he{m + 2}", e - 1) if m < 2 else MV.at(f"he{m - 2}", e))
                        pe.wait_ge(MV.sem, MV.at(f"lo{j}", e))
                        column_part(pe, j, banks[4 + m % 2][:, T * (j % 2):T * (j % 2) + T])\
                            .then_inc(MP.sem, MP.one(f"part{j}"))
                    pe.wait_ge(MV.sem, MV.at("acc", e))
                    for i in range(CH // P):
                        ins = pe.matmul(banks[7][:, i:i + 1], accs[:, P * i:P * i + P], ones[:, 0:1],
                                        start=True, stop=True)
                    ins.then_inc(MP.sem, MP.one("mods"))
                    for k in range(4):
                        pe.wait_ge(MV.sem, MV.at(f"he{k}", e))
                        pe.wait_ge(MV.sem, MV.at(f"lo{8 + k}", e))
                        row_part(pe, 8 + k, k).then_inc(MP.sem, MP.one(f"part{8 + k}"))
            def unit(u, base):
                s = A_SLOT[u] if base is A_BASE else u % SLOTS
                pe.wait_ge(ring_full[s], 16 * (base[s] + u // SLOTS + 1))

            def r_job(name):
                if name in r_old:
                    old, by = r_old[name]
                    who = AR if by == "act" else VR
                    pe.wait_ge(who.sem, who.at(old))
                return r_bank[name]

            def sum_squares(b, sq, n):
                for k in range(n):
                    ins = pe.matmul(b[:, 0:T], ones, sq[:, k, :], start=(k == 0), stop=(k == n - 1))
                return ins

            pe.wait_ge(AR.sem, AR.at("sq0"))
            sum_squares(r_job("final norm"), h_t, KT).then_inc(PR.sem, PR.one("final norm"))
            pe.wait_ge(AR.sem, AR.at("sq1"))
            sum_squares(r_job("norm1"), h_t, KT).then_inc(PR.sem, PR.one("norm1"))
            pe.wait_ge(VR.sem, VR.at("h1"))
            def lru_input(i):
                name = f"xr{i}" if i < 8 else f"gelu{i - 8}"
                if i % 2 == 0:
                    unit(i // 2, R_BASE)
                b = r_job(name)
                for j in range(2):
                    ins = tiles(b, j, slot(i // 2, KT, 352), LB * (2 * (i % 2) + j), KT, h_t, P, width=LB)
                ins.then_inc(PR.sem, PR.one(name))

            for i in range(12):
                lru_input(i)
            pe.wait_ge(VR.sem, VR.at("conv"))
            unit(8, R_BASE)
            pe.wait_ge(gate_half, 16)
            wg = slot(8, 2 * LN, LB, parts=LB)
            for n in range(LN):
                b = r_job(f"ri{n}")
                pe.matmul(b[LBS, 0:T], wg[:, n, :], xc[LBS, n, :], start=True, stop=True)
                pe.matmul(b[LBS, T:2 * T], wg[:, LN + n, :], xc[LBS, n, :], start=True, stop=True)\
                    .then_inc(PR.sem, PR.one(f"ri{n}"))
            for i in range(12, 16):
                lru_input(i)
            outs = [r_job(f"out{i}") for i in range(4)]
            for b in outs:
                pe.matmul(b[:, :], zeros[:, 0:P], zeros[:, :], start=True, stop=True, skip_group_check=True)
            pe.wait_ge(VR.sem, VR.at("y"))
            for u in range(4):
                unit(9 + u, R_BASE)
                wo = slot(9 + u, 4, D, parts=LB)
                for o in range(KT):
                    for k in range(4):
                        ins = pe.matmul(outs[o // 2][:, T * (o % 2):T * (o % 2) + T], wo[:, k, P * o:P * o + P],
                                        gelu[LBS, 4 * u + k, :], start=False, stop=False, skip_group_check=True)
                    if u == 3 and o % 2:
                        ins.then_inc(PR.sem, PR.one(f"out{o // 2}"))
            pe.wait_ge(AR.sem, AR.at("sq2"))
            sum_squares(r_job("norm2"), h_t, KT).then_inc(PR.sem, PR.one("norm2"))

            def mlp_pe(layer, h2):
                pe_steps, act_steps_, dve_steps_ = MLP[layer]
                pe.wait_ge(h2.sem, h2.at("h lo"))
                pe.drain().then_inc(pe_steps.sem, pe_steps.first)
                clear_sums(pe)
                with pe.Fori(0, MLP_TURNS) as e:
                    for m in range(4):
                        pe.wait_ge(act_steps_.sem, act_steps_.at(*[("g3", e - 1), ("g1", e - 1),
                                                                   ("g2", e - 1), ("g0", e)][m]))
                        pe.wait_ge(dve_steps_.sem, dve_steps_.at(f"lo{m}", e))
                        column_part(pe, m, banks[MLP_BANK[m]][:, 0:T])\
                            .then_inc(pe_steps.sem, pe_steps.one(f"part{m}"))
                    for k in range(4):
                        pe.wait_ge(dve_steps_.sem, dve_steps_.at(f"he{k}", e))
                        pe.wait_ge(dve_steps_.sem, dve_steps_.at(f"lo{4 + k}", e))
                        row_part(pe, 4 + k, k).then_inc(pe_steps.sem, pe_steps.one(f"part{4 + k}"))
                        if layer == 0 and k == 1:
                            pe.wait_ge(dve_steps_.sem, dve_steps_.at("acc1", e))
                            pe.wait_ge(kv_summed, e + 1)
                            at = 0
                            for i, n in enumerate(MLP_CHUNKS):
                                for c in range(n // P):
                                    ins = pe.matmul(banks[7][:, at:at + 1], accs2[i][:, P * c:P * c + P],
                                                    ones[:, 0:1], start=True, stop=True)
                                    at += 1
                            ins.then_inc(pe_steps.sem, pe_steps.one("mods"))

            mlp_pe(0, VR)

            def a_job(name):
                if name in a_old:
                    old, by = a_old[name]
                    who = AA if by == "act" else VA
                    pe.wait_ge(who.sem, who.at(old))
                return a_bank[name]

            pe.wait_ge(AA.sem, AA.at("sq"))
            sum_squares(a_job("norm"), h_t, KT).then_inc(PA.sem, PA.one("norm"))
            pe.wait_ge(VA.sem, VA.at("h"))

            def projected(name, u0, rhs):
                for i in range(4):
                    u = u0 + i // 2
                    if i % 2 == 0:
                        unit(u, A_BASE)
                    b = a_job(f"{name}{i}")
                    for j in range(2):
                        ins = tiles(b, j, slot(A_SLOT[u], KT, 512), P * (2 * (i % 2) + j), KT, rhs, P)
                    ins.then_inc(PA.sem, PA.one(f"{name}{i}"))

            def head_squares(name, sq):
                for i in range(4):
                    b = a_job(f"{name}{i}")
                    pe.matmul(b[:, :], heads_ones, sq[:, 2 * i:2 * i + 2, :], start=True, stop=True)\
                        .then_inc(PA.sem, PA.one(f"{name}{i}"))

            projected("k", 0, h_t)
            for i in range(4):
                u, t = 2 + i // 2, i % 2
                if t == 0:
                    unit(u, A_BASE)
                b = a_job(f"v{i}")
                for k in range(KT):
                    ins = pe.matmul(b[:, :], h_t[:, k, P * t:P * t + P], slot(u, KT, 512)[:, k, :],
                                    start=(k == 0), stop=(k == KT - 1))
                ins.then_inc(PA.sem, PA.one(f"v{i}"))
            pe.wait_ge(AA.sem, AA.at("k sq"))
            head_squares("kn", ksq)
            pe.wait_ge(VA.sem, VA.at("hq"))
            projected("q", 4, hq)
            pe.wait_ge(AA.sem, AA.at("q sq"))
            head_squares("qn", h_t)
            pe.wait_ge(VA.sem, VA.at("q"))
            for half, tag in enumerate(("A ", "B ")):
                attention_pe(pe, a_job, PA, AA, VA, 0, tag,
                             lambda h, t: q2_[:, 4 * half + h // 2, h % 2, P * t:P * t + P],
                             lambda h, n: k2_[:, 4 * half + h // 2, 0:n],
                             lambda h, t: v2_[:, t, HD * (8 * half + h):HD * (8 * half + h) + HD],
                             p2_, pT2, ident)
            pe.wait_ge(AA.sem, AA.at("B ov3"))
            projected("out", 8, o2_)
            pe.wait_ge(AA.sem, AA.at("sq2"))
            sum_squares(a_job("norm2"), h_t, KT).then_inc(PA.sem, PA.one("norm2"))
            mlp_pe(1, VA)

        @block.gpsimd
        def _(pool):
            with pool.Fori(0, MLP_TURNS) as e:
                pool.wait_ge(chunk2_full[2], e * 16 + 16)
                pool.wait_ge(MLP[0][0].sem, MLP[0][0].at("mods", e - 1))
                ck = chunks2[2]
                c = cact[:, KT:2 * KT].unsqueeze(2).broadcast_to([P, KT, MLP_CHUNKS[2]])
                nc.gpsimd.tensor_tensor(ck, ck, c, ALU.mult)
                for n in (4, 2, 1):
                    pool.drain()
                    out = ck[:, 0:n, :] if n > 1 else accs2[2].unsqueeze(1)
                    ins = nc.gpsimd.tensor_tensor(out, ck[:, 0:n, :], ck[:, n:2 * n, :], ALU.add)
                ins.then_inc(kv_summed, 1)

        def rstd(act, bank, out, n, width=T):
            act.activation(out, bank[:, 0:width], ACT.Ln, scale=1.0 / n, bias=epsb[:, 0:1])
            act.drain()
            return act.activation(out, out, ACT.Exp, scale=-0.5)

        @block.scalar
        def _(act):
            act.wait_ge(V0.sem, V0.at("zeros"))
            act.wait_ge(loaded, 16 * 5)
            act.activation(cact[:, :], col("c", 0, 2 * KT), ACT.Silu).then_inc(A0.sem, A0.one("c"))
            for u in range(12):
                if u == 6:
                    act.wait_ge(V0.sem, V0.at("angles"))
                    act.activation(trig[:, :], mix[:, 0:2 * T], ACT.Sin).then_inc(A0.sem, A0.one("trig"))
                    act.wait_ge(V0.sem, V0.at("lb"))
                    act.activation(lbs[:, 0:2 * HH], lbs[:, 0:2 * HH], ACT.Exp).then_inc(A0.sem, A0.one("lb"))
                act.wait_ge(ring_full[u % SLOTS], 16 * (u // SLOTS + 1))
                unit = slot(u, KT, 512)
                if u == 0:
                    act.drain()
                for k in range(KT):
                    ins = act.activation(unit[:, k, :], unit[:, k, :], ACT.Copy, scale=cact[:, k:k + 1])
                ins.then_inc(A0.sem, A0.one(f"mul{u}"))
            with act.Fori(0, 2) as l:
                def emptied(name, out, func, rows=P, width=512, **kw):
                    act.wait_ge(PE.sem, PE.at(name, l))
                    src = bank_of[name][0:rows, 0:width]
                    if len(out.shape) == 3:
                        src = src.rearrange("p (a b) -> p a b", a=out.shape[1])
                    act.activation(out, src, func, **kw).then_inc(AC.sem, AC.one(name))

                def two(t, i, n=2):
                    return t[:, 2 * i:2 * i + n, :]

                act.wait_ge(DV.sem, DV.at("mods", l))
                act.activation(h_t, x_t, ACT.Square).then_inc(AC.sem, AC.one("sq1"))
                act.wait_ge(PE.sem, PE.at("norm1", l))
                rstd(act, bank_of["norm1"], rs[:, 0, :], D).then_inc(AC.sem, AC.one("norm1"))
                for i in range(2):
                    emptied(f"f{i}", two(fwd, i), ACT.Sigmoid)
                for i in range(2):
                    emptied(f"q{i}", two(qf, i), ACT.Silu)
                for i in range(2):
                    emptied(f"v{i}", vt[:, i, :], ACT.Copy)

                def fill(name):
                    if name.startswith("hgate"):
                        emptied(name, two(hgate, int(name[-1])), ACT.Silu)
                    elif name.startswith("gates"):
                        emptied(name, two(gates, int(name[-1])), ACT.Sigmoid)
                    elif name == "kr":
                        act.wait_ge(PE.sem, PE.at(name, l))
                        act.activation(krs[NOPE:DQK, :], bank_of[name][0:ROPE, 0:T], ACT.Copy)\
                            .then_inc(AC.sem, AC.one(name))
                    elif name == "cq1":
                        emptied(name, cq[:, 2:3, :], ACT.Copy, width=T)
                    elif name == "cq0":
                        emptied(name, cq[:, 0:2, :], ACT.Copy)
                    else:
                        emptied(name, ckv, ACT.Copy)

                fills = list(FILL)
                for _ in MASKED:
                    fill(fills.pop(0))
                emptied("cross", cross, ACT.Copy, scale=DK ** -0.5)
                fill(fills.pop(0))
                fill(fills.pop(0))
                emptied("o0", two(oraw, 0), ACT.Copy)
                emptied("o1", two(oraw, 1), ACT.Copy)
                act.drain()
                act.activation(osq, oraw, ACT.Square).then_inc(AC.sem, AC.one("o sq"))
                for name in fills:
                    fill(name)
                act.activation(csq, view(cqkv, 0, 5, T), ACT.Square).then_inc(AC.sem, AC.one("c sq"))
                act.wait_ge(PE.sem, PE.at("cq norm", l))
                rstd(act, bank_of["cq norm"], rs[:, 0, :], QL).then_inc(AC.sem, AC.one("cq norm"))
                act.wait_ge(PE.sem, PE.at("ckv norm", l))
                rstd(act, bank_of["ckv norm"], rs[:, 1, :], KVL).then_inc(AC.sem, AC.one("ckv norm"))
                for i in range(2):
                    act.wait_ge(PE.sem, PE.at(f"o norm{i}", l))
                    rstd(act, bank_of[f"o norm{i}"], mix[:, 2048 + 512 * i:2560 + 512 * i], DK, 512)\
                        .then_inc(AC.sem, AC.one(f"o norm{i}"))
                act.wait_ge(DV.sem, DV.at("oa", l))
                for i in range(4):
                    emptied(f"q up{i}", q_a[0:DQK, 2 * i:2 * i + 2, :], ACT.Copy, rows=DQK)
                for i in range(4):
                    emptied(f"k up{i}", k_a[0:NOPE, 2 * i:2 * i + 2, :], ACT.Copy, rows=NOPE)
                for i in range(2):
                    emptied(f"v up{i}", v_a[:, i, :], ACT.Copy)
                attention_act(nc, act, lambda n: bank_of[n], PE, AC, DV, l, "", p_a, pT_a, ob, nmax, sums)
                act.wait_ge(DV.sem, DV.at("out3", l))
                act.activation(h_t, x_t, ACT.Square).then_inc(AC.sem, AC.one("sq2"))
                act.wait_ge(PE.sem, PE.at("norm2", l))
                rstd(act, bank_of["norm2"], rs[:, 0, :], D).then_inc(AC.sem, AC.one("norm2"))
                act.wait_ge(DV.sem, DV.at("h2", l))
                act.activation(h_hi, h_t, ACT.Copy).then_inc(AC.sem, AC.one("h hi"))
                emptied("router", scores, ACT.Sigmoid, width=TT * NE)
                with act.Fori(0, NE) as it:
                    e = l * NE + it

                    def round_part(j):
                        act.wait_ge(MP.sem, MP.at(f"part{(j + 8) % 12}", e - 1 if j < 4 else e))
                        if j in (0, 4):
                            act.wait_ge(gu_full[j // 4], e * 32 + 32)
                        if j == 8:
                            act.wait_ge(down_full, e * 16 + 16)
                        act.activation(part_hi(j), moe_raw(j), ACT.Copy).then_inc(MA.sem, MA.one(f"hi{j}"))

                    for j in range(5):
                        round_part(j)
                    for m in range(4):
                        act.wait_ge(MP.sem, MP.at(f"part{2 * m + 1}", e))
                        act.activation(sg[:, m, :], banks[4 + m % 2][:, 0:T], ACT.Silu)\
                            .then_inc(MA.sem, MA.one(f"sg{m}"))
                        for j in (2 * m + 5, 2 * m + 6):
                            if j < 12:
                                round_part(j)
            def norm_act(A, V, Pj, bank, sq, name, ready):
                act.wait_ge(V.sem, ready)
                act.activation(h_t, x_t, ACT.Square).then_inc(A.sem, A.one(sq))
                act.wait_ge(Pj.sem, Pj.at(name))
                rstd(act, bank[name], rs[:, 0, :], D).then_inc(A.sem, A.one(name))

            norm_act(AR, DV, PR, r_bank, "sq0", "final norm", DV.at("x2", 1))
            norm_act(AR, VR, PR, r_bank, "sq1", "norm1", VR.at("x"))
            act.activation(lam[2][LBS, :], lam[1][LBS, :], ACT.Exp, scale=-1.0)
            act.drain()
            act.activation(lam[2][LBS, :], lam[2][LBS, :], ACT.Ln, bias=epsb[LBS, 1:2])\
                .then_inc(AR.sem, AR.one("softplus"))
            for i in range(8):
                act.wait_ge(PR.sem, PR.at(f"xr{i}"))
                act.activation(xr[LBS, 2 * i:2 * i + 2, 3:T + 3],
                               r_bank[f"xr{i}"][LBS, :].rearrange("p (a b) -> p a b", a=2), ACT.Copy)\
                    .then_inc(AR.sem, AR.one(f"xr{i}"))
            def gelu_act(i):
                act.wait_ge(PR.sem, PR.at(f"gelu{i}"))
                act.activation(gelu[LBS, 2 * i:2 * i + 2, :],
                               r_bank[f"gelu{i}"][LBS, :].rearrange("p (a b) -> p a b", a=2),
                               ACT.Gelu_apprx_tanh).then_inc(AR.sem, AR.one(f"gelu{i}"))

            for i in range(4):
                gelu_act(i)
            for n in range(LN):
                act.wait_ge(PR.sem, PR.at(f"ri{n}"))
                b = r_bank[f"ri{n}"]
                act.activation(rg[LBS, n, :], b[LBS, 0:T], ACT.Sigmoid, bias=col("ba", n)[LBS, :])
                act.activation(ig[LBS, n, :], b[LBS, T:2 * T], ACT.Sigmoid, bias=col("bx", n)[LBS, :])\
                    .then_inc(AR.sem, AR.one(f"ri{n}"))
            act.drain()
            for n in range(LN):
                act.wait_ge(VR.sem, VR.at(f"ix{n // 4}"))
                ins = act.activation(xc[LBS, n, :], rg[LBS, n, :], ACT.Tanh, scale=lam[3][LBS, n:n + 1])
            ins.then_inc(AR.sem, AR.one("tanh"))
            for n in range(LN):
                ins = act.activation(rg[LBS, n, :], rg[LBS, n, :], ACT.Exp, scale=lam[4][LBS, n:n + 1])
            ins.then_inc(AR.sem, AR.one("decay"))
            for i in range(4, 8):
                gelu_act(i)
            act.wait_ge(VR.sem, VR.at("u"))
            act.activation(xc[LBS, :, :], xc[LBS, :, :], ACT.Sqrt).then_inc(AR.sem, AR.one("root"))
            norm_act(AR, VR, PR, r_bank, "sq2", "norm2", VR.at("out3"))

            def round_stream(A, V):
                act.wait_ge(V.sem, V.at("h2"))
                act.activation(h_hi, h_t, ACT.Copy).then_inc(A.sem, A.one("h hi"))

            round_stream(AR, VR)

            def mlp_act(layer, base):
                pe_steps, act_steps_, dve_steps_ = MLP[layer]
                act.drain().then_inc(act_steps_.sem, act_steps_.first)
                with act.Fori(0, MLP_TURNS // 2) as it:
                    for pair in range(2):
                        e = it * 2 + pair
                        slots = MLP_SLOTS[layer][2 * pair:2 * pair + 2]

                        def round_part(j):
                            pe_turn = e - 1 if j < 4 else e
                            act.wait_ge(pe_steps.sem, pe_steps.at(f"part{(j + 4) % 8}", pe_turn))
                            if j % 4 == 0:
                                s = slots[j // 4]
                                act.wait_ge(ring_full[s], it * 16 + 16 * (base[s] + 1))
                            act.activation(part_hi(j), mlp_raw(slots, j), ACT.Copy)\
                                .then_inc(act_steps_.sem, act_steps_.one(f"hi{j}"))

                        for j in range(4):
                            round_part(j)
                            if layer == 0 and j in (0, 2):
                                i = j // 2
                                act.wait_ge(chunk2_full[i], e * 16 + 16)
                                for k in range(KT):
                                    ins = act.activation(chunks2[i][:, k, :], chunks2[i][:, k, :], ACT.Copy,
                                                         scale=cact[:, KT + k:KT + k + 1])
                                ins.then_inc(act_steps_.sem, act_steps_.one(f"mul{i}"))
                        for m in range(4):
                            act.wait_ge(pe_steps.sem, pe_steps.at(f"part{m}", e))
                            act.activation(sg[:, m, :], banks[MLP_BANK[m]][:, 0:T], ACT.Relu)
                            act.drain()
                            act.activation(he[:, m, :], sg[:, m, :], ACT.Square)\
                                .then_inc(act_steps_.sem, act_steps_.one(f"g{m}"))
                            round_part(m + 4)

            mlp_act(0, M0_BASE)
            norm_act(AA, VA, PA, a_bank, "sq", "norm", VA.at("mods"))

            def taken(name, out):
                act.wait_ge(PA.sem, PA.at(name))
                src = a_bank[name][:, :]
                if len(out.shape) == 3:
                    src = src.rearrange("p (a b) -> p a b", a=2)
                act.activation(out, src, ACT.Copy).then_inc(AA.sem, AA.one(name))

            def head_norm(name, out):
                for i in range(4):
                    act.wait_ge(PA.sem, PA.at(f"{name}{i}"))
                    rstd(act, a_bank[f"{name}{i}"], out[:, 512 * i:512 * i + 512], HD, 512)\
                        .then_inc(AA.sem, AA.one(f"{name}{i}"))

            for i in range(4):
                taken(f"k{i}", k2_[:, 2 * i:2 * i + 2, :])
            act.drain()
            act.activation(ksq, k2_, ACT.Square).then_inc(AA.sem, AA.one("k sq"))
            for i in range(4):
                taken(f"v{i}", v2_[:, i % 2, 512 * (i // 2):512 * (i // 2) + 512])
            head_norm("kn", mix[:, 8192:10240])
            for i in range(4):
                act.wait_ge(PA.sem, PA.at(f"q{i}"))
                for rows, j in own:
                    ins = act.activation(q2_[rows, 2 * i:2 * i + 2, j, :],
                                         a_bank[f"q{i}"][rows, :].rearrange("p (a b) -> p a b", a=2), ACT.Copy)
                ins.then_inc(AA.sem, AA.one(f"q{i}"))
            act.drain()
            for rows, j in own:
                ins = act.activation(h_t[rows, :, :], q2_[rows, :, j, :], ACT.Square)
            ins.then_inc(AA.sem, AA.one("q sq"))
            head_norm("qn", mix[:, 11264:13312])
            for half, tag in enumerate(("A ", "B ")):
                attention_act(nc, act, lambda n: a_bank[n], PA, AA, VA, 0, tag, p2_, pT2,
                              o2_[:, 4 * half:4 * half + 4, :], nmax, sums)
            norm_act(AA, VA, PA, a_bank, "sq2", "norm2", VA.at("out3"))
            round_stream(AA, VA)
            mlp_act(1, M1_BASE)

        def routing():
            tt, ts = nc.vector.tensor_tensor, nc.vector.tensor_scalar
            wait = nc.vector.drain
            at = [0]

            def cols(*shape):
                n = int(np.prod(shape))
                ap = sm[:, at[0]:at[0] + n]
                at[0] += n
                if len(shape) == 3:
                    return ap.rearrange("p (a b c) -> p a b c", a=shape[0], b=shape[1])
                return ap.rearrange("p (a b) -> p a b", a=shape[0])

            s = scores.rearrange("p (t e) -> p t e", t=TT)
            v = biased.rearrange("p (t e) -> p t e", t=TT)
            tt(v, s, heads(rbias, TT), ALU.add)
            wait()
            g = biased.rearrange("p (g e) -> p g e", g=TT * NG)
            sums6 = cols(TT * NG, 6)
            tt(sums6[:, :, 0:3], g[:, :, 0:3], g[:, :, 1:4], ALU.add)
            tt(sums6[:, :, 3:5], g[:, :, 0:2], g[:, :, 2:4], ALU.add)
            tt(sums6[:, :, 5:6], g[:, :, 0:1], g[:, :, 3:4], ALU.add)
            wait()
            score = cols(TT, NG)
            nc.vector.tensor_reduce(score.rearrange("p t g -> p (t g)"), sums6, AX, ALU.max)

            def first_best(x, n, order):
                top = cols(TT, 1)
                wait()
                nc.vector.tensor_reduce(top.rearrange("p t a -> p (t a)"), x, AX, ALU.max)
                wait()
                is_top = cols(TT, n)
                tt(is_top, x, top.broadcast_to([P, TT, n]), ALU.is_equal)
                wait()
                tt(is_top, is_top, heads(order, TT), ALU.mult)
                wait()
                lowest = cols(TT, 1)
                nc.vector.tensor_reduce(lowest.rearrange("p t a -> p (t a)"), is_top, AX, ALU.max)
                wait()
                tt(is_top, is_top, lowest.broadcast_to([P, TT, n]), ALU.is_equal)
                wait()
                return is_top

            order = cols(1, NE)[:, 0, :]
            for i in range(NE):
                nc.vector.memset(order[:, i:i + 1], float(NE - i))
            best = first_best(score, NG, order[:, 0:NG])
            inside = cols(TT * NG, EG)
            nc.vector.tensor_copy(inside, best.rearrange("p t g -> p (t g)").unsqueeze(2)
                                  .broadcast_to([P, TT * NG, EG]))
            wait()
            left = cols(TT * NG, EG)
            out = cols(TT * NG, EG)
            tt(left, g, inside, ALU.mult)
            ts(out, inside, -NEG, NEG, ALU.mult, ALU.add)
            wait()
            tt(left, left, out, ALU.add)
            wait()
            flat = lambda ap: ap.rearrange("p g e -> p (g e)").rearrange("p (t e) -> p t e", t=TT)
            one = first_best(flat(left), NE, order)
            ts(out, one.rearrange("p t e -> p (t e)").rearrange("p (g e) -> p g e", e=EG), 2 * NEG, None, ALU.mult)
            wait()
            tt(left, left, out, ALU.add)
            two = first_best(flat(left), NE, order)
            tt(one, one, two, ALU.add)
            wait()
            tt(one, one, s, ALU.mult)
            wait()
            total = cols(TT, 1)
            nc.vector.tensor_reduce(total.rearrange("p t a -> p (t a)"), one, AX, ALU.add)
            wait()
            nc.vector.reciprocal(total, total)
            wait()
            tt(combw.rearrange("p (t e) -> p t e", t=TT), one, total.broadcast_to([P, TT, NE]), ALU.mult)

        @block.vector
        def _(dve):
            tt, ts, stt = nc.vector.tensor_tensor, nc.vector.tensor_scalar, nc.vector.scalar_tensor_tensor
            nc.vector.memset(zeros[:, :], 0.0)
            nc.vector.memset(epsb[:, 0:1], EPS)
            nc.vector.memset(epsb[:, 1:2], 1.0)
            dve.drain().then_inc(V0.sem, V0.one("zeros"))
            dve.drain().then_inc(MV.sem, MV.first)
            dve.wait_ge(loaded, 16 * 5)
            ang, n = mix[:, 2 * T:3 * T], mix[:, 3 * T:4 * T]
            nc.vector.tensor_copy(ang, posi[:, :])
            dve.drain()
            ts(ang, ang, const("freq"), None, ALU.mult)
            dve.drain()
            for out, quarter in ((mix[:, 0:T], 0.25), (mix[:, T:2 * T], 0.0)):
                ts(n, ang, 1.0 / TWO_PI, quarter, ALU.mult, ALU.add)
                dve.drain()
                ts(n, n, MAGIC, None, ALU.add)
                dve.drain()
                ts(n, n, -MAGIC, None, ALU.add)
                dve.drain()
                stt(out, n, -C1, ang, ALU.mult, ALU.add)
                dve.drain()
                stt(out, n, -C2, out, ALU.mult, ALU.add)
                dve.drain()
                stt(out, n, -C3, out, ALU.mult, ALU.add)
                dve.drain()
                if quarter:
                    ts(out, out, float(np.pi / 2), None, ALU.add)
                    dve.drain()
                ts(out, out, 3.1415925, -3.1415925, ALU.min, ALU.max)
            dve.drain().then_inc(V0.sem, V0.one("angles"))
            a0, a1 = col("lb", 0, HH), col("lb", HH, HH)
            top = small[:, 0:HH]
            tt(top, a0, a1, ALU.max)
            dve.drain()
            tt(lbs[:, 0:HH], a0, top, ALU.subtract)
            tt(lbs[:, HH:2 * HH], a1, top, ALU.subtract).then_inc(V0.sem, V0.one("lb"))

            def unit_sum(u):
                dve.wait_ge(A0.sem, A0.at(f"mul{u}"))
                nc.vector.tensor_reduce(unit_sums[u], slot(u, KT, 512).rearrange("p k n -> p n k"), AX, ALU.add)\
                    .then_inc(V0.sem, V0.one(f"sum{u}"))

            for u in range(6):
                unit_sum(u)
            dve.wait_ge(A0.sem, A0.at("lb"))
            e0, e1, total = small[:, 4:8], small[:, 8:12], small[:, 12:16]
            tt(total, lbs[:, 0:HH], lbs[:, HH:2 * HH], ALU.add)
            dve.drain()
            nc.vector.reciprocal(total, total)
            dve.drain()
            tt(e0, lbs[:, 0:HH], total, ALU.mult)
            tt(e1, lbs[:, HH:2 * HH], total, ALU.mult)
            dve.drain()
            tt(lbs[:, 0:HH], e0, e0, ALU.subtract)
            tt(total, e0, e1, ALU.add)
            dve.drain()
            tt(lbs[:, 2 * HH:3 * HH], total, e0, ALU.subtract)
            dve.drain()
            for i in range(2):
                ts(lbs[:, (2 * i + 1) * HH:(2 * i + 2) * HH], lbs[:, 2 * i * HH:(2 * i + 1) * HH], -1.0, 1.0,
                   ALU.mult, ALU.add)
            for u in range(6, 12):
                unit_sum(u)
            dve.wait_ge(x_loaded, 16)
            dve.wait_ge(P0.sem, P0.at("mods"))
            tt(modn[:, 0:MODS], banks[7][:, 0:MODS], col("ada_b", 0, MODS), ALU.add)
            dve.drain().then_inc(V0.sem, V0.one("mods"))

            def modulated(src, gain_scale, shift, r):
                tt(h_t, src, heads(r, KT), ALU.mult)
                dve.drain()
                for k in range(KT):
                    ins = ts(h_t[:, k, :], h_t[:, k, :], gain_scale[:, k:k + 1], shift[:, k:k + 1],
                             ALU.mult, ALU.add)
                return ins

            with dve.Fori(0, 2) as l:
                bank = lambda name: bank_of[name]
                nc.vector.tensor_copy(lp[:, :], par[:, bass.ds(l * LP, LP)])
                nc.vector.tensor_copy(lbl[:, :], lbs[:, bass.ds(l * (2 * HH), 2 * HH)])
                nc.vector.tensor_copy(mod[:, :], modn[:, 0:MODS])
                dve.drain()
                stt(amod[:, 0:KT], mod[:, KT:2 * KT], 1.0, lp[:, N1G:N1G + KT], ALU.add, ALU.mult)
                stt(amod[:, KT:2 * KT], mod[:, 4 * KT:5 * KT], 1.0, lp[:, N2G:N2G + KT], ALU.add, ALU.mult)
                dve.drain().then_inc(DV.sem, DV.one("mods"))
                dve.wait_ge(AC.sem, AC.at("norm1", l))
                modulated(x_t, amod[:, 0:KT], mod[:, 0:KT], rs[:, 0, :]).then_inc(DV.sem, DV.one("h1"))
                dve.wait_ge(AC.sem, AC.at("f1", l))
                nc.vector.memset(bwd, 1.0)
                for h in range(HH):
                    ts(fwd[:, h, :], fwd[:, h, :], lbl[:, HH + h:HH + h + 1], lbl[:, h:h + 1], ALU.mult, ALU.add)
                dve.drain()
                ts(kf, fwd, -1.0, 1.0, ALU.mult, ALU.add).then_inc(DV.sem, DV.one("fk"))

                def halves(t, n):
                    return t.rearrange("p h t -> p (h t)").rearrange("p (b two n) -> p b two n", two=2, n=n)

                def weigh(n, i):
                    if n <= 2:
                        tt(qd[i], qf, fwd, ALU.mult)
                        return tt(kd[i], kf, bwd, ALU.mult)
                    s = lambda t, half: halves(t, n)[:, :, half, :]
                    tt(s(qd[i], 1), s(qf, 1), s(fwd, 1), ALU.mult)
                    return tt(s(kd[i], 0), s(kf, 0), s(bwd, 0), ALU.mult)

                def pair_sums(i, first):
                    name = MASKED[i]
                    mask = heads(const("pair")[:, P * i:P * i + P], HH)
                    for t in range(TT):
                        dve.wait_ge(PE.sem, PE.at(f"{name} t{t}", l))
                        out = pairs[t] if first else tmps[t]
                        ins = tt(out, bank(f"{name} t{t}")[:, :].rearrange("p (h n) -> p h n", h=HH),
                                 mask, ALU.mult)
                        if t == 0 or first:
                            ins.then_inc(DV.sem, DV.one(f"{name} t{t}"))
                    dve.drain()
                    if not first:
                        for t in range(TT):
                            ins = tt(pairs[t], pairs[t], tmps[t], ALU.add)
                        ins.then_inc(DV.sem, DV.one(f"{name} t1"))

                dve.drain()
                dve.wait_ge(AC.sem, AC.at("q1", l))
                weigh(1, 1).then_inc(DV.sem, DV.one("qk L1"))
                pair_sums(0, True)
                for i, n in enumerate(LEVELS):
                    f, b = halves(fwd, n), halves(bwd, n)
                    nb = HH * T // (2 * n)
                    wide = lambda ap: ap.broadcast_to([P, nb, n])
                    tt(b[:, :, 0, :], b[:, :, 0, :], wide(f[:, :, 1, n - 1:n]), ALU.mult)
                    dve.drain()
                    tt(f[:, :, 1, :], f[:, :, 1, :], wide(f[:, :, 0, n - 1:n]), ALU.mult)
                    dve.drain()
                    weigh(2 * n, i % 2).then_inc(DV.sem, DV.one(f"qk L{2 * n}"))
                    pair_sums(i + 1, False)
                dve.wait_ge(AC.sem, AC.at("ckv norm", l))
                tt(cq, cq, heads(rs[:, 0, :], 3), ALU.mult)
                tt(ckv, ckv, heads(rs[:, 1, :], 2), ALU.mult)
                dve.drain()
                for k in range(3):
                    ts(cq[:, k, :], cq[:, k, :], lp[:, QNG + k:QNG + k + 1], None, ALU.mult)
                for k in range(2):
                    ins = ts(ckv[:, k, :], ckv[:, k, :], lp[:, KVNG + k:KVNG + k + 1], None, ALU.mult)
                ins.then_inc(DV.sem, DV.one("cn"))
                dve.wait_ge(AC.sem, AC.at("o norm1", l))
                tt(oa, oraw, ors, ALU.mult)
                dve.drain()
                for h in range(HH):
                    ins = stt(oa[:, h, :], oa[:, h, :], lp[:, HGN + h:HGN + h + 1], hgate[:, h, :],
                              ALU.mult, ALU.mult)
                ins.then_inc(DV.sem, DV.one("oa"))
                rows = slice(NOPE, DQK)
                for i in range(4):
                    dve.wait_ge(PE.sem, PE.at(f"q turn{i}", l))
                    q2 = q_a[rows, 2 * i:2 * i + 2, :]
                    t2 = mix[rows, 8192 + 512 * i:8704 + 512 * i].rearrange("p (a b) -> p a b", a=2)
                    tt(t2, bank(f"q turn{i}")[rows, :].rearrange("p (a b) -> p a b", a=2),
                       heads(sin[rows, :], 2), ALU.mult)
                    tt(q2, q2, heads(cos[rows, :], 2), ALU.mult)
                    dve.drain()
                    tt(q2, q2, t2, ALU.add).then_inc(DV.sem, DV.one(f"q turn{i}"))
                dve.wait_ge(PE.sem, PE.at("k turn", l))
                t1 = mix[rows, 8192 + 2048:8192 + 2048 + T]
                tt(t1, bank("k turn")[rows, 0:T], sin[rows, :], ALU.mult)
                tt(krs[rows, :], krs[rows, :], cos[rows, :], ALU.mult)
                dve.drain()
                tt(krs[rows, :], krs[rows, :], t1, ALU.add)
                dve.drain()
                nc.vector.tensor_copy(k_a[rows, :, :], heads(krs[rows, :], NH)).then_inc(DV.sem, DV.one("k turn"))
                future = const("future")
                attention_dve(nc, dve, bank, PE, AC, DV, l, "", DQK ** -0.5,
                              lambda g, nh, n: heads(future[:, 2 * P - n:2 * P], nh), p_a, nmax, sums)
                two = lambda t, i: t[:, 2 * i:2 * i + 2, :]
                half = lambda name: bank(name)[:, :].rearrange("p (a b) -> p a b", a=2)
                for i in range(4):
                    dve.wait_ge(PE.sem, PE.at(f"ya{i}", l))
                    tt(two(h_t, i), half(f"ya{i}"), two(gates, i), ALU.mult).then_inc(DV.sem, DV.one(f"ya{i}"))
                for i in range(4):
                    dve.wait_ge(PE.sem, PE.at(f"yb{i}", l))
                    t2 = view(mix, 5120 + 512 * i, 2, T)
                    tt(t2, half(f"yb{i}"), two(gates, 4 + i), ALU.mult)
                    dve.drain()
                    tt(two(h_t, i), two(h_t, i), t2, ALU.add).then_inc(DV.sem, DV.one(f"yb{i}"))
                for i in range(4):
                    dve.wait_ge(PE.sem, PE.at(f"out{i}", l))
                    for k in (2 * i, 2 * i + 1):
                        ins = stt(x_t[:, k, :], bank(f"out{i}")[:, T * (k % 2):T * (k % 2) + T],
                                  mod[:, 2 * KT + k:2 * KT + k + 1], x_t[:, k, :], ALU.mult, ALU.add)
                    ins.then_inc(DV.sem, DV.one(f"out{i}"))
                dve.wait_ge(AC.sem, AC.at("norm2", l))
                modulated(x_t, amod[:, KT:2 * KT], mod[:, 3 * KT:4 * KT], rs[:, 0, :])\
                    .then_inc(DV.sem, DV.one("h2"))
                dve.wait_ge(AC.sem, AC.at("h hi", l))
                tt(h_lo, h_t, as_f32(h_hi), ALU.subtract).then_inc(DV.sem, DV.one("h lo"))
                dve.wait_ge(AC.sem, AC.at("router", l))
                routing()
                dve.drain().then_inc(DV.sem, DV.one("comb"))
                dve.wait_ge(PE.sem, PE.at("combine", l))
                nc.vector.tensor_copy(combt, bank("combine")[0:NE, 0:T])
                dve.drain()
                ts(pick, combt, ident[0:NE, 0:1], None, ALU.mult)
                dve.drain().then_inc(DV.sem, DV.one("combine"))
                with dve.Fori(0, NE) as it:
                    e = l * NE + it

                    def rest_of_part(j):
                        dve.wait_ge(MA.sem, MA.at(f"hi{j}", e))
                        tt(part_lo(j), moe_raw(j), as_f32(part_hi(j)), ALU.subtract)\
                            .then_inc(MV.sem, MV.one(f"lo{j}"))

                    def hidden(m):
                        dve.wait_ge(MA.sem, MA.at(f"sg{m}", e))
                        tt(tg[:, m, :], sg[:, m, :], banks[6][:, 0:T], ALU.mult)
                        dve.drain()
                        up = banks[4 + m % 2][:, T:2 * T]
                        tt(he_hi[:, m, :], tg[:, m, :], up, ALU.mult)
                        tt(he[:, m, :], tg[:, m, :], up, ALU.mult)
                        dve.drain()
                        tt(he_lo[:, m, :], he[:, m, :], as_f32(he_hi[:, m, :]), ALU.subtract)\
                            .then_inc(MV.sem, MV.one(f"he{m}"))

                    rest_of_part(0)
                    dve.wait_ge(chunk_full, e * 16 + 16)
                    ck = chunk.rearrange("p (k n) -> p k n", k=KT)
                    cs = cact[:, bass.ds(l * KT, KT)].unsqueeze(2).broadcast_to([P, KT, CH])
                    tt(ck, ck, cs, ALU.mult)
                    rest_of_part(1)
                    rest_of_part(2)
                    dve.drain()
                    nc.vector.tensor_reduce(accs, chunk.rearrange("p (k n) -> p n k", k=KT), AX, ALU.add)\
                        .then_inc(MV.sem, MV.one("acc"))
                    rest_of_part(3)
                    rest_of_part(4)
                    hidden(0)
                    rest_of_part(5)
                    rest_of_part(6)
                    for m in (1, 2):
                        hidden(m)
                        rest_of_part(2 * m + 5)
                        rest_of_part(2 * m + 6)
                    hidden(3)
                    ts(pick, combt, ident[0:NE, bass.ds(it + 1, 1)], None, ALU.mult)\
                        .then_inc(MV.sem, MV.one("next"))
                    dve.wait_ge(MP.sem, MP.at("mods", e))
                    tt(modn[:, bass.ds(it * 3, 3)], banks[7][:, 0:3],
                       par[:, bass.ds(l * MODS + it * 3 + (COLS["ada_b"][0] + MODS), 3)], ALU.add)\
                        .then_inc(MV.sem, MV.one("mods"))
                    rest_of_part(11)
                dve.wait_ge(MP.sem, MP.at("part11", l * NE + (NE - 1)))
                for k in range(KT):
                    stt(x_t[:, k, :], banks[k // 2][:, T * (k % 2):T * (k % 2) + T],
                        mod[:, 5 * KT + k:5 * KT + k + 1], x_t[:, k, :], ALU.mult, ALU.add)
                dve.drain().then_inc(DV.sem, DV.one("x2"))
            def modulation(n1, n2):
                nc.vector.tensor_copy(mod[:, :], modn[:, 0:MODS])
                dve.drain()
                stt(amod[:, 0:KT], mod[:, KT:2 * KT], 1.0, n1, ALU.add, ALU.mult)
                stt(amod[:, KT:2 * KT], mod[:, 4 * KT:5 * KT], 1.0, n2, ALU.add, ALU.mult)
                dve.drain()

            lam0 = col("lam", 0, LN)[LBS, :]
            ts(lam[0][LBS, :], lam0, -1.0, None, ALU.mult)
            dve.drain()
            tt(lam[1][LBS, :], lam[0][LBS, :], lam0, ALU.max).then_inc(VR.sem, VR.one("lambda"))
            modulation(col("n1g2", 0, KT), col("n2g2", 0, KT))
            dve.wait_ge(AR.sem, AR.at("final norm"))
            tt(h_t, x_t, heads(rs[:, 0, :], KT), ALU.mult)
            dve.drain()
            for k in range(KT):
                ins = ts(x_t[:, k, :], h_t[:, k, :], col("final_g", k), None, ALU.mult)
            ins.then_inc(VR.sem, VR.one("x"))
            dve.wait_ge(AR.sem, AR.at("norm1"))
            modulated(x_t, amod[:, 0:KT], mod[:, 0:KT], rs[:, 0, :]).then_inc(VR.sem, VR.one("h1"))
            nc.vector.memset(xr[LBS, :, 0:3], 0.0)
            dve.wait_ge(AR.sem, AR.at("softplus"))
            stt(lam[2][LBS, :], lam[0][LBS, :], 0.0, lam[2][LBS, :], ALU.max, ALU.add)
            dve.drain()
            ts(lam[3][LBS, :], lam[2][LBS, :], 8.0, None, ALU.mult)
            ts(lam[4][LBS, :], lam[2][LBS, :], -8.0, None, ALU.mult)
            for i in range(8):
                dve.wait_ge(AR.sem, AR.at(f"xr{i}"))
                for n in (2 * i, 2 * i + 1):
                    ts(xc[LBS, n, :], xr[LBS, n, 3:T + 3], col("conv_w", 3 * LN + n)[LBS, :],
                       col("conv_b", n)[LBS, :], ALU.mult, ALU.add)
            for tap in (2, 1, 0):
                dve.drain()
                for n in range(LN):
                    ins = stt(xc[LBS, n, :], xr[LBS, n, tap:tap + T], col("conv_w", tap * LN + n)[LBS, :],
                              xc[LBS, n, :], ALU.mult, ALU.add)
            ins.then_inc(VR.sem, VR.one("conv"))
            for i in range(4):
                dve.wait_ge(AR.sem, AR.at(f"ri{4 * i + 3}"))
                g = slice(4 * i, 4 * i + 4)
                tt(ig[LBS, g, :], ig[LBS, g, :], xc[LBS, g, :], ALU.mult).then_inc(VR.sem, VR.one(f"ix{i}"))
            dve.wait_ge(AR.sem, AR.at("decay"))
            for i in range(4):
                part = slice(4 * i, 4 * i + 4)
                dve.drain()
                tt(oa[LBS, :, :], rg[LBS, part, :], rg[LBS, part, :], ALU.mult)
                dve.drain()
                ins = stt(xc[LBS, part, :], oa[LBS, :, :], 1.0, xc[LBS, part, :], ALU.add, ALU.mult)
            ins.then_inc(VR.sem, VR.one("u"))
            dve.wait_ge(AR.sem, AR.at("root"))
            tt(xc[LBS, :, :], xc[LBS, :, :], ig[LBS, :, :], ALU.mult)
            dve.drain()
            for n in range(LN):
                nc.vector.tensor_tensor_scan(ig[LBS, n, :], rg[LBS, n, :], xc[LBS, n, :], 0.0, ALU.mult, ALU.add)
            dve.drain()
            tt(gelu[LBS, :, :], gelu[LBS, :, :], ig[LBS, :, :], ALU.mult).then_inc(VR.sem, VR.one("y"))

            def into_x(V, Pj, bank, g1):
                for i in range(4):
                    dve.wait_ge(Pj.sem, Pj.at(f"out{i}"))
                    for k in (2 * i, 2 * i + 1):
                        ins = stt(x_t[:, k, :], bank[f"out{i}"][:, T * (k % 2):T * (k % 2) + T],
                                  g1[:, k:k + 1], x_t[:, k, :], ALU.mult, ALU.add)
                    ins.then_inc(V.sem, V.one(f"out{i}"))

            into_x(VR, PR, r_bank, mod[:, 2 * KT:3 * KT])
            dve.wait_ge(AR.sem, AR.at("norm2"))
            modulated(x_t, amod[:, KT:2 * KT], mod[:, 3 * KT:4 * KT], rs[:, 0, :]).then_inc(VR.sem, VR.one("h2"))
            dve.wait_ge(AR.sem, AR.at("h hi"))
            tt(h_lo, h_t, as_f32(h_hi), ALU.subtract).then_inc(VR.sem, VR.one("h lo"))

            def mlp_dve(layer):
                pe_steps, act_steps_, dve_steps_ = MLP[layer]
                dve.drain().then_inc(dve_steps_.sem, dve_steps_.first)
                with dve.Fori(0, MLP_TURNS // 2) as it:
                    for pair in range(2):
                        e = it * 2 + pair
                        slots = MLP_SLOTS[layer][2 * pair:2 * pair + 2]

                        def rest_of_part(j):
                            dve.wait_ge(act_steps_.sem, act_steps_.at(f"hi{j}", e))
                            tt(part_lo(j), mlp_raw(slots, j), as_f32(part_hi(j)), ALU.subtract)\
                                .then_inc(dve_steps_.sem, dve_steps_.one(f"lo{j}"))

                        for j in range(4):
                            rest_of_part(j)
                            if layer == 0 and j in (1, 3):
                                i = j // 2
                                dve.wait_ge(act_steps_.sem, act_steps_.at(f"mul{i}", e))
                                nc.vector.tensor_reduce(accs2[i], chunks2[i].rearrange("p k n -> p n k"), AX,
                                                        ALU.add)\
                                    .then_inc(dve_steps_.sem, dve_steps_.one(f"acc{i}"))
                        for m in range(4):
                            dve.wait_ge(act_steps_.sem, act_steps_.at(f"g{m}", e))
                            nc.vector.tensor_copy(he_hi[:, m, :], he[:, m, :])
                            dve.drain()
                            tt(he_lo[:, m, :], he[:, m, :], as_f32(he_hi[:, m, :]), ALU.subtract)\
                                .then_inc(dve_steps_.sem, dve_steps_.one(f"he{m}"))
                            rest_of_part(m + 4)
                        if layer == 0:
                            dve.wait_ge(pe_steps.sem, pe_steps.at("mods", e))
                            tt(modn[:, bass.ds(e * 6, 6)], banks[7][:, 0:6],
                               par[:, bass.ds(e * 6 + (COLS["ada_b"][0] + 3 * MODS), 6)], ALU.add)
                            tt(modn[:, bass.ds(e * 2 + MODS, 2)], banks[7][:, 6:8],
                               par[:, bass.ds(e * 2 + COLS["kv_ada_b"][0], 2)], ALU.add)\
                                .then_inc(dve_steps_.sem, dve_steps_.one("mods"))
                dve.wait_ge(pe_steps.sem, pe_steps.at("part7", MLP_TURNS - 1))
                for k in range(KT):
                    ins = stt(x_t[:, k, :], banks[k // 2][:, T * (k % 2):T * (k % 2) + T],
                              mod[:, 5 * KT + k:5 * KT + k + 1], x_t[:, k, :], ALU.mult, ALU.add)
                return ins

            mlp_dve(0)
            dve.drain()
            modulation(col("n1g2", KT, KT), col("n2g2", KT, KT))
            stt(akv, modn[:, MODS + KT:MODS + 2 * KT], 1.0, col("kvng2", 0, KT), ALU.add, ALU.mult)
            dve.drain().then_inc(VA.sem, VA.one("mods"))
            dve.wait_ge(AA.sem, AA.at("norm"))
            modulated(x_t, akv, modn[:, MODS:MODS + KT], rs[:, 0, :]).then_inc(VA.sem, VA.one("h"))
            tt(hq, x_t, heads(rs[:, 0, :], KT), ALU.mult)
            dve.drain()
            for k in range(KT):
                ins = ts(hq[:, k, :], hq[:, k, :], amod[:, k:k + 1], mod[:, k:k + 1], ALU.mult, ALU.add)
            ins.then_inc(VA.sem, VA.one("hq"))
            bias_a, bias_b = slot(A_SLOT[6], NH2, P), slot(A_SLOT[7], NH2, T)
            for u, ap in ((6, bias_a[0:64, :, 64:P]), (7, bias_b[0:64, :, T - 64:T])):
                dve.wait_ge(ring_full[A_SLOT[u]], 16 * (A_BASE[A_SLOT[u]] + 2))
                nc.vector.memset(ap, NEG)
            dve.drain().then_inc(VA.sem, VA.one("bias"))

            for rows, j in own:
                nc.vector.memset(q2_[rows, :, 1 - j, :], 0.0)
            dve.wait_ge(AA.sem, AA.at("kn3"))
            stt(k2_, k2_, col("kng"), krs2, ALU.mult, ALU.mult).then_inc(VA.sem, VA.one("k"))
            dve.wait_ge(AA.sem, AA.at("qn3"))
            for rows, j in own:
                ins = stt(q2_[rows, :, j, :], q2_[rows, :, j, :], col("qng")[rows, :], qrs2[rows, :, :],
                          ALU.mult, ALU.mult)
            ins.then_inc(VA.sem, VA.one("q"))
            for half, tag in enumerate(("A ", "B ")):
                def bias(g, nh, n):
                    h0 = 8 * half + (4 * g if g < 2 else 2 * (g - 2))
                    return (bias_a if g < 2 else bias_b)[:, h0:h0 + nh, :]
                attention_dve(nc, dve, lambda n: a_bank[n], PA, AA, VA, 0, tag, HD ** -0.5, bias, p2_, nmax, sums)
            into_x(VA, PA, a_bank, mod[:, 2 * KT:3 * KT])
            dve.wait_ge(AA.sem, AA.at("norm2"))
            modulated(x_t, amod[:, KT:2 * KT], mod[:, 3 * KT:4 * KT], rs[:, 0, :]).then_inc(VA.sem, VA.one("h2"))
            dve.wait_ge(AA.sem, AA.at("h hi"))
            tt(h_lo, h_t, as_f32(h_hi), ALU.subtract).then_inc(VA.sem, VA.one("h lo"))
            mlp_dve(1).then_inc(VA.sem, VA.one("x"))


def shape_constants():
    con = np.zeros((P, NCONST), np.float32)
    def put(name, v):
        con[:v.shape[0], CONST[name][0]:CONST[name][0] + v.shape[1]] = v

    put("ident", np.eye(P, dtype=np.float32))
    put("ones", np.ones((P, P), np.float32))
    put("heads", np.kron(np.eye(2, dtype=np.float32), np.ones((HD, HD), np.float32)))
    turn = np.zeros((P, DQK), np.float32)
    half = ROPE // 2
    for i in range(half):
        turn[NOPE + half + i, NOPE + i] = -1.0
        turn[NOPE + i, NOPE + half + i] = 1.0
    put("turn", turn)
    s, t = np.arange(P)[:, None], np.arange(P)[None, :]
    masks = [s == t] + [(s // (2 * n) == t // (2 * n)) & (s // n % 2 == 0) & (t // n % 2 == 1) for n in LEVELS]
    put("pair", np.concatenate([m.astype(np.float32) * np.float32(DK ** -0.5) for m in masks], 1))
    future = np.zeros((P, 2 * P), np.float32)
    future[:64, P + 64:] = NEG
    put("future", future)
    freq = (np.float32(10000.0) ** (-np.arange(half, dtype=np.float32) / np.float32(half))).astype(np.float32)
    put("freq", np.tile(freq, P // half)[:, None])
    return con


def columns(v):
    return v.reshape(-1, P).T


def kernel(**inputs):
    import concourse.bacc as bacc
    from concourse.bass_utils import run_bass_kernel_spmd

    a = {k: np.asarray(v) for k, v in inputs.items()}
    cols = np.zeros((P, NCOLS), np.float32)

    def put(name, v):
        cols[:v.shape[0], COLS[name][0]:COLS[name][0] + v.shape[1]] = v

    put("layer", np.concatenate([columns(a[n][l]) for l in range(2) for n in
                                 ("norm1_g", "hg_norm_g", "q_norm_g", "kv_norm_g", "norm2_g")], 1))
    put("lb", columns(a["hg_lb_logits"]))
    put("ada_b", np.concatenate([columns(a["ada_b"]), columns(a["ada_b_2"])], 1))
    put("kv_ada_b", columns(a["kv_ada_b_2"]))
    put("c", np.concatenate([columns(a["c"]), columns(a["c_2"])], 1))
    put("final_g", columns(a["final_g"]))
    put("n1g2", columns(a["norm1_g_2"]))
    put("n2g2", columns(a["norm2_g_2"]))
    put("kvng2", columns(a["kv_norm_g_2"]))
    put("kng", columns(np.tile(a["k_norm_g_2"], 2)))
    put("qng", columns(np.tile(a["q_norm_g_2"][0], 2)))
    put("conv_w", a["lru_conv_w_2"][0].reshape(4 * LN, LB).T)
    for name, v in (("conv_b", "lru_conv_b_2"), ("ba", "lru_gate_a_b_2"), ("bx", "lru_gate_x_b_2"), ("lam", "lru_lambda_2")):
        put(name, a[v][0].reshape(LN, LB).T)
    rb = a["rel_bias_2"][0]
    ext = np.concatenate([np.repeat(rb[:, 256:257], 127, 1), rb[:, ::-1], np.repeat(rb[:, 0:1], 128, 1)], 1)
    arrays = {
        "x": np.ascontiguousarray(a["x"][0].T.reshape(KT, P, T).transpose(1, 0, 2)),
        "positions": a["positions"],
        "cols": cols,
        "consts": shape_constants(),
        "ext": np.ascontiguousarray(ext),
        "ada": np.concatenate([a["ada_w"], a["ada_w_2"]], 0),
        "w_router": a["w_router"], "router_bias": a["router_bias"],
    }
    for n in ("w_in", "w_q_up", "w_kv_up", "w_br_a", "w_br_b", "w_out", "w_gate", "w_up", "w_down",
              "mlp_w1_2", "mlp_w2_2", "lru_w_in_2", "lru_gate_a_w_2", "lru_gate_x_w_2", "lru_w_out_2",
              "kv_ada_w_2", "kv_w_2", "attn_w_q_2", "attn_w_o_2"):
        arrays[n] = np.ascontiguousarray(a[n])
    nc = bacc.Bacc("TRN2", target_bir_lowering=False, num_devices=1)
    w = {n: nc.dram_tensor("in_" + n, v.shape, mybir.dt.from_np(v.dtype), kind="ExternalInput").ap()
         for n, v in arrays.items()}
    w["out"] = nc.dram_tensor("out", (P, KT, T), F32, kind="ExternalOutput").ap()
    program(nc, w["x"], w["positions"], w["cols"], w["consts"], w["ext"], w)
    r = run_bass_kernel_spmd(nc, [{"in_" + n: v for n, v in arrays.items()}], core_ids=[0])
    out = np.asarray(r.results[0]["out"])
    return out.transpose(2, 1, 0).reshape(1, T, D)
```

```python
from contextlib import ExitStack

import numpy as np

import concourse.bass as bass
from concourse import mybir

ALU = mybir.AluOpType
ACT = mybir.ActivationFunctionType
AX = mybir.AxisListType.X
F32 = mybir.dt.float32
F32R = mybir.dt.float32r
I32 = mybir.dt.int32

P = 128
D = 1024
T = 256
KT = D // P
TT = T // P
EPS = 1e-6
HH, DK = 4, 128
NH, NOPE, ROPE, VD = 8, 64, 32, 64
DQK = NOPE + ROPE
QL, KVL = 384, 256
NE, NG, DE = 16, 4, 512
EG = NE // NG
LW, LN = 1408, 16
LB = LW // LN
NH2, HD = 16, 64
FF = 4096
SLOTS, SLOT = 6, 4096
PARTS, PART = 4, 1024
MODS = 6 * KT
CH = 384
LEVELS = [1, 2, 4, 8, 16, 32, 64]
NEG = -1e30
TWO_PI = 2 * np.pi
C1 = 6.28125
C2 = float(np.float32(np.round((TWO_PI - C1) * 2**22) / 2**22))
C3 = float(TWO_PI - C1 - C2)
MAGIC = 12582912.0

COLS = {}


def _cols():
    at = 0
    for name, n in [("layer", 2 * 25), ("lb", 2 * HH), ("ada_b", 4 * MODS), ("kv_ada_b", 2 * KT),
                    ("c", 2 * KT), ("final_g", KT), ("n1g2", 2 * KT), ("n2g2", 2 * KT),
                    ("kvng2", KT), ("kng", 1), ("qng", 1), ("conv_w", 4 * LN), ("conv_b", LN),
                    ("ba", LN), ("bx", LN), ("lam", LN)]:
        COLS[name] = (at, n)
        at += n
    return at


NCOLS = _cols()
N1G, HGN, QNG, KVNG, N2G, LP = 0, 8, 12, 15, 17, 25

CONST = {}


def _const():
    at = 0
    for name, n in [("ident", P), ("ones", P), ("heads", P), ("turn", DQK), ("pair", 8 * P),
                    ("future", 2 * P), ("freq", 1)]:
        CONST[name] = (at, n)
        at += n
    return at


NCONST = _const()


UNITS = [("w_in", D, 512, 512), ("w_in", D, 0, 512), ("w_in", D, 1024, 512), ("w_in", D, 1536, 512),
         ("w_in", D, 2048, QL), ("w_in", D, 2432, KVL + ROPE)]
UNITS += [("w_in", D, 2720 + 512 * i, 512) for i in range(4)]
UNITS += [("w_q_up", QL, 0, NH * DQK), ("w_kv_up", KVL, 0, NH * (NOPE + VD)),
          ("w_br_a", HH * DK, 0, D), ("w_br_b", NH * VD, 0, D),
          ("w_out", D, 0, 512), ("w_out", D, 512, 512)]
LAST_USE = ["f1", "q1", "v1", "hgate1", "cq1", "kr", "gates1", "gates3", "gates5", "gates7",
            "q up3", "v up1", "ya3", "yb3", "out1", "out3"]
STATIC_IN = [len(range(s, len(UNITS), SLOTS)) for s in range(SLOTS)]
PER_LAYER = STATIC_IN
LAST_USE_OF_SLOT = [LAST_USE[s + SLOTS * (STATIC_IN[s] - 1)] for s in range(SLOTS)]


SQ2 = [f"sq2 {i}" for i in range(4)]
H2 = ["h2 0", "h2 1"]
SQ0 = [f"sq0 {i}" for i in range(4)]
SQ1 = [f"sq1 {i}" for i in range(4)]
X2 = [f"x2 {i}" for i in range(4)]


class Steps:

    def __init__(self, sem, names):
        assert len(set(names)) == len(names)
        self.sem, self.names, self.n, self.given = sem, names, len(names), 0

    def one(self, name):
        assert self.names[self.given] == name, (self.names[self.given], name)
        self.given += 1
        return 1

    def at(self, name, turn=0):
        return turn * self.n + self.names.index(name) + 1


class Turns(Steps):

    def __init__(self, sem, names, first):
        super().__init__(sem, names)
        self.first = first

    def one(self, name):
        assert self.names[self.given % self.n] == name, (self.names[self.given % self.n], name)
        self.given += 1
        return 1

    def at(self, name, turn=0):
        return turn * self.n + (self.first + self.names.index(name) + 1)


FILL = ["hgate0", "hgate1", "cq0", "cq1", "ckv", "kr", "gates0", "gates1", "gates2",
        "gates3", "gates4", "gates5", "gates6", "gates7"]
MASKED = ["diag"] + [f"L{n}" for n in LEVELS]


def pe_jobs():
    jobs = [(n, "act") for n in ("f0", "f1", "q0", "q1", "v0", "v1")]
    fill = list(FILL)
    for name in MASKED:
        jobs += [(f"{name} t0", "dve"), (f"{name} t1", "dve"), (fill.pop(0), "act")]
    jobs += [("cross", "act")] + [(fill.pop(0), "act") for _ in range(2)]
    jobs += [("o0", "act"), ("o1", "act")]
    jobs += [(n, "act") for n in fill[:2]]
    jobs += [("cq norm", "act"), ("ckv norm", "act"), ("o norm0", "act"), ("o norm1", "act")]
    jobs += [(n, "act") for n in fill[2:]]
    jobs += [(f"q up{i}", "act") for i in range(4)] + [(f"k up{i}", "act") for i in range(4)]
    jobs += [(f"v up{i}", "act") for i in range(2)]
    jobs += [(f"q turn{i}", "dve") for i in range(4)] + [("k turn", "dve")]
    jobs += [(n, "dve") for n in ["ya0", "ya1"] + six("s") + ["ya2", "ya3"]] + value_jobs()
    jobs += [(f"yb{i}", "dve") for i in range(4)]
    jobs += [(f"out{i}", "dve") for i in range(4)]
    jobs += [("norm2", "act"), ("router", "act"), ("combine", "dve")]
    return jobs


def group(g):
    return (0, 4, P, 4 * g) if g < 2 else (1, 2, T, 2 * (g - 2))


def scores_pe(pe, job, PE, tag, q, k):
    for g in range(6):
        t, nh, n, h0 = group(g)
        b = job(f"{tag}s{g}")
        for j in range(nh):
            ins = pe.matmul(b[:, n * j:n * j + n], q(h0 + j, t), k(h0 + j, n), start=True, stop=True)
        ins.then_inc(PE.sem, PE.one(f"{tag}s{g}"))


def values_pe(pe, job, PE, AC, DV, l, tag, v, p, pT, ident):
    for g in range(6):
        pe.wait_ge(DV.sem, DV.at(f"{tag}p{g}", l))
        b = job(f"{tag}pT{g}")
        for j in range(4):
            c = 512 * g + P * j
            ins = pe.transpose(b[:, P * j:P * j + P], p[:, c:c + P], ident)
        ins.then_inc(PE.sem, PE.one(f"{tag}pT{g}"))
    for g in range(4):
        pe.wait_ge(AC.sem, AC.at(f"{tag}pT{2 + g}", l))
        b = job(f"{tag}ov{g}")
        for h in (2 * g, 2 * g + 1):
            o = b[0:VD, T * (h % 2):T * (h % 2) + T]
            w = lambda i: pT[:, P * i:P * i + P]
            pe.matmul(o[:, 0:P], v(h, 0), w(h), start=True, stop=True)
            pe.matmul(o[:, P:T], v(h, 0), w(8 + 2 * h), start=True, stop=False)
            ins = pe.matmul(o[:, P:T], v(h, 1), w(9 + 2 * h), start=False, stop=True)
        ins.then_inc(PE.sem, PE.one(f"{tag}ov{g}"))


def exp_act(nc, act, AC, DV, l, tag, g, p, nmax, sums):
    _, nh, n, _ = group(g)
    act.wait_ge(DV.sem, DV.at(f"{tag}s{g}", l))
    for j in range(nh):
        s = p[:, 512 * g + n * j:512 * g + n * j + n]
        ins = nc.scalar.activation(s, s, ACT.Exp, bias=nmax[:, 4 * g + j:4 * g + j + 1],
                                   accum_out=sums[:, 4 * g + j:4 * g + j + 1])
    ins.then_inc(AC.sem, AC.one(f"{tag}e{g}"))


def transposed_act(nc, act, bank, PE, AC, l, tag, g, pT):
    act.wait_ge(PE.sem, PE.at(f"{tag}pT{g}", l))
    nc.scalar.activation(pT[:, 512 * g:512 * g + 512], bank(f"{tag}pT{g}")[:, :], ACT.Copy)\
        .then_inc(AC.sem, AC.one(f"{tag}pT{g}"))


def outputs_act(nc, act, bank, PE, AC, l, tag, o):
    for g in range(4):
        act.wait_ge(PE.sem, PE.at(f"{tag}ov{g}", l))
        for j in range(2):
            ins = nc.scalar.activation(o[VD * j:VD * j + VD, g, :],
                                       bank(f"{tag}ov{g}")[0:VD, T * j:T * j + T], ACT.Copy)
        ins.then_inc(AC.sem, AC.one(f"{tag}ov{g}"))


def scores_dve(nc, dve, bank, PE, DV, l, tag, g, scale, bias, p, nmax):
    _, nh, n, h0 = group(g)
    s = p[:, 512 * g:512 * g + 512].rearrange("p (h n) -> p h n", h=nh)
    dve.wait_ge(PE.sem, PE.at(f"{tag}s{g}", l))
    nc.vector.scalar_tensor_tensor(s, bank(f"{tag}s{g}")[:, :].rearrange("p (h n) -> p h n", h=nh),
                                   scale, bias(h0, nh, n), ALU.mult, ALU.add)
    dve.drain()
    nc.vector.tensor_reduce(nmax[:, 4 * g:4 * g + nh], s, AX, ALU.max, negate=True)\
        .then_inc(DV.sem, DV.one(f"{tag}s{g}"))


def normed_dve(nc, dve, AC, DV, l, tag, g, p, sums):
    _, nh, n, _ = group(g)
    dve.wait_ge(AC.sem, AC.at(f"{tag}e{g}", l))
    r = sums[:, 4 * g:4 * g + nh]
    nc.vector.reciprocal(r, r)
    dve.drain()
    for j in range(nh):
        s = p[:, 512 * g + n * j:512 * g + n * j + n]
        ins = nc.vector.tensor_scalar(s, s, r[:, j:j + 1], None, ALU.mult)
    ins.then_inc(DV.sem, DV.one(f"{tag}p{g}"))


def both(*lists):
    return [x for items in zip(*lists) for x in items]


def six(name):
    return [f"{name}{g}" for g in range(6)]


def four(name):
    return [f"{name}{g}" for g in range(4)]


def value_jobs(tag=""):
    return [(n, "act") for n in six(f"{tag}pT") + four(f"{tag}ov")]


def act_steps():
    s = ["f0", "f1", "q0", "q1", "v0", "v1"]
    fill = list(FILL)
    s += [fill.pop(0) for _ in MASKED] + ["cross", fill.pop(0), fill.pop(0), "o0", "o1", "o sq", "c sq"]
    s += fill[:2] + ["cq norm", "ckv norm", "o norm0", "o norm1", "c rs", "o rs"] + fill[2:]
    s += [f"q up{i}" for i in range(4)] + [f"k up{i}" for i in range(4)] + ["v up0", "v up1"]
    s += six("e") + six("pT") + four("ov") + SQ2 + ["norm2", "h hi0", "h hi1", "router"] + SQ0 + ["next norm"]
    return s


def dve_steps():
    s = ["h1 0", "h1 1", "fk"]
    s += ["qk L1", "diag t0", "diag t1"]
    for i, n in enumerate(LEVELS):
        s += [f"qk L{2 * n}", f"L{n} t0", f"L{n} t1"]
    s += ["cn", "oa"]
    s += [f"q turn{i}" for i in range(4)] + ["k turn"]
    s += six("s") + both(four("ya"), six("p")[:4]) + six("p")[4:] + four("yb")
    s += [f"out{i}" for i in range(4)] + ["h2 0", "h2 1", "h lo0", "h lo1", "comb", "combine"] + X2
    return s


MOE_PE = ["pick"] + [f"part{j}" for j in range(8)] + ["mods"] + [f"part{j}" for j in range(8, 12)]
MOE_ACT = (["hi0", "hi1", "hi2", "hi3", "hi4", "acc hi", "sg0", "hi5", "hi6", "sg1", "hi7", "hi8", "sg2", "hi9",
            "hi10", "sg3", "hi11"])
MOE_DVE = ["lo0", "lo1", "lo2", "acc", "lo3", "lo4", "he0", "lo5", "acc lo", "lo6", "he1", "lo7", "lo8", "he2", "lo9",
           "lo10", "he3", "next", "mods", "lo11"]

R_JOBS = ([("norm1", "act")] + [(f"xr{i}", "act") for i in range(8)]
          + [(f"gelu{i}", "act") for i in range(4)] + [(f"ri{n}", "act") for n in range(LN)]
          + [(f"gelu{i}", "act") for i in range(4, 8)]
          + [(f"out{i}", "dve") for i in range(4)] + [("norm2", "act")])
R_ACT = (SQ1 + ["norm1", "softplus"] + [f"xr{i}" for i in range(8)]
         + [f"gelu{i}" for i in range(4)] + [f"ri{n}" for n in range(LN)]
         + ["tanh", "decay"] + [f"gelu{i}" for i in range(4, 8)] + ["root0", "root1", "root2", "root3"] + SQ2 + ["norm2", "h hi0", "h hi1"])
R_DVE = ["lambda", "x0", "x1", "x2", "x3", "h1 0", "h1 1", "conv", "ix0", "ix1", "ix2", "ix3", "u0", "u1", "u2", "u3", "y0", "y1", "y2", "y3"] + [f"out{i}" for i in range(4)] + H2 + ["h lo0", "h lo1"]
R_UNITS = [("lru_w_in_2", P, KT, 0, LW + 352 * i, 352) for i in range(4)]
R_UNITS += [("lru_w_in_2", P, KT, 0, 352 * i, 352) for i in range(4)]
R_UNITS += [("lru_gates", LB, 2, 0, 0, LN * LB)]
R_UNITS += [("lru_w_out_2", LB, 4, 4 * LB * i, 0, D) for i in range(4)]
R_LAST = ["xr1", "xr3", "xr5", "xr7", "gelu1", "gelu3", "gelu5", "gelu7", f"ri{LN - 1}", "out3", "out3", "out3", "out3"]
A_JOBS = ([("norm", "act")] + [(n, "act") for n in four("k") + ["q0", "q1"] + four("kn") + ["q2", "q3"]
                               + ["v0", "v1"] + four("qn") + ["v2", "v3"]] + [(n, "dve") for n in six("A s") + six("B s")]
          + value_jobs("A ") + value_jobs("B ")
          + [(f"out{i}", "dve") for i in range(4)] + [("norm2", "act")])
A_ACT = (SQ0 + ["norm"] + four("k") + ["k sq", "q0", "q1"] + four("kn") + ["kn rs", "q2", "q3", "q sq"]
         + ["v0", "v1"] + four("qn") + ["qn rs", "v2", "v3"]
         + six("A e") + both(six("A pT"), six("B e"))
         + four("A ov") + six("B pT") + four("B ov") + SQ2 + ["norm2", "h hi0", "h hi1"])
A_DVE = (X2 + ["h 0", "h 1", "hq", "bias", "k", "q"] + six("A s") + both(six("A p"), six("B s")) + six("B p")
         + [f"out{i}" for i in range(4)] + H2 + ["h lo0", "h lo1", "x"])
A_UNITS = [("kv_w_2", P, KT, 0, 512 * i, 512) for i in range(4)]
A_UNITS += [("attn_w_q_2", P, KT, 0, 512 * i, 512) for i in range(2)]
A_UNITS += [("bias a",), ("bias b",)]
A_UNITS += [("attn_w_o_2", P, KT, 0, 512 * i, 512) for i in range(2)]
A_SLOT = [0, 1, 2, 3, 4, 5, 0, 1, 4, 5]
A_LAST = ["k1", "k3", "v1", "v3", "q1", "q3", None, None, "out1", "out3"]
MLP_TURNS = FF // 512
MLP_BANK = [4, 5, 6, 4]
MLP_SLOTS = [[0, 1, 2, 3], [2, 3, 0, 1]]
MLP_PARTS = [f"part{j}" for j in range(8)]
MLP_SPLIT = [f"hi{j}" for j in range(4)], [f"lo{j}" for j in range(4)]
MLP_STEPS = [(MLP_PARTS[:6] + ["mods"] + MLP_PARTS[6:],
              ["hi0", "mul0", "hi1", "hi2", "mul1", "hi3"] + [x for j in range(4) for x in (f"g{j}", f"hi{j + 4}")],
              ["lo0", "lo1", "acc0", "lo2", "lo3", "acc1"]
              + [x for j in range(4) for x in (f"he{j}", f"lo{j + 4}")] + ["mods"]),
             (MLP_PARTS, MLP_SPLIT[0] + [x for j in range(4) for x in (f"g{j}", f"hi{j + 4}")],
              MLP_SPLIT[1] + [x for j in range(4) for x in (f"he{j}", f"lo{j + 4}")])]
MLP_CHUNKS = [CH, CH, 2 * D // MLP_TURNS]


def program(nc, xT, positions, cols, consts, ext, w):
    pe1, act1, dve1 = pe_jobs(), act_steps(), dve_steps()
    with ExitStack() as ctx:
        sem = lambda name: ctx.enter_context(nc.semaphore(name))

        def next_offset():
            return (nc.sbuf_base + 31) // 32 * 32

        ring_at = next_offset()
        ring = ctx.enter_context(nc.sbuf_tensor("ring", [P, SLOTS * SLOT], F32))
        def sb(name, *shape, dt=F32, parts=P):
            n = int(np.prod(shape))
            t = ctx.enter_context(nc.sbuf_tensor(name, [parts, n], dt))
            return t

        def view(t, off, *shape):
            n = int(np.prod(shape))
            ap = t[:, off:off + n]
            if len(shape) == 2:
                return ap.rearrange("p (a b) -> p a b", a=shape[0])
            if len(shape) == 3:
                return ap.rearrange("p (a b c) -> p a b c", a=shape[0], b=shape[1])
            return ap

        x_t = view(sb("x_t", KT * T), 0, KT, T)
        h_t = view(sb("h_t", KT * T), 0, KT, T)
        par = sb("par", NCOLS)
        con = sb("con", NCONST)
        posi = sb("posi", T, dt=I32)
        trig = sb("trig", 2 * T)
        lp = sb("lp", LP)
        modn = sb("modn", MODS + 2 * KT)
        mod = sb("mod", MODS)
        amod = sb("amod", 2 * KT)
        lbs = sb("lbs", 4 * HH)
        cact = sb("cact", 2 * KT)
        rs = view(sb("rs", 2 * T), 0, 2, T)
        small = sb("small", 640)
        epsb = sb("epsb", 2)
        order = sb("order", NE)[:, :]
        acc_split = ctx.enter_context(nc.sbuf_tensor("acc_split", [P, 2 * CH], F32R))
        one_r = ctx.enter_context(nc.sbuf_tensor("one_r", [P, 2], F32R))
        zeros = ctx.enter_context(nc.sbuf_tensor("zeros", [P, 512], mybir.dt.bfloat16))
        lbl = sb("lbl", 2 * HH)
        wr_sb = sb("w_router", KT * NE)
        oa = view(sb("oa", HH * T), 0, HH, T)
        cqkv = sb("cqkv", 5 * T)
        krs = sb("krs", T)
        mix_at = next_offset()
        mix = sb("mix", 11264 + 16 * T + 4 * T)
        split_w = nc.alloc_sbuf_tensor_at("split_w", [P, 2 * PARTS * PART], F32R, offset=ring_at + 4 * SLOT * 4)
        split_x = nc.alloc_sbuf_tensor_at("split_x", [P, 2 * (KT + 4) * T], F32R,
                                          offset=mix_at + 4 * (11264 + 20 * T - 2 * (KT + 4) * T))

        def col(name, i=0, n=1):
            a = COLS[name][0] + i
            return par[:, a:a + n]

        def const(name):
            a, n = CONST[name]
            return con[:, a:a + n]

        ident, ones, heads_ones = const("ident"), const("ones"), const("heads")
        cos, sin = trig[:, 0:T], trig[:, T:2 * T]

        def slot(u, *shape, parts=P):
            ap = ring[0:parts, (u % SLOTS) * SLOT:(u % SLOTS) * SLOT + int(np.prod(shape))]
            return ap.rearrange("p (a b) -> p a b", a=shape[0])

        banks = [ctx.enter_context(nc.psum_tensor(f"bank{i}", [P, 512], F32)) for i in range(8)]

        qf = view(mix, 0, HH, T)
        kf = view(mix, 1024, HH, T)
        fwd = view(mix, 2048, HH, T)
        bwd = view(mix, 3072, HH, T)
        qd = [view(mix, 4096 + 1024 * i, HH, T) for i in range(2)]
        kd = [view(mix, 6144 + 1024 * i, HH, T) for i in range(2)]
        vt = view(mix, 8192, TT, HH * DK)
        pairs = [view(mix, 9216 + 512 * i, HH, P) for i in range(2)]
        cross = view(mix, 10240, HH, P)
        tmp = view(mix, 10752, HH, P)
        osq = view(mix, 1024, HH, T)
        oraw = view(mix, 0, HH, T)
        ors = view(mix, 2048, HH, T)
        gates = view(mix, 11264, 16, T)
        hgate = view(mix, 11264 + 16 * T, HH, T)
        cq, ckv = view(cqkv, 0, 3, T), view(cqkv, 3 * T, 2, T)
        csq = view(mix, 3072, 5, T)
        q_a = view(mix, 0, NH, T)
        k_a = view(mix, 2048, NH, T)
        v_a = view(mix, 4096, TT, NH * VD)
        p_a = view(mix, 5120, 3072)
        pT_a = view(mix, 8192, 3072)
        ob = view(cqkv, 0, 4, T)
        he = oa
        sg = view(mix, 0, 4, T)
        tg = view(mix, 1024, 4, T)
        chunk = mix[:, 2048:2048 + KT * CH]
        accs = mix[:, 5120:5120 + CH]
        combt = mix[0:NE, 5632:5632 + T]
        pick = mix[0:NE, 5888:5888 + T]
        h_hi, h_lo = view(split_x, 0, KT, T), view(split_x, KT * T, KT, T)
        he_hi, he_lo = view(split_x, 2 * KT * T, 4, T), view(split_x, (2 * KT + 4) * T, 4, T)

        xsq = view(mix, 0, KT, T)

        def part_hi(j):
            return view(split_w, 2 * PART * (j % PARTS), KT, P)

        def part_lo(j):
            return view(split_w, 2 * PART * (j % PARTS) + PART, KT, P)

        def moe_raw(j):
            if j < 8:
                return slot(j % 2, KT, DE)[:, :, P * (j // 2):P * (j // 2) + P]
            return slot(2, 4, D)[:, j - 8, :].rearrange("p (o n) -> p o n", n=P)

        def mlp_raw(slots, j):
            if j < 4:
                return slot(slots[0], KT, 512)[:, :, P * j:P * j + P]
            return slot(slots[1], 4, D)[:, j - 4, :].rearrange("p (o n) -> p o n", n=P)
        ones16 = ones[0:NE, :]
        tmps = [tmp, oa[:, 0:2, :].rearrange("p a (b c) -> p (a b) c", c=P)]
        wr = view(wr_sb, 0, KT, NE)
        rbias = sb("router_bias", NE)[:, :]
        scores, biased = small[:, 0:32], small[:, 32:64]
        combw = small[:, 64:96]
        sm = small[:, 96:640]
        nmax = [small[:, 96:120], small[:, 256:280]]
        sums = [small[:, 120:144], small[:, 280:304]]

        def as_f32(ap):
            return ap.bitcast(F32)

        loaded = sem("inputs_loaded")
        x_loaded = sem("x_loaded")
        ring_full = [sem(f"ring_full{i}") for i in range(SLOTS)]
        chunk_full = sem("chunk_full")
        gu_full = [sem(f"expert_gate_up_half{i}_full") for i in range(2)]
        down_full = sem("expert_down_full")
        gate_half = sem("lru_gate_a_loaded")
        P0 = Steps(sem("prologue_pe"), ["norm", "mods"])
        A0 = Steps(sem("prologue_act"), ["c"] + [f"mul{u}" for u in range(6)] + ["sq", "trig", "lb"]
                   + [f"mul{u}" for u in range(6, 12)])
        V0 = Steps(sem("prologue_dve"), ["zeros", "angles", "lb"] + [f"sum{u}" for u in range(12)] + ["mods"])
        unit_sums = [mix[:, 4096 + 512 * u:4608 + 512 * u] for u in range(12)]
        PE = Steps(sem("pe_done"), [n for n, _ in pe1] + ["next norm"])
        AC = Turns(sem("act_done"), act1, 1)
        DV = Steps(sem("dve_done"), dve1)
        MP = Turns(sem("moe_pe_done"), MOE_PE, len(MOE_PE))
        MA = Turns(sem("moe_act_done"), MOE_ACT, 0)
        MV = Turns(sem("moe_dve_done"), MOE_DVE, len(MOE_DVE))
        bank_of = {n: banks[i % 8] for i, (n, _) in enumerate(pe1)}
        before = {n: pe1[i - 8] for i, (n, _) in enumerate(pe1) if i >= 8}
        LBS = slice(0, LB)
        xc = view(mix, 0, LN, T)
        gelu = view(mix, 4096, LN, T)
        rg = view(mix, 8192, LN, T)
        ig = view(mix, 12288, LN, T)
        xr = view(mix, 12240, LN, T + 3)
        lam = [small[:, 144 + 16 * i:160 + 16 * i] for i in range(5)]
        q2_ = view(mix, 0, KT, 2, T)
        own = [(slice(HD * i, HD * i + HD), i) for i in range(2)]
        k2_ = view(mix, 4096, KT, T)
        v2_ = view(mix, 6144, TT, D)
        p2_, pT2 = [view(mix, 8192, 3072), ring[:, 3 * SLOT:3 * SLOT + 3072]], view(mix, 11264, 3072)
        o2_ = view(mix, 14336, KT, T)
        hq = view(mix, 14336, KT, T)
        ksq = view(mix, 11264, KT, T)
        krs2, qrs2 = view(mix, 8192, KT, T), view(mix, 11264, KT, T)
        akv = small[:, 240:240 + KT]
        chunks2 = [mix[:, 1024 + 3072 * i:1024 + 3072 * i + KT * n].rearrange("p (k n) -> p k n", k=KT)
                   for i, n in enumerate(MLP_CHUNKS)]
        accs2 = [mix[:, 9216 + CH * i:9216 + CH * i + n] for i, n in enumerate(MLP_CHUNKS)]
        chunk2_full = [sem(f"mlp_chunk_full{i}") for i in range(3)]
        PR, AR, VR = Steps(sem("lru_pe_done"), [n for n, _ in R_JOBS]), Steps(sem("lru_act_done"), R_ACT), Steps(sem("lru_dve_done"), R_DVE)
        PA, AA, VA = Steps(sem("attn_pe_done"), [n for n, _ in A_JOBS]), Steps(sem("attn_act_done"), A_ACT), Steps(sem("attn_dve_done"), A_DVE)
        MLP = [(Turns(sem(f"mlp{i}_pe_done"), p, 2 * len(p)), Turns(sem(f"mlp{i}_act_done"), a, 2 * len(a)),
                Turns(sem(f"mlp{i}_dve_done"), v, 2 * len(v))) for i, (p, a, v) in enumerate(MLP_STEPS)]
        kv_summed = sem("kv_chunk_summed")
        stored = sem("output_stored")
        rows_stored = sem("bias_rows_stored")
        rows = nc.dram_tensor("bias_rows", (NH2, P, 512), F32, kind="Internal").ap()
        R_BASE = [2 + 2 * PER_LAYER[i] for i in range(SLOTS)]
        M0_BASE = [R_BASE[i] + len(range(i, len(R_UNITS), SLOTS)) for i in range(SLOTS)]
        A_BASE = [M0_BASE[i] + (MLP_TURNS // 2 if i in MLP_SLOTS[0] else 0) for i in range(SLOTS)]
        M1_BASE = [A_BASE[i] + A_SLOT.count(i) for i in range(SLOTS)]

        def banks_of(jobs):
            at = {n: banks[i % 8] for i, (n, _) in enumerate(jobs)}
            old = {n: jobs[i - 8] for i, (n, _) in enumerate(jobs) if i >= 8}
            return at, old

        r_bank, r_old = banks_of(R_JOBS)
        a_bank, a_old = banks_of(A_JOBS)

        def heads(ap, n):
            return ap.unsqueeze(1).broadcast_to([ap.shape[0], n, ap.shape[1]])

        block = ctx.enter_context(nc.Block())

        @block.sync
        def _(sp):
            sp.dma_start(par[:, :], cols).then_inc(loaded, 16)
            sp.dma_start(con[:, :], consts).then_inc(loaded, 16)
            sp.dma_start(wr, w["w_router"].rearrange("(k p) n -> p k n", p=P)).then_inc(loaded, 16)
            sp.dma_start(rbias, w["router_bias"].rearrange("(a n) -> a n", a=1).to_broadcast([P, NE]))\
                .then_inc(loaded, 16)
            sp.dma_start(posi[:, :], positions.to_broadcast([P, T])).then_inc(loaded, 16)
            ada = w["ada"]
            for u in range(12):
                if u >= SLOTS:
                    sp.wait_ge(V0.sem, V0.at(f"sum{u - SLOTS}"))
                sp.dma_start(slot(u, KT, 512), ada[0, :, 512 * u:512 * u + 512].rearrange(
                    "(k p) n -> p k n", p=P)).then_inc(ring_full[u % SLOTS], 16)
                if u == 1:
                    sp.dma_start(x_t, xT).then_inc(x_loaded, 16)
            with sp.Fori(0, 2) as l:
                for u, (name, height, c0, n) in enumerate(UNITS):
                    if u < SLOTS:
                        sp.wait_ge(V0.sem, V0.at(f"sum{SLOTS + u}"))
                        if u == 0:
                            sp.wait_ge(MV.sem, MV.at("lo7", l * NE - 1))
                        elif u == 2:
                            sp.wait_ge(MV.sem, MV.at("lo11", l * NE - 1))
                        elif u == 4:
                            sp.wait_ge(MP.sem, MP.at("part11", l * NE - 1))
                    else:
                        sp.wait_ge(PE.sem, PE.at(LAST_USE[u - SLOTS], l))
                    src = w[name][bass.ds(l, 1), :, c0:c0 + n].rearrange(
                        "a (k p) n -> p (a k) n", p=P)
                    sp.dma_start(slot(u, height // P, n), src).then_inc(ring_full[u % SLOTS], 16)

                def expert(e, waits):
                    waits("chunk", None)
                    src = w["ada"][bass.ds(l + 1, 1), :, bass.ds(e * CH, CH)].rearrange(
                        "a (k p) n -> p (a k) n", p=P)
                    sp.dma_start(chunk.rearrange("p (k n) -> p k n", k=KT), src).then_inc(chunk_full, 16)
                    for half in range(2):
                        for s, name in enumerate(("w_gate", "w_up")):
                            waits(f"gate up {half}", s)
                            src = w[name][bass.ds(l, 1), bass.ds(e, 1), :, 256 * half:256 * half + 256]
                            sp.dma_start(slot(s, KT, DE)[:, :, 256 * half:256 * half + 256],
                                         src.rearrange("a b (k p) n -> p (a b k) n", p=P))\
                                .then_inc(gu_full[half], 16)
                    waits("down", 2)
                    sp.dma_start(slot(2, 4, D), w["w_down"][bass.ds(l, 1), bass.ds(e, 1)].rearrange(
                        "a b (k p) n -> p (a b k) n", p=P)).then_inc(down_full, 16)

                def statics_used(what, s):
                    if what == "gate up 0" or what == "down":
                        sp.wait_ge(PE.sem, PE.at(LAST_USE_OF_SLOT[s], l))
                    elif what == "chunk":
                        sp.wait_ge(DV.sem, DV.at("yb3", l))

                expert(0, statics_used)
                with sp.Fori(1, NE) as e:
                    def used(what, s):
                        if s != 1:
                            k = {"gate up 0": "lo3", "gate up 1": "lo7", "down": "lo11", "chunk": "acc"}[what]
                            sp.wait_ge(MV.sem, MV.at(k, l * NE + (e - 1)))
                    expert(e, used)

            for u, (name, height, nk, r0, c0, n) in enumerate(R_UNITS):
                s = u % SLOTS
                if u < SLOTS:
                    if s < 4:
                        sp.wait_ge(MV.sem, MV.at("lo7" if s < 2 else "lo11", 2 * NE - 1))
                    else:
                        sp.wait_ge(MP.sem, MP.at("part11", 2 * NE - 1))
                else:
                    sp.wait_ge(PR.sem, PR.at(R_LAST[u - SLOTS]))
                if name == "lru_gates":
                    for i, part in enumerate(("lru_gate_a_w_2", "lru_gate_x_w_2")):
                        sp.dma_start(slot(u, 2 * LN, LB, parts=LB)[:, LN * i:LN * i + LN, :],
                                     w[part][0].rearrange("n d e -> d n e")).then_inc(
                                         ring_full[s] if i else gate_half, 16)
                else:
                    sp.dma_start(slot(u, nk, n, parts=height),
                                 w[name][0][r0:r0 + height * nk, c0:c0 + n].rearrange(
                                     "(k p) n -> p k n", p=height)).then_inc(ring_full[s], 16)

            def mlp_units(layer, j, pair, waits):
                s1, s2 = MLP_SLOTS[layer][2 * pair:2 * pair + 2]
                waits(0)
                sp.dma_start(slot(s1, KT, 512), w["mlp_w1_2"][layer, :, bass.ds(j * 512, 512)].rearrange(
                    "(k p) n -> p k n", p=P)).then_inc(ring_full[s1], 16)
                waits(1)
                sp.dma_start(slot(s2, 4, D), w["mlp_w2_2"][layer, bass.ds(j * 512, 512), :].rearrange(
                    "(k p) n -> p k n", p=P)).then_inc(ring_full[s2], 16)

            def mlp_chunks(j, waits):
                for i, n in enumerate(MLP_CHUNKS):
                    waits(i)
                    src = w["ada"][3, :, bass.ds(j * (2 * CH) + CH * i, CH)] if i < 2 else \
                        w["kv_ada_w_2"][:, bass.ds(j * n, n)]
                    sp.dma_start(chunks2[i], src.rearrange("(k p) n -> p k n", p=P))\
                        .then_inc(chunk2_full[i], 16)

            def mlp_sync(layer, first_waits):
                dve_steps_ = MLP[layer][2]
                for j in range(2):
                    mlp_units(layer, j, j, lambda i: first_waits(2 * j + i))
                    if layer == 0:
                        if j == 0:
                            sp.wait_ge(VR.sem, VR.at("h2 1"))
                            mlp_chunks(j, lambda i: None)
                        else:
                            mlp_chunks(j, lambda i: sp.wait_ge(dve_steps_.sem, dve_steps_.at(f"acc{i}", 0)) if i < 2
                                       else sp.wait_ge(kv_summed, 1))
                with sp.Fori(1, MLP_TURNS // 2) as it:
                    for j in range(2):
                        mlp_units(layer, it * 2 + j, j, lambda i: sp.wait_ge(
                            dve_steps_.sem, dve_steps_.at("lo7" if i else "lo3", it * 2 + (j - 2))))
                        if layer == 0:
                            mlp_chunks(it * 2 + j, lambda i: sp.wait_ge(
                                dve_steps_.sem, dve_steps_.at(f"acc{i}", it * 2 + (j - 1))) if i < 2
                                       else sp.wait_ge(kv_summed, it * 2 + j))

            sp.dma_start(rows, ext.unsqueeze(1).broadcast_to([NH2, P, 512])).then_inc(rows_stored, 16)
            r_last = [R_LAST[max(range(i, len(R_UNITS), SLOTS))] for i in range(SLOTS)]
            mlp_sync(0, lambda i: sp.wait_ge(PR.sem, PR.at(r_last[MLP_SLOTS[0][i]])))
            for u, unit in enumerate(A_UNITS):
                s = A_SLOT[u]
                if u >= SLOTS:
                    sp.wait_ge(PA.sem, PA.at(A_LAST[A_SLOT.index(s)]))
                elif s in MLP_SLOTS[0]:
                    sp.wait_ge(MLP[0][2].sem, MLP[0][2].at("lo7" if s % 2 else "lo3", MLP_TURNS - 2 + s // 2))
                elif s == 4:
                    sp.wait_ge(MLP[0][0].sem, MLP[0][0].at("part7", MLP_TURNS - 1))
                if len(unit) == 1:
                    n, off = (P, 255) if unit[0] == "bias a" else (T, 127)
                    if unit[0] == "bias a":
                        sp.wait_ge(rows_stored, 16)
                    src = bass.AP(rows.tensor, off, [[511, P], [P * 512, NH2], [1, n]])
                    sp.dma_start(slot(s, NH2, n), src).then_inc(ring_full[s], 16)
                else:
                    name, _, nk, _, c0, n = unit
                    m = w[name] if name == "kv_w_2" else w[name][0]
                    sp.dma_start(slot(s, nk, n), m[:, c0:c0 + n].rearrange("(k p) n -> p k n", p=P))\
                        .then_inc(ring_full[s], 16)

            def before_mlp1(i):
                s = MLP_SLOTS[1][i]
                if s in (0, 1):
                    sp.wait_ge(VA.sem, VA.at("B s1" if s == 0 else "B s5"))
                elif s == 3:
                    sp.wait_ge(PA.sem, PA.at("B pT5"))
                else:
                    sp.wait_ge(PA.sem, PA.at(A_LAST[s]))
            mlp_sync(1, before_mlp1)
            sp.wait_ge(VA.sem, VA.at("x"))
            sp.dma_start(w["out"], x_t).then_inc(stored, 16)
            sp.wait_ge(stored, 16)

        def clear_sums(pe):
            for i in range(4):
                pe.matmul(banks[i][:, :], zeros[:, 0:P], zeros[:, :], start=True, stop=True,
                          skip_group_check=True)

        def split_products(pe, out, hi, lo, x_hi, x_lo, start=False, stop=False, **kw):
            pe.matmul(out, hi, x_hi, start=start, stop=False, **kw)
            pe.matmul(out, hi, x_lo, start=False, stop=False, **kw)
            return pe.matmul(out, lo, x_hi, start=False, stop=stop, **kw)

        def column_part(pe, j, out):
            for k in range(KT):
                ins = split_products(pe, out, part_hi(j)[:, k, :], part_lo(j)[:, k, :],
                                     h_hi[:, k, :], h_lo[:, k, :], start=(k == 0), stop=(k == KT - 1))
            return ins

        def row_part(pe, j, k):
            for o in range(KT):
                ins = split_products(pe, banks[o // 2][:, T * (o % 2):T * (o % 2) + T], part_hi(j)[:, o, :],
                                     part_lo(j)[:, o, :], he_hi[:, k, :], he_lo[:, k, :],
                                     skip_group_check=True)
            return ins

        @block.tensor
        def _(pe):
            pe.wait_ge(V0.sem, V0.at("zeros"))
            def full(u, l):
                s = u % SLOTS
                turn = u // SLOTS
                pe.wait_ge(ring_full[s], l * (16 * PER_LAYER[s]) + 16 * (2 + turn + 1))

            def tiles(bank, place, w_ap, c0, nk, rhs, width=P, halfway=None):
                for k in range(nk):
                    if halfway and k == nk // 2:
                        halfway()
                    ins = pe.matmul(bank[0:width, place * T:place * T + T], w_ap[:, k, c0:c0 + width],
                                    rhs[:, k, :], start=(k == 0), stop=(k == nk - 1))
                return ins

            pe.wait_ge(loaded, 16 * 5)
            for u in range(12):
                if u == 5:
                    pe.wait_ge(A0.sem, A0.at("sq"))
                    for k in range(KT):
                        ins = pe.matmul(banks[6][:, 0:T], ones, h_t[:, k, :], start=(k == 0), stop=(k == KT - 1))
                    ins.then_inc(P0.sem, P0.one("norm"))
                pe.wait_ge(V0.sem, V0.at(f"sum{u}"))
                for m in range(4):
                    pe.matmul(banks[7][:, 4 * u + m:4 * u + m + 1], unit_sums[u][:, P * m:P * m + P],
                              ones[:, 0:1], start=True, stop=True)
            pe.drain().then_inc(P0.sem, P0.one("mods"))
            pe.drain().then_inc(MP.sem, MP.first)
            with pe.Fori(0, 2) as l:
                def job(name):
                    if name in before:
                        old, by = before[name]
                        who = AC if by == "act" else DV
                        pe.wait_ge(who.sem, who.at(old, l))
                    return bank_of[name]

                def mean_squares(name, sq, n, lhs=ones, width=T):
                    b = job(name)
                    for k in range(n):
                        ins = pe.matmul(b[:, 0:width], lhs, sq[:, k, :], start=(k == 0), stop=(k == n - 1))
                    ins.then_inc(PE.sem, PE.one(name))

                def pair_tiles(name, u, j0, rhs, nk, n=2, halfway=None):
                    b = job(name)
                    for i in range(n):
                        ins = tiles(b, i, slot(u, nk, UNITS[u][3]), P * (j0 + i), nk, rhs,
                                    halfway=halfway if i == 0 else None)
                    ins.then_inc(PE.sem, PE.one(name))

                pe.wait_ge(DV.sem, DV.at("h1 0", l))
                full(0, l)
                pair_tiles("f0", 0, 0, h_t, KT, halfway=lambda: pe.wait_ge(DV.sem, DV.at("h1 1", l)))
                pair_tiles("f1", 0, 2, h_t, KT)
                full(1, l)
                pair_tiles("q0", 1, 0, h_t, KT)
                pair_tiles("q1", 1, 2, h_t, KT)
                full(2, l)
                for t in range(TT):
                    b = job(f"v{t}")
                    for k in range(KT):
                        ins = pe.matmul(b[:, :], h_t[:, k, P * t:P * t + P], slot(2, KT, 512)[:, k, :],
                                        start=(k == 0), stop=(k == KT - 1))
                    ins.then_inc(PE.sem, PE.one(f"v{t}"))

                def fill(name):
                    if name.startswith("hgate"):
                        i = int(name[-1])
                        if i == 0:
                            full(3, l)
                        pair_tiles(name, 3, 2 * i, h_t, KT)
                    elif name.startswith("gates"):
                        i = int(name[-1])
                        if i % 2 == 0:
                            full(6 + i // 2, l)
                        pair_tiles(name, 6 + i // 2, 2 * (i % 2), h_t, KT)
                    elif name == "cq0":
                        full(4, l)
                        pair_tiles(name, 4, 0, h_t, KT)
                    elif name == "cq1":
                        pair_tiles(name, 4, 2, h_t, KT, n=1)
                    elif name == "ckv":
                        full(5, l)
                        pair_tiles(name, 5, 0, h_t, KT)
                    else:
                        b = job("kr")
                        tiles(b, 0, slot(5, KT, KVL + ROPE), KVL, KT, h_t, width=ROPE)\
                            .then_inc(PE.sem, PE.one("kr"))

                fills = list(FILL)
                for i, name in enumerate(MASKED):
                    if i == 0:
                        pe.wait_ge(DV.sem, DV.at("fk", l))
                        pe.wait_ge(AC.sem, AC.at("q1", l))
                    else:
                        pe.wait_ge(DV.sem, DV.at(f"qk {name}", l))
                    qs, ks = (qf, kf) if i == 0 else (qd[i % 2], kd[i % 2])
                    for t in range(TT):
                        b = job(f"{name} t{t}")
                        for h in range(HH):
                            ins = pe.matmul(b[:, P * h:P * h + P], ks[:, h, P * t:P * t + P],
                                            qs[:, h, P * t:P * t + P], start=True, stop=True)
                        ins.then_inc(PE.sem, PE.one(f"{name} t{t}"))
                    fill(fills.pop(0))
                pe.wait_ge(DV.sem, DV.at(f"qk L{P}", l))
                b = job("cross")
                for h in range(HH):
                    ins = pe.matmul(b[:, P * h:P * h + P], kd[0][:, h, 0:P], qd[0][:, h, P:T],
                                    start=True, stop=True)
                ins.then_inc(PE.sem, PE.one("cross"))
                fill(fills.pop(0))
                fill(fills.pop(0))
                pe.wait_ge(DV.sem, DV.at("L64 t1", l))
                pe.wait_ge(AC.sem, AC.at("cross", l))
                for i in range(2):
                    b = job(f"o{i}")
                    for h in (2 * i, 2 * i + 1):
                        o = b[:, T * (h % 2):T * (h % 2) + T]
                        v = lambda t: vt[:, t, DK * h:DK * h + DK]
                        pe.matmul(o[:, 0:P], v(0), pairs[0][:, h, :], start=True, stop=True)
                        pe.matmul(o[:, P:T], v(0), cross[:, h, :], start=True, stop=False)
                        ins = pe.matmul(o[:, P:T], v(1), pairs[1][:, h, :], start=False, stop=True)
                    ins.then_inc(PE.sem, PE.one(f"o{i}"))
                for name in fills[:2]:
                    fill(name)
                pe.wait_ge(AC.sem, AC.at("c sq", l))
                mean_squares("cq norm", csq[:, 0:3, :], 3)
                mean_squares("ckv norm", csq[:, 3:5, :], 2)
                for i in range(2):
                    b = job(f"o norm{i}")
                    pe.matmul(b[:, :], ones, osq[:, 2 * i:2 * i + 2, :], start=True, stop=True)\
                        .then_inc(PE.sem, PE.one(f"o norm{i}"))
                for name in fills[2:]:
                    fill(name)
                pe.wait_ge(DV.sem, DV.at("cn", l))
                full(10, l)
                wq = slot(10, 3, NH * DQK)
                for i in range(4):
                    b = job(f"q up{i}")
                    for j in range(2):
                        ins = tiles(b, j, wq, DQK * (2 * i + j), 3, cq, width=DQK)
                    ins.then_inc(PE.sem, PE.one(f"q up{i}"))
                full(11, l)
                wkv = slot(11, 2, NH * (NOPE + VD))
                for i in range(4):
                    b = job(f"k up{i}")
                    for j in range(2):
                        ins = tiles(b, j, wkv, (NOPE + VD) * (2 * i + j), 2, ckv, width=NOPE)
                    ins.then_inc(PE.sem, PE.one(f"k up{i}"))
                for t in range(TT):
                    b = job(f"v up{t}")
                    for k in range(2):
                        ins = pe.matmul(b[:, :], ckv[:, k, P * t:P * t + P],
                                        wkv[:, k, :].rearrange("p (h c) -> p h c", h=NH)[:, :, NOPE:NOPE + VD],
                                        start=(k == 0), stop=(k == 1))
                    ins.then_inc(PE.sem, PE.one(f"v up{t}"))
                turn = const("turn")[NOPE:DQK, :]
                for i in range(4):
                    pe.wait_ge(AC.sem, AC.at(f"q up{i}", l))
                    b = job(f"q turn{i}")
                    pe.matmul(b[0:DQK, :], turn, q_a[NOPE:DQK, 2 * i:2 * i + 2, :], start=True, stop=True)\
                        .then_inc(PE.sem, PE.one(f"q turn{i}"))
                pe.wait_ge(AC.sem, AC.at("kr", l))
                b = job("k turn")
                pe.matmul(b[0:DQK, 0:T], turn, krs[NOPE:DQK, :], start=True, stop=True)\
                    .then_inc(PE.sem, PE.one("k turn"))
                pe.wait_ge(DV.sem, DV.at("oa", l))
                full(12, l)
                for i in range(2):
                    pair_tiles(f"ya{i}", 12, 2 * i, oa, 4)
                pe.wait_ge(DV.sem, DV.at("k turn", l))
                pe.wait_ge(AC.sem, AC.at("v up1", l))
                scores_pe(pe, job, PE, "", lambda h, t: q_a[0:DQK, h, P * t:P * t + P],
                          lambda h, n: k_a[0:DQK, h, 0:n])
                for i in range(2, 4):
                    pair_tiles(f"ya{i}", 12, 2 * i, oa, 4)
                values_pe(pe, job, PE, AC, DV, l, "", lambda h, t: v_a[:, t, VD * h:VD * h + VD],
                          p_a, pT_a, ident)
                pe.wait_ge(AC.sem, AC.at("ov3", l))
                full(13, l)
                for i in range(4):
                    pair_tiles(f"yb{i}", 13, 2 * i, ob, 4)
                pe.wait_ge(DV.sem, DV.at("yb3", l))
                for i in range(4):
                    if i % 2 == 0:
                        full(14 + i // 2, l)
                    pair_tiles(f"out{i}", 14 + i // 2, 2 * (i % 2), h_t, KT)
                b = job("norm2")
                for k in range(KT):
                    if k % 2 == 0:
                        pe.wait_ge(AC.sem, AC.at(SQ2[k // 2], l))
                    ins = pe.matmul(b[:, 0:T], ones, xsq[:, k, :], start=(k == 0), stop=(k == KT - 1))
                ins.then_inc(PE.sem, PE.one("norm2"))
                pe.wait_ge(DV.sem, DV.at("h2 0", l))
                b = job("router")
                for t in range(TT):
                    for k in range(KT):
                        if t == 0 and k == KT // 2:
                            pe.wait_ge(DV.sem, DV.at("h2 1", l))
                        ins = pe.matmul(b[:, NE * t:NE * t + NE], h_t[:, k, P * t:P * t + P],
                                        wr[:, k, :], start=(k == 0), stop=(k == KT - 1))
                ins.then_inc(PE.sem, PE.one("router"))
                pe.wait_ge(DV.sem, DV.at("comb", l))
                b = job("combine")
                for t in range(TT):
                    ins = pe.transpose(b[0:NE, P * t:P * t + P], combw[:, NE * t:NE * t + NE], ident)
                ins.then_inc(PE.sem, PE.one("combine"))
                pe.wait_ge(DV.sem, DV.at("combine", l))

                clear_sums(pe)
                with pe.Fori(0, NE) as it:
                    e = l * NE + it
                    pe.wait_ge(MV.sem, MV.at("next", e - 1))
                    pe.matmul(banks[6][:, 0:T], ones16, pick, start=True, stop=True)\
                        .then_inc(MP.sem, MP.one("pick"))
                    for j in range(8):
                        m = j // 2
                        if j % 2 == 0:
                            pe.wait_ge(MV.sem, MV.at(f"he{m + 2}", e - 1) if m < 2 else MV.at(f"he{m - 2}", e))
                        pe.wait_ge(MV.sem, MV.at(f"lo{j}", e))
                        column_part(pe, j, banks[4 + m % 2][:, T * (j % 2):T * (j % 2) + T])\
                            .then_inc(MP.sem, MP.one(f"part{j}"))
                    pe.wait_ge(MV.sem, MV.at("acc lo", e))
                    for i in range(CH // P):
                        for j in range(2):
                            ins = pe.matmul(banks[7][:, 2 * i:2 * i + 2],
                                            acc_split[:, CH * j + P * i:CH * j + P * i + P], one_r[:, :],
                                            start=(j == 0), stop=(j == 1))
                    ins.then_inc(MP.sem, MP.one("mods"))
                    for k in range(4):
                        pe.wait_ge(MV.sem, MV.at(f"he{k}", e))
                        pe.wait_ge(MV.sem, MV.at(f"lo{8 + k}", e))
                        row_part(pe, 8 + k, k).then_inc(MP.sem, MP.one(f"part{8 + k}"))
                for k in range(KT):
                    if k % 2 == 0:
                        pe.wait_ge(AC.sem, AC.at(SQ0[k // 2], l))
                    ins = pe.matmul(banks[7][:, 0:T], ones, h_t[:, k, :], start=(k == 0), stop=(k == KT - 1))
                ins.then_inc(PE.sem, PE.one("next norm"))
            def unit(u, base):
                s = A_SLOT[u] if base is A_BASE else u % SLOTS
                pe.wait_ge(ring_full[s], 16 * (base[s] + u // SLOTS + 1))

            def r_job(name):
                if name in r_old:
                    old, by = r_old[name]
                    who = AR if by == "act" else VR
                    pe.wait_ge(who.sem, who.at(old))
                return r_bank[name]

            def sum_squares(b, sq, n, A=None, names=None):
                for k in range(n):
                    if names and k % 2 == 0:
                        pe.wait_ge(A.sem, A.at(names[k // 2]))
                    ins = pe.matmul(b[:, 0:T], ones, sq[:, k, :], start=(k == 0), stop=(k == n - 1))
                return ins

            sum_squares(r_job("norm1"), h_t, KT, AR, SQ1).then_inc(PR.sem, PR.one("norm1"))
            pe.wait_ge(VR.sem, VR.at("h1 0"))
            def lru_input(i):
                name = f"xr{i}" if i < 8 else f"gelu{i - 8}"
                if i % 2 == 0:
                    unit(i // 2, R_BASE)
                b = r_job(name)
                for j in range(2):
                    ins = tiles(b, j, slot(i // 2, KT, 352), LB * (2 * (i % 2) + j), KT, h_t, width=LB,
                                halfway=None if i + j else lambda: pe.wait_ge(VR.sem, VR.at("h1 1")))
                ins.then_inc(PR.sem, PR.one(name))

            for i in range(12):
                lru_input(i)
            pe.wait_ge(VR.sem, VR.at("conv"))
            unit(8, R_BASE)
            pe.wait_ge(gate_half, 16)
            wg = slot(8, 2 * LN, LB, parts=LB)
            for n in range(LN):
                b = r_job(f"ri{n}")
                pe.matmul(b[LBS, 0:T], wg[:, n, :], xc[LBS, n, :], start=True, stop=True)
                pe.matmul(b[LBS, T:2 * T], wg[:, LN + n, :], xc[LBS, n, :], start=True, stop=True)\
                    .then_inc(PR.sem, PR.one(f"ri{n}"))
            for i in range(12, 16):
                lru_input(i)
            outs = [r_job(f"out{i}") for i in range(4)]
            for b in outs:
                pe.matmul(b[:, :], zeros[:, 0:P], zeros[:, :], start=True, stop=True, skip_group_check=True)
            for u in range(4):
                pe.wait_ge(VR.sem, VR.at(f"y{u}"))
                unit(9 + u, R_BASE)
                wo = slot(9 + u, 4, D, parts=LB)
                for o in range(KT):
                    for k in range(4):
                        ins = pe.matmul(outs[o // 2][:, T * (o % 2):T * (o % 2) + T], wo[:, k, P * o:P * o + P],
                                        gelu[LBS, 4 * u + k, :], start=False, stop=False, skip_group_check=True)
                    if u == 3 and o % 2:
                        ins.then_inc(PR.sem, PR.one(f"out{o // 2}"))
            sum_squares(r_job("norm2"), h_t, KT, AR, SQ2).then_inc(PR.sem, PR.one("norm2"))

            def mlp_pe(layer, h2):
                pe_steps, act_steps_, dve_steps_ = MLP[layer]
                pe.wait_ge(h2.sem, h2.at("h lo1"))
                pe.drain().then_inc(pe_steps.sem, pe_steps.first)
                clear_sums(pe)
                with pe.Fori(0, MLP_TURNS) as e:
                    for m in range(4):
                        pe.wait_ge(act_steps_.sem, act_steps_.at(*[("g3", e - 1), ("g1", e - 1),
                                                                   ("g2", e - 1), ("g0", e)][m]))
                        pe.wait_ge(dve_steps_.sem, dve_steps_.at(f"lo{m}", e))
                        column_part(pe, m, banks[MLP_BANK[m]][:, 0:T])\
                            .then_inc(pe_steps.sem, pe_steps.one(f"part{m}"))
                    for k in range(4):
                        pe.wait_ge(dve_steps_.sem, dve_steps_.at(f"he{k}", e))
                        pe.wait_ge(dve_steps_.sem, dve_steps_.at(f"lo{4 + k}", e))
                        row_part(pe, 4 + k, k).then_inc(pe_steps.sem, pe_steps.one(f"part{4 + k}"))
                        if layer == 0 and k == 1:
                            pe.wait_ge(dve_steps_.sem, dve_steps_.at("acc1", e))
                            pe.wait_ge(kv_summed, e + 1)
                            at = 0
                            for i, n in enumerate(MLP_CHUNKS):
                                for c in range(n // P):
                                    ins = pe.matmul(banks[7][:, at:at + 1], accs2[i][:, P * c:P * c + P],
                                                    ones[:, 0:1], start=True, stop=True)
                                    at += 1
                            ins.then_inc(pe_steps.sem, pe_steps.one("mods"))

            mlp_pe(0, VR)

            def a_job(name):
                if name in a_old:
                    old, by = a_old[name]
                    who = AA if by == "act" else VA
                    pe.wait_ge(who.sem, who.at(old))
                return a_bank[name]

            sum_squares(a_job("norm"), h_t, KT, AA, SQ0).then_inc(PA.sem, PA.one("norm"))
            pe.wait_ge(VA.sem, VA.at("h 0"))

            def projected(name, u0, rhs, which=range(4)):
                for i in which:
                    u = u0 + i // 2
                    if i % 2 == 0:
                        unit(u, A_BASE)
                    b = a_job(f"{name}{i}")
                    for j in range(2):
                        ins = tiles(b, j, slot(A_SLOT[u], KT, 512), P * (2 * (i % 2) + j), KT, rhs,
                                    halfway=(lambda: pe.wait_ge(VA.sem, VA.at("h 1")))
                                    if name == "k" and i + j == 0 else None)
                    ins.then_inc(PA.sem, PA.one(f"{name}{i}"))

            def head_squares(name, sq):
                for i in range(4):
                    b = a_job(f"{name}{i}")
                    pe.matmul(b[:, :], heads_ones, sq[:, 2 * i:2 * i + 2, :], start=True, stop=True)\
                        .then_inc(PA.sem, PA.one(f"{name}{i}"))

            def values(which):
                for i in which:
                    u, t = 2 + i // 2, i % 2
                    if t == 0:
                        unit(u, A_BASE)
                    b = a_job(f"v{i}")
                    for k in range(KT):
                        ins = pe.matmul(b[:, :], h_t[:, k, P * t:P * t + P], slot(u, KT, 512)[:, k, :],
                                        start=(k == 0), stop=(k == KT - 1))
                    ins.then_inc(PA.sem, PA.one(f"v{i}"))

            projected("k", 0, h_t)
            pe.wait_ge(VA.sem, VA.at("hq"))
            projected("q", 4, hq, (0, 1))
            pe.wait_ge(AA.sem, AA.at("k sq"))
            head_squares("kn", ksq)
            projected("q", 4, hq, (2, 3))
            values((0, 1))
            pe.wait_ge(AA.sem, AA.at("q sq"))
            head_squares("qn", ksq)
            values((2, 3))
            pe.wait_ge(VA.sem, VA.at("q"))
            for half, tag in enumerate(("A ", "B ")):
                scores_pe(pe, a_job, PA, tag,
                          lambda h, t: q2_[:, 4 * half + h // 2, h % 2, P * t:P * t + P],
                          lambda h, n: k2_[:, 4 * half + h // 2, 0:n])
            for half, tag in enumerate(("A ", "B ")):
                values_pe(pe, a_job, PA, AA, VA, 0, tag,
                          lambda h, t: v2_[:, t, HD * (8 * half + h):HD * (8 * half + h) + HD],
                          p2_[half], pT2, ident)
            pe.wait_ge(AA.sem, AA.at("B ov3"))
            projected("out", 8, o2_)
            sum_squares(a_job("norm2"), h_t, KT, AA, SQ2).then_inc(PA.sem, PA.one("norm2"))
            mlp_pe(1, VA)

        @block.gpsimd
        def _(pool):
            with pool.Fori(0, MLP_TURNS) as e:
                pool.wait_ge(chunk2_full[2], e * 16 + 16)
                pool.wait_ge(MLP[0][0].sem, MLP[0][0].at("mods", e - 1))
                ck = chunks2[2]
                c = cact[:, KT:2 * KT].unsqueeze(2).broadcast_to([P, KT, MLP_CHUNKS[2]])
                nc.gpsimd.tensor_tensor(ck, ck, c, ALU.mult)
                for n in (4, 2, 1):
                    pool.drain()
                    out = ck[:, 0:n, :] if n > 1 else accs2[2].unsqueeze(1)
                    ins = nc.gpsimd.tensor_tensor(out, ck[:, 0:n, :], ck[:, n:2 * n, :], ALU.add)
                ins.then_inc(kv_summed, 1)

        def rstd_ln(act, bank, out, n, width=T):
            return act.activation(out, bank[:, 0:width], ACT.Ln, scale=1.0 / n, bias=epsb[:, 0:1])

        def rstd_exp(act, out):
            return act.activation(out, out, ACT.Exp, scale=-0.5)

        def rstd(act, bank, out, n, width=T):
            rstd_ln(act, bank, out, n, width)
            act.drain()
            return rstd_exp(act, out)

        @block.scalar
        def _(act):
            act.wait_ge(V0.sem, V0.at("zeros"))
            act.wait_ge(loaded, 16 * 5)
            act.activation(cact[:, :], col("c", 0, 2 * KT), ACT.Silu).then_inc(A0.sem, A0.one("c"))
            for u in range(12):
                if u == 6:
                    act.wait_ge(x_loaded, 16)
                    act.activation(h_t, x_t, ACT.Square).then_inc(A0.sem, A0.one("sq"))
                    act.wait_ge(V0.sem, V0.at("angles"))
                    act.activation(trig[:, :], mix[:, 0:2 * T], ACT.Sin).then_inc(A0.sem, A0.one("trig"))
                    act.wait_ge(V0.sem, V0.at("lb"))
                    act.activation(lbs[:, 0:2 * HH], lbs[:, 0:2 * HH], ACT.Exp).then_inc(A0.sem, A0.one("lb"))
                if u == 8:
                    act.wait_ge(P0.sem, P0.at("norm"))
                    rstd(act, banks[6], rs[:, 0, :], D).then_inc(AC.sem, AC.first)
                act.wait_ge(ring_full[u % SLOTS], 16 * (u // SLOTS + 1))
                unit = slot(u, KT, 512)
                if u == 0:
                    act.drain()
                for k in range(KT):
                    ins = act.activation(unit[:, k, :], unit[:, k, :], ACT.Copy, scale=cact[:, k:k + 1])
                ins.then_inc(A0.sem, A0.one(f"mul{u}"))

            def round_stream(A, V, turn=0):
                for i in range(2):
                    act.wait_ge(V.sem, V.at(H2[i], turn))
                    half = slice(4 * i, 4 * i + 4)
                    act.activation(h_hi[:, half, :], h_t[:, half, :], ACT.Copy).then_inc(A.sem, A.one(f"h hi{i}"))

            with act.Fori(0, 2) as l:
                def emptied(name, out, func, rows=P, width=512, **kw):
                    act.wait_ge(PE.sem, PE.at(name, l))
                    src = bank_of[name][0:rows, 0:width]
                    if len(out.shape) == 3:
                        src = src.rearrange("p (a b) -> p a b", a=out.shape[1])
                    act.activation(out, src, func, **kw).then_inc(AC.sem, AC.one(name))

                def two(t, i, n=2):
                    return t[:, 2 * i:2 * i + n, :]

                for i in range(2):
                    emptied(f"f{i}", two(fwd, i), ACT.Sigmoid)
                for i in range(2):
                    emptied(f"q{i}", two(qf, i), ACT.Silu)
                for i in range(2):
                    emptied(f"v{i}", vt[:, i, :], ACT.Copy)

                def fill(name):
                    if name.startswith("hgate"):
                        emptied(name, two(hgate, int(name[-1])), ACT.Silu)
                    elif name.startswith("gates"):
                        emptied(name, two(gates, int(name[-1])), ACT.Sigmoid)
                    elif name == "kr":
                        act.wait_ge(PE.sem, PE.at(name, l))
                        act.activation(krs[NOPE:DQK, :], bank_of[name][0:ROPE, 0:T], ACT.Copy)\
                            .then_inc(AC.sem, AC.one(name))
                    elif name == "cq1":
                        emptied(name, cq[:, 2:3, :], ACT.Copy, width=T)
                    elif name == "cq0":
                        emptied(name, cq[:, 0:2, :], ACT.Copy)
                    else:
                        emptied(name, ckv, ACT.Copy)

                fills = list(FILL)
                for _ in MASKED:
                    fill(fills.pop(0))
                emptied("cross", cross, ACT.Copy, scale=DK ** -0.5)
                fill(fills.pop(0))
                fill(fills.pop(0))
                emptied("o0", two(oraw, 0), ACT.Copy)
                emptied("o1", two(oraw, 1), ACT.Copy)
                act.drain()
                act.activation(osq, oraw, ACT.Square).then_inc(AC.sem, AC.one("o sq"))
                act.activation(csq, view(cqkv, 0, 5, T), ACT.Square).then_inc(AC.sem, AC.one("c sq"))
                for name in fills[:2]:
                    fill(name)
                for name, n, out in (("cq norm", QL, rs[:, 0, :]), ("ckv norm", KVL, rs[:, 1, :])):
                    act.wait_ge(PE.sem, PE.at(name, l))
                    rstd_ln(act, bank_of[name], out, n).then_inc(AC.sem, AC.one(name))
                for i in range(2):
                    act.wait_ge(PE.sem, PE.at(f"o norm{i}", l))
                    rstd_ln(act, bank_of[f"o norm{i}"], mix[:, 2048 + 512 * i:2560 + 512 * i], DK, 512)\
                        .then_inc(AC.sem, AC.one(f"o norm{i}"))
                act.drain()
                rstd_exp(act, rs).then_inc(AC.sem, AC.one("c rs"))
                rstd_exp(act, ors).then_inc(AC.sem, AC.one("o rs"))
                for name in fills[2:]:
                    fill(name)
                act.wait_ge(DV.sem, DV.at("oa", l))
                for i in range(4):
                    emptied(f"q up{i}", q_a[0:DQK, 2 * i:2 * i + 2, :], ACT.Copy, rows=DQK)
                for i in range(4):
                    emptied(f"k up{i}", k_a[0:NOPE, 2 * i:2 * i + 2, :], ACT.Copy, rows=NOPE)
                for i in range(2):
                    emptied(f"v up{i}", v_a[:, i, :], ACT.Copy)
                for g in range(6):
                    exp_act(nc, act, AC, DV, l, "", g, p_a, nmax[0], sums[0])
                for g in range(6):
                    transposed_act(nc, act, lambda n: bank_of[n], PE, AC, l, "", g, pT_a)
                outputs_act(nc, act, lambda n: bank_of[n], PE, AC, l, "", ob)
                for i in range(4):
                    act.wait_ge(DV.sem, DV.at(f"out{i}", l))
                    act.activation(two(xsq, i), two(x_t, i), ACT.Square).then_inc(AC.sem, AC.one(SQ2[i]))
                act.wait_ge(PE.sem, PE.at("norm2", l))
                rstd(act, bank_of["norm2"], rs[:, 0, :], D).then_inc(AC.sem, AC.one("norm2"))
                round_stream(AC, DV, l)
                emptied("router", scores, ACT.Sigmoid, width=TT * NE)
                with act.Fori(0, NE) as it:
                    e = l * NE + it

                    def round_part(j):
                        act.wait_ge(MP.sem, MP.at(f"part{(j + 8) % 12}", e - 1 if j < 4 else e))
                        if j in (0, 4):
                            act.wait_ge(gu_full[j // 4], e * 32 + 32)
                        if j == 8:
                            act.wait_ge(down_full, e * 16 + 16)
                        act.activation(part_hi(j), moe_raw(j), ACT.Copy).then_inc(MA.sem, MA.one(f"hi{j}"))

                    for j in range(5):
                        round_part(j)
                    act.wait_ge(MV.sem, MV.at("acc", e))
                    act.activation(acc_split[:, 0:CH], accs, ACT.Copy).then_inc(MA.sem, MA.one("acc hi"))
                    for m in range(4):
                        act.wait_ge(MP.sem, MP.at(f"part{2 * m + 1}", e))
                        act.activation(sg[:, m, :], banks[4 + m % 2][:, 0:T], ACT.Silu)\
                            .then_inc(MA.sem, MA.one(f"sg{m}"))
                        for j in (2 * m + 5, 2 * m + 6):
                            if j < 12:
                                round_part(j)
                for i in range(4):
                    act.wait_ge(DV.sem, DV.at(X2[i], l))
                    act.activation(two(h_t, i), two(x_t, i), ACT.Square).then_inc(AC.sem, AC.one(SQ0[i]))
                act.wait_ge(PE.sem, PE.at("next norm", l))
                rstd(act, banks[7], rs[:, 0, :], D).then_inc(AC.sem, AC.one("next norm"))
            def norm_act(A, V, Pj, bank, sq, name, ready):
                if len(ready) == 1:
                    act.wait_ge(V.sem, ready[0])
                    act.activation(h_t, x_t, ACT.Square).then_inc(A.sem, A.one(sq[0]))
                else:
                    for i in range(4):
                        act.wait_ge(V.sem, ready[i])
                        act.activation(h_t[:, 2 * i:2 * i + 2, :], x_t[:, 2 * i:2 * i + 2, :], ACT.Square)\
                            .then_inc(A.sem, A.one(sq[i]))
                act.wait_ge(Pj.sem, Pj.at(name))
                rstd(act, bank[name], rs[:, 0, :], D).then_inc(A.sem, A.one(name))

            norm_act(AR, VR, PR, r_bank, SQ1, "norm1", [VR.at(f"x{i}") for i in range(4)])
            act.activation(lam[2][LBS, :], lam[1][LBS, :], ACT.Exp, scale=-1.0)
            act.drain()
            act.activation(lam[2][LBS, :], lam[2][LBS, :], ACT.Ln, bias=epsb[LBS, 1:2])\
                .then_inc(AR.sem, AR.one("softplus"))
            for i in range(8):
                act.wait_ge(PR.sem, PR.at(f"xr{i}"))
                act.activation(xr[LBS, 2 * i:2 * i + 2, 3:T + 3],
                               r_bank[f"xr{i}"][LBS, :].rearrange("p (a b) -> p a b", a=2), ACT.Copy)\
                    .then_inc(AR.sem, AR.one(f"xr{i}"))
            def gelu_act(i):
                act.wait_ge(PR.sem, PR.at(f"gelu{i}"))
                act.activation(gelu[LBS, 2 * i:2 * i + 2, :],
                               r_bank[f"gelu{i}"][LBS, :].rearrange("p (a b) -> p a b", a=2),
                               ACT.Gelu_apprx_tanh).then_inc(AR.sem, AR.one(f"gelu{i}"))

            for i in range(4):
                gelu_act(i)
            for n in range(LN):
                act.wait_ge(PR.sem, PR.at(f"ri{n}"))
                b = r_bank[f"ri{n}"]
                act.activation(rg[LBS, n, :], b[LBS, 0:T], ACT.Sigmoid, bias=col("ba", n)[LBS, :])
                act.activation(ig[LBS, n, :], b[LBS, T:2 * T], ACT.Sigmoid, bias=col("bx", n)[LBS, :])\
                    .then_inc(AR.sem, AR.one(f"ri{n}"))
            act.drain()
            for n in range(LN):
                act.wait_ge(VR.sem, VR.at(f"ix{n // 4}"))
                ins = act.activation(xc[LBS, n, :], rg[LBS, n, :], ACT.Tanh, scale=lam[3][LBS, n:n + 1])
            ins.then_inc(AR.sem, AR.one("tanh"))
            for n in range(LN):
                ins = act.activation(rg[LBS, n, :], rg[LBS, n, :], ACT.Exp, scale=lam[4][LBS, n:n + 1])
            ins.then_inc(AR.sem, AR.one("decay"))
            for i in range(4, 8):
                gelu_act(i)
            for i in range(4):
                act.wait_ge(VR.sem, VR.at(f"u{i}"))
                g = slice(4 * i, 4 * i + 4)
                act.activation(xc[LBS, g, :], xc[LBS, g, :], ACT.Sqrt).then_inc(AR.sem, AR.one(f"root{i}"))
            norm_act(AR, VR, PR, r_bank, SQ2, "norm2", [VR.at(f"out{i}") for i in range(4)])

            round_stream(AR, VR)

            def mlp_act(layer, base):
                pe_steps, act_steps_, dve_steps_ = MLP[layer]
                act.drain().then_inc(act_steps_.sem, act_steps_.first)
                with act.Fori(0, MLP_TURNS // 2) as it:
                    for pair in range(2):
                        e = it * 2 + pair
                        slots = MLP_SLOTS[layer][2 * pair:2 * pair + 2]

                        def round_part(j):
                            pe_turn = e - 1 if j < 4 else e
                            act.wait_ge(pe_steps.sem, pe_steps.at(f"part{(j + 4) % 8}", pe_turn))
                            if j % 4 == 0:
                                s = slots[j // 4]
                                act.wait_ge(ring_full[s], it * 16 + 16 * (base[s] + 1))
                            act.activation(part_hi(j), mlp_raw(slots, j), ACT.Copy)\
                                .then_inc(act_steps_.sem, act_steps_.one(f"hi{j}"))

                        for j in range(4):
                            round_part(j)
                            if layer == 0 and j in (0, 2):
                                i = j // 2
                                act.wait_ge(chunk2_full[i], e * 16 + 16)
                                for k in range(KT):
                                    ins = act.activation(chunks2[i][:, k, :], chunks2[i][:, k, :], ACT.Copy,
                                                         scale=cact[:, KT + k:KT + k + 1])
                                ins.then_inc(act_steps_.sem, act_steps_.one(f"mul{i}"))
                        for m in range(4):
                            act.wait_ge(pe_steps.sem, pe_steps.at(f"part{m}", e))
                            act.activation(sg[:, m, :], banks[MLP_BANK[m]][:, 0:T], ACT.Relu)
                            act.drain()
                            act.activation(he[:, m, :], sg[:, m, :], ACT.Square)\
                                .then_inc(act_steps_.sem, act_steps_.one(f"g{m}"))
                            round_part(m + 4)

            mlp_act(0, M0_BASE)
            norm_act(AA, VA, PA, a_bank, SQ0, "norm", [VA.at(n) for n in X2])

            def taken(name, out):
                act.wait_ge(PA.sem, PA.at(name))
                src = a_bank[name][:, :]
                if len(out.shape) == 3:
                    src = src.rearrange("p (a b) -> p a b", a=2)
                act.activation(out, src, ACT.Copy).then_inc(AA.sem, AA.one(name))

            def head_norm(name, out):
                for i in range(4):
                    act.wait_ge(PA.sem, PA.at(f"{name}{i}"))
                    rstd_ln(act, a_bank[f"{name}{i}"], out[:, 512 * i:512 * i + 512], HD, 512)\
                        .then_inc(AA.sem, AA.one(f"{name}{i}"))
                act.drain()
                rstd_exp(act, out).then_inc(AA.sem, AA.one(f"{name} rs"))

            for i in range(4):
                taken(f"k{i}", k2_[:, 2 * i:2 * i + 2, :])
            act.drain()
            act.activation(ksq, k2_, ACT.Square).then_inc(AA.sem, AA.one("k sq"))

            def queries(i):
                act.wait_ge(PA.sem, PA.at(f"q{i}"))
                for rows, j in own:
                    ins = act.activation(q2_[rows, 2 * i:2 * i + 2, j, :],
                                         a_bank[f"q{i}"][rows, :].rearrange("p (a b) -> p a b", a=2), ACT.Copy)
                ins.then_inc(AA.sem, AA.one(f"q{i}"))

            def values(i):
                taken(f"v{i}", v2_[:, i % 2, 512 * (i // 2):512 * (i // 2) + 512])

            queries(0)
            queries(1)
            head_norm("kn", mix[:, 8192:10240])
            queries(2)
            queries(3)
            act.drain()
            for rows, j in own:
                ins = act.activation(ksq[rows, :, :], q2_[rows, :, j, :], ACT.Square)
            ins.then_inc(AA.sem, AA.one("q sq"))
            values(0)
            values(1)
            head_norm("qn", mix[:, 11264:13312])
            values(2)
            values(3)
            a_of = lambda n: a_bank[n]
            for g in range(6):
                exp_act(nc, act, AA, VA, 0, "A ", g, p2_[0], nmax[0], sums[0])
            for g in range(6):
                transposed_act(nc, act, a_of, PA, AA, 0, "A ", g, pT2)
                exp_act(nc, act, AA, VA, 0, "B ", g, p2_[1], nmax[1], sums[1])
            outputs_act(nc, act, a_of, PA, AA, 0, "A ", o2_[:, 0:4, :])
            for g in range(6):
                transposed_act(nc, act, a_of, PA, AA, 0, "B ", g, pT2)
            outputs_act(nc, act, a_of, PA, AA, 0, "B ", o2_[:, 4:8, :])
            norm_act(AA, VA, PA, a_bank, SQ2, "norm2", [VA.at(f"out{i}") for i in range(4)])
            round_stream(AA, VA)
            mlp_act(1, M1_BASE)

        def routing():
            tt, ts = nc.vector.tensor_tensor, nc.vector.tensor_scalar
            wait = nc.vector.drain
            at = [0]

            def cols(*shape):
                n = int(np.prod(shape))
                ap = sm[:, at[0]:at[0] + n]
                at[0] += n
                if len(shape) == 3:
                    return ap.rearrange("p (a b c) -> p a b c", a=shape[0], b=shape[1])
                return ap.rearrange("p (a b) -> p a b", a=shape[0])

            s = scores.rearrange("p (t e) -> p t e", t=TT)
            v = biased.rearrange("p (t e) -> p t e", t=TT)
            tt(v, s, heads(rbias, TT), ALU.add)
            wait()
            g = biased.rearrange("p (g e) -> p g e", g=TT * NG)
            sums6 = cols(TT * NG, 6)
            tt(sums6[:, :, 0:3], g[:, :, 0:3], g[:, :, 1:4], ALU.add)
            tt(sums6[:, :, 3:5], g[:, :, 0:2], g[:, :, 2:4], ALU.add)
            tt(sums6[:, :, 5:6], g[:, :, 0:1], g[:, :, 3:4], ALU.add)
            wait()
            score = cols(TT, NG)
            nc.vector.tensor_reduce(score.rearrange("p t g -> p (t g)"), sums6, AX, ALU.max)

            def first_best(x, n, order):
                top = cols(TT, 1)
                wait()
                nc.vector.tensor_reduce(top.rearrange("p t a -> p (t a)"), x, AX, ALU.max)
                wait()
                is_top = cols(TT, n)
                tt(is_top, x, top.broadcast_to([P, TT, n]), ALU.is_equal)
                wait()
                tt(is_top, is_top, heads(order, TT), ALU.mult)
                wait()
                lowest = cols(TT, 1)
                nc.vector.tensor_reduce(lowest.rearrange("p t a -> p (t a)"), is_top, AX, ALU.max)
                wait()
                tt(is_top, is_top, lowest.broadcast_to([P, TT, n]), ALU.is_equal)
                wait()
                return is_top

            best = first_best(score, NG, order[:, 0:NG])
            inside = cols(TT * NG, EG)
            nc.vector.tensor_copy(inside, best.rearrange("p t g -> p (t g)").unsqueeze(2)
                                  .broadcast_to([P, TT * NG, EG]))
            wait()
            left = cols(TT * NG, EG)
            out = cols(TT * NG, EG)
            tt(left, g, inside, ALU.mult)
            ts(out, inside, -NEG, NEG, ALU.mult, ALU.add)
            wait()
            tt(left, left, out, ALU.add)
            wait()
            flat = lambda ap: ap.rearrange("p g e -> p (g e)").rearrange("p (t e) -> p t e", t=TT)
            one = first_best(flat(left), NE, order)
            ts(out, one.rearrange("p t e -> p (t e)").rearrange("p (g e) -> p g e", e=EG), 2 * NEG, None, ALU.mult)
            wait()
            tt(left, left, out, ALU.add)
            two = first_best(flat(left), NE, order)
            tt(one, one, two, ALU.add)
            wait()
            tt(one, one, s, ALU.mult)
            wait()
            total = cols(TT, 1)
            nc.vector.tensor_reduce(total.rearrange("p t a -> p (t a)"), one, AX, ALU.add)
            wait()
            nc.vector.reciprocal(total, total)
            wait()
            tt(combw.rearrange("p (t e) -> p t e", t=TT), one, total.broadcast_to([P, TT, NE]), ALU.mult)

        @block.vector
        def _(dve):
            tt, ts, stt = nc.vector.tensor_tensor, nc.vector.tensor_scalar, nc.vector.scalar_tensor_tensor
            nc.vector.memset(zeros[:, :], 0.0)
            nc.vector.memset(epsb[:, 0:1], EPS)
            nc.vector.memset(epsb[:, 1:2], 1.0)
            dve.drain()
            nc.vector.tensor_copy(one_r[:, :], epsb[:, 1:2].broadcast_to([P, 2]))
            for i in range(NE):
                nc.vector.memset(order[:, i:i + 1], float(NE - i))
            dve.drain().then_inc(V0.sem, V0.one("zeros"))
            dve.drain().then_inc(MV.sem, MV.first)
            dve.wait_ge(loaded, 16 * 5)
            ang, n = mix[:, 2 * T:3 * T], mix[:, 3 * T:4 * T]
            nc.vector.tensor_copy(ang, posi[:, :])
            dve.drain()
            ts(ang, ang, const("freq"), None, ALU.mult)
            dve.drain()
            for out, quarter in ((mix[:, 0:T], 0.25), (mix[:, T:2 * T], 0.0)):
                ts(n, ang, 1.0 / TWO_PI, quarter, ALU.mult, ALU.add)
                dve.drain()
                ts(n, n, MAGIC, None, ALU.add)
                dve.drain()
                ts(n, n, -MAGIC, None, ALU.add)
                dve.drain()
                stt(out, n, -C1, ang, ALU.mult, ALU.add)
                dve.drain()
                stt(out, n, -C2, out, ALU.mult, ALU.add)
                dve.drain()
                stt(out, n, -C3, out, ALU.mult, ALU.add)
                dve.drain()
                if quarter:
                    ts(out, out, float(np.pi / 2), None, ALU.add)
                    dve.drain()
                ts(out, out, 3.1415925, -3.1415925, ALU.min, ALU.max)
            dve.drain().then_inc(V0.sem, V0.one("angles"))
            a0, a1 = col("lb", 0, HH), col("lb", HH, HH)
            top = small[:, 0:HH]
            tt(top, a0, a1, ALU.max)
            dve.drain()
            tt(lbs[:, 0:HH], a0, top, ALU.subtract)
            tt(lbs[:, HH:2 * HH], a1, top, ALU.subtract).then_inc(V0.sem, V0.one("lb"))

            def unit_sum(u):
                dve.wait_ge(A0.sem, A0.at(f"mul{u}"))
                nc.vector.tensor_reduce(unit_sums[u], slot(u, KT, 512).rearrange("p k n -> p n k"), AX, ALU.add)\
                    .then_inc(V0.sem, V0.one(f"sum{u}"))

            for u in range(6):
                unit_sum(u)
            dve.wait_ge(A0.sem, A0.at("lb"))
            e0, e1, total = small[:, 4:8], small[:, 8:12], small[:, 12:16]
            tt(total, lbs[:, 0:HH], lbs[:, HH:2 * HH], ALU.add)
            dve.drain()
            nc.vector.reciprocal(total, total)
            dve.drain()
            tt(e0, lbs[:, 0:HH], total, ALU.mult)
            tt(e1, lbs[:, HH:2 * HH], total, ALU.mult)
            dve.drain()
            tt(lbs[:, 0:HH], e0, e0, ALU.subtract)
            tt(total, e0, e1, ALU.add)
            dve.drain()
            tt(lbs[:, 2 * HH:3 * HH], total, e0, ALU.subtract)
            dve.drain()
            for i in range(2):
                ts(lbs[:, (2 * i + 1) * HH:(2 * i + 2) * HH], lbs[:, 2 * i * HH:(2 * i + 1) * HH], -1.0, 1.0,
                   ALU.mult, ALU.add)
            for u in range(6, 12):
                unit_sum(u)
            dve.wait_ge(x_loaded, 16)
            dve.wait_ge(P0.sem, P0.at("mods"))
            tt(modn[:, 0:MODS], banks[7][:, 0:MODS], col("ada_b", 0, MODS), ALU.add)
            dve.drain().then_inc(V0.sem, V0.one("mods"))

            def modulated(src, gain_scale, shift, r, V, names):
                for i, name in enumerate(names):
                    half = slice(4 * i, 4 * i + 4)
                    tt(h_t[:, half, :], src[:, half, :], heads(r, 4), ALU.mult)
                    dve.drain()
                    for k in range(4 * i, 4 * i + 4):
                        ins = ts(h_t[:, k, :], h_t[:, k, :], gain_scale[:, k:k + 1], shift[:, k:k + 1],
                                 ALU.mult, ALU.add)
                    ins.then_inc(V.sem, V.one(name))

            def stream_lo(V, A, turn=0):
                for i in range(2):
                    dve.wait_ge(A.sem, A.at(f"h hi{i}", turn))
                    half = slice(4 * i, 4 * i + 4)
                    tt(h_lo[:, half, :], h_t[:, half, :], as_f32(h_hi[:, half, :]), ALU.subtract)\
                        .then_inc(V.sem, V.one(f"h lo{i}"))

            with dve.Fori(0, 2) as l:
                bank = lambda name: bank_of[name]
                nc.vector.tensor_copy(lp[:, :], par[:, bass.ds(l * LP, LP)])
                nc.vector.tensor_copy(lbl[:, :], lbs[:, bass.ds(l * (2 * HH), 2 * HH)])
                nc.vector.tensor_copy(mod[:, :], modn[:, 0:MODS])
                dve.drain()
                stt(amod[:, 0:KT], mod[:, KT:2 * KT], 1.0, lp[:, N1G:N1G + KT], ALU.add, ALU.mult)
                stt(amod[:, KT:2 * KT], mod[:, 4 * KT:5 * KT], 1.0, lp[:, N2G:N2G + KT], ALU.add, ALU.mult)
                dve.drain()
                dve.wait_ge(AC.sem, AC.at("next norm", l - 1))
                modulated(x_t, amod[:, 0:KT], mod[:, 0:KT], rs[:, 0, :], DV, ["h1 0", "h1 1"])
                dve.wait_ge(AC.sem, AC.at("f1", l))
                nc.vector.memset(bwd, 1.0)
                for h in range(HH):
                    ts(fwd[:, h, :], fwd[:, h, :], lbl[:, HH + h:HH + h + 1], lbl[:, h:h + 1], ALU.mult, ALU.add)
                dve.drain()
                ts(kf, fwd, -1.0, 1.0, ALU.mult, ALU.add).then_inc(DV.sem, DV.one("fk"))

                def halves(t, n):
                    return t.rearrange("p h t -> p (h t)").rearrange("p (b two n) -> p b two n", two=2, n=n)

                def weigh(n, i):
                    if n <= 2:
                        tt(qd[i], qf, fwd, ALU.mult)
                        return tt(kd[i], kf, bwd, ALU.mult)
                    s = lambda t, half: halves(t, n)[:, :, half, :]
                    tt(s(qd[i], 1), s(qf, 1), s(fwd, 1), ALU.mult)
                    return tt(s(kd[i], 0), s(kf, 0), s(bwd, 0), ALU.mult)

                def pair_sums(i, first):
                    name = MASKED[i]
                    mask = heads(const("pair")[:, P * i:P * i + P], HH)
                    for t in range(TT):
                        dve.wait_ge(PE.sem, PE.at(f"{name} t{t}", l))
                        out = pairs[t] if first else tmps[t]
                        ins = tt(out, bank(f"{name} t{t}")[:, :].rearrange("p (h n) -> p h n", h=HH),
                                 mask, ALU.mult)
                        if t == 0 or first:
                            ins.then_inc(DV.sem, DV.one(f"{name} t{t}"))
                    dve.drain()
                    if not first:
                        for t in range(TT):
                            ins = tt(pairs[t], pairs[t], tmps[t], ALU.add)
                        ins.then_inc(DV.sem, DV.one(f"{name} t1"))

                dve.drain()
                dve.wait_ge(AC.sem, AC.at("q1", l))
                weigh(1, 1).then_inc(DV.sem, DV.one("qk L1"))
                pair_sums(0, True)
                for i, n in enumerate(LEVELS):
                    f, b = halves(fwd, n), halves(bwd, n)
                    nb = HH * T // (2 * n)
                    wide = lambda ap: ap.broadcast_to([P, nb, n])
                    tt(b[:, :, 0, :], b[:, :, 0, :], wide(f[:, :, 1, n - 1:n]), ALU.mult)
                    dve.drain()
                    tt(f[:, :, 1, :], f[:, :, 1, :], wide(f[:, :, 0, n - 1:n]), ALU.mult)
                    dve.drain()
                    weigh(2 * n, i % 2).then_inc(DV.sem, DV.one(f"qk L{2 * n}"))
                    pair_sums(i + 1, False)
                dve.wait_ge(AC.sem, AC.at("c rs", l))
                tt(cq, cq, heads(rs[:, 0, :], 3), ALU.mult)
                tt(ckv, ckv, heads(rs[:, 1, :], 2), ALU.mult)
                dve.drain()
                for k in range(3):
                    ts(cq[:, k, :], cq[:, k, :], lp[:, QNG + k:QNG + k + 1], None, ALU.mult)
                for k in range(2):
                    ins = ts(ckv[:, k, :], ckv[:, k, :], lp[:, KVNG + k:KVNG + k + 1], None, ALU.mult)
                ins.then_inc(DV.sem, DV.one("cn"))
                dve.wait_ge(AC.sem, AC.at("o rs", l))
                tt(oa, oraw, ors, ALU.mult)
                dve.drain()
                for h in range(HH):
                    ins = stt(oa[:, h, :], oa[:, h, :], lp[:, HGN + h:HGN + h + 1], hgate[:, h, :],
                              ALU.mult, ALU.mult)
                ins.then_inc(DV.sem, DV.one("oa"))
                rows = slice(NOPE, DQK)
                for i in range(4):
                    dve.wait_ge(PE.sem, PE.at(f"q turn{i}", l))
                    q2 = q_a[rows, 2 * i:2 * i + 2, :]
                    t2 = mix[rows, 8192 + 512 * i:8704 + 512 * i].rearrange("p (a b) -> p a b", a=2)
                    tt(t2, bank(f"q turn{i}")[rows, :].rearrange("p (a b) -> p a b", a=2),
                       heads(sin[rows, :], 2), ALU.mult)
                    tt(q2, q2, heads(cos[rows, :], 2), ALU.mult)
                    dve.drain()
                    tt(q2, q2, t2, ALU.add).then_inc(DV.sem, DV.one(f"q turn{i}"))
                dve.wait_ge(PE.sem, PE.at("k turn", l))
                t1 = mix[rows, 8192 + 2048:8192 + 2048 + T]
                tt(t1, bank("k turn")[rows, 0:T], sin[rows, :], ALU.mult)
                tt(krs[rows, :], krs[rows, :], cos[rows, :], ALU.mult)
                dve.drain()
                tt(krs[rows, :], krs[rows, :], t1, ALU.add)
                dve.drain()
                nc.vector.tensor_copy(k_a[rows, :, :], heads(krs[rows, :], NH)).then_inc(DV.sem, DV.one("k turn"))
                future = const("future")
                for g in range(6):
                    scores_dve(nc, dve, bank, PE, DV, l, "", g, DQK ** -0.5,
                               lambda h0, nh, n: heads(future[:, 2 * P - n:2 * P], nh), p_a, nmax[0])
                two = lambda t, i: t[:, 2 * i:2 * i + 2, :]
                half = lambda name: bank(name)[:, :].rearrange("p (a b) -> p a b", a=2)
                for g in range(6):
                    if g < 4:
                        dve.wait_ge(PE.sem, PE.at(f"ya{g}", l))
                        tt(two(h_t, g), half(f"ya{g}"), two(gates, g), ALU.mult).then_inc(DV.sem, DV.one(f"ya{g}"))
                    normed_dve(nc, dve, AC, DV, l, "", g, p_a, sums[0])
                for i in range(4):
                    dve.wait_ge(PE.sem, PE.at(f"yb{i}", l))
                    t2 = view(mix, 5120 + 512 * i, 2, T)
                    tt(t2, half(f"yb{i}"), two(gates, 4 + i), ALU.mult)
                    dve.drain()
                    tt(two(h_t, i), two(h_t, i), t2, ALU.add).then_inc(DV.sem, DV.one(f"yb{i}"))
                for i in range(4):
                    dve.wait_ge(PE.sem, PE.at(f"out{i}", l))
                    for k in (2 * i, 2 * i + 1):
                        ins = stt(x_t[:, k, :], bank(f"out{i}")[:, T * (k % 2):T * (k % 2) + T],
                                  mod[:, 2 * KT + k:2 * KT + k + 1], x_t[:, k, :], ALU.mult, ALU.add)
                    ins.then_inc(DV.sem, DV.one(f"out{i}"))
                dve.wait_ge(AC.sem, AC.at("norm2", l))
                modulated(x_t, amod[:, KT:2 * KT], mod[:, 3 * KT:4 * KT], rs[:, 0, :], DV, H2)
                stream_lo(DV, AC, l)
                dve.wait_ge(AC.sem, AC.at("router", l))
                routing()
                dve.drain().then_inc(DV.sem, DV.one("comb"))
                dve.wait_ge(PE.sem, PE.at("combine", l))
                nc.vector.tensor_copy(combt, bank("combine")[0:NE, 0:T])
                dve.drain()
                ts(pick, combt, ident[0:NE, 0:1], None, ALU.mult)
                dve.drain().then_inc(DV.sem, DV.one("combine"))
                with dve.Fori(0, NE) as it:
                    e = l * NE + it

                    def rest_of_part(j):
                        dve.wait_ge(MA.sem, MA.at(f"hi{j}", e))
                        tt(part_lo(j), moe_raw(j), as_f32(part_hi(j)), ALU.subtract)\
                            .then_inc(MV.sem, MV.one(f"lo{j}"))

                    def hidden(m):
                        dve.wait_ge(MA.sem, MA.at(f"sg{m}", e))
                        tt(tg[:, m, :], sg[:, m, :], banks[6][:, 0:T], ALU.mult)
                        dve.drain()
                        up = banks[4 + m % 2][:, T:2 * T]
                        tt(he_hi[:, m, :], tg[:, m, :], up, ALU.mult)
                        tt(he[:, m, :], tg[:, m, :], up, ALU.mult)
                        dve.drain()
                        tt(he_lo[:, m, :], he[:, m, :], as_f32(he_hi[:, m, :]), ALU.subtract)\
                            .then_inc(MV.sem, MV.one(f"he{m}"))

                    rest_of_part(0)
                    dve.wait_ge(chunk_full, e * 16 + 16)
                    ck = chunk.rearrange("p (k n) -> p k n", k=KT)
                    cs = cact[:, bass.ds(l * KT, KT)].unsqueeze(2).broadcast_to([P, KT, CH])
                    tt(ck, ck, cs, ALU.mult)
                    rest_of_part(1)
                    rest_of_part(2)
                    dve.drain()
                    nc.vector.tensor_reduce(accs, chunk.rearrange("p (k n) -> p n k", k=KT), AX, ALU.add)\
                        .then_inc(MV.sem, MV.one("acc"))
                    rest_of_part(3)
                    rest_of_part(4)
                    hidden(0)
                    rest_of_part(5)
                    dve.wait_ge(MA.sem, MA.at("acc hi", e))
                    tt(acc_split[:, CH:2 * CH], accs, as_f32(acc_split[:, 0:CH]), ALU.subtract)\
                        .then_inc(MV.sem, MV.one("acc lo"))
                    rest_of_part(6)
                    for m in (1, 2):
                        hidden(m)
                        rest_of_part(2 * m + 5)
                        rest_of_part(2 * m + 6)
                    hidden(3)
                    ts(pick, combt, ident[0:NE, bass.ds(it + 1, 1)], None, ALU.mult)\
                        .then_inc(MV.sem, MV.one("next"))
                    dve.wait_ge(MP.sem, MP.at("mods", e))
                    tt(modn[:, bass.ds(it * 3, 3)], banks[7][:, 0:6].rearrange("p (a b) -> p b a", b=2)[:, 0, :],
                       par[:, bass.ds(l * MODS + it * 3 + (COLS["ada_b"][0] + MODS), 3)], ALU.add)\
                        .then_inc(MV.sem, MV.one("mods"))
                    rest_of_part(11)
                dve.wait_ge(MP.sem, MP.at("part11", l * NE + (NE - 1)))
                for k in range(KT):
                    ins = stt(x_t[:, k, :], banks[k // 2][:, T * (k % 2):T * (k % 2) + T],
                              mod[:, 5 * KT + k:5 * KT + k + 1], x_t[:, k, :], ALU.mult, ALU.add)
                    if k % 2:
                        ins.then_inc(DV.sem, DV.one(X2[k // 2]))
                dve.drain()
            def modulation(n1, n2):
                nc.vector.tensor_copy(mod[:, :], modn[:, 0:MODS])
                dve.drain()
                stt(amod[:, 0:KT], mod[:, KT:2 * KT], 1.0, n1, ALU.add, ALU.mult)
                stt(amod[:, KT:2 * KT], mod[:, 4 * KT:5 * KT], 1.0, n2, ALU.add, ALU.mult)
                dve.drain()

            lam0 = col("lam", 0, LN)[LBS, :]
            ts(lam[0][LBS, :], lam0, -1.0, None, ALU.mult)
            dve.drain()
            tt(lam[1][LBS, :], lam[0][LBS, :], lam0, ALU.max).then_inc(VR.sem, VR.one("lambda"))
            modulation(col("n1g2", 0, KT), col("n2g2", 0, KT))
            dve.wait_ge(AC.sem, AC.at("next norm", 1))
            tt(h_t, x_t, heads(rs[:, 0, :], KT), ALU.mult)
            dve.drain()
            for k in range(KT):
                ins = ts(x_t[:, k, :], h_t[:, k, :], col("final_g", k), None, ALU.mult)
                if k % 2:
                    ins.then_inc(VR.sem, VR.one(f"x{k // 2}"))
            dve.wait_ge(AR.sem, AR.at("norm1"))
            modulated(x_t, amod[:, 0:KT], mod[:, 0:KT], rs[:, 0, :], VR, ["h1 0", "h1 1"])
            nc.vector.memset(xr[LBS, :, 0:3], 0.0)
            dve.wait_ge(AR.sem, AR.at("softplus"))
            stt(lam[2][LBS, :], lam[0][LBS, :], 0.0, lam[2][LBS, :], ALU.max, ALU.add)
            dve.drain()
            ts(lam[3][LBS, :], lam[2][LBS, :], 8.0, None, ALU.mult)
            ts(lam[4][LBS, :], lam[2][LBS, :], -8.0, None, ALU.mult)
            for i in range(8):
                dve.wait_ge(AR.sem, AR.at(f"xr{i}"))
                for n in (2 * i, 2 * i + 1):
                    ts(xc[LBS, n, :], xr[LBS, n, 3:T + 3], col("conv_w", 3 * LN + n)[LBS, :],
                       col("conv_b", n)[LBS, :], ALU.mult, ALU.add)
            for tap in (2, 1, 0):
                dve.drain()
                for n in range(LN):
                    ins = stt(xc[LBS, n, :], xr[LBS, n, tap:tap + T], col("conv_w", tap * LN + n)[LBS, :],
                              xc[LBS, n, :], ALU.mult, ALU.add)
            ins.then_inc(VR.sem, VR.one("conv"))
            for i in range(4):
                dve.wait_ge(AR.sem, AR.at(f"ri{4 * i + 3}"))
                g = slice(4 * i, 4 * i + 4)
                tt(ig[LBS, g, :], ig[LBS, g, :], xc[LBS, g, :], ALU.mult).then_inc(VR.sem, VR.one(f"ix{i}"))
            dve.wait_ge(AR.sem, AR.at("decay"))
            for i in range(4):
                g = slice(4 * i, 4 * i + 4)
                dve.drain()
                tt(oa[LBS, :, :], rg[LBS, g, :], rg[LBS, g, :], ALU.mult)
                dve.drain()
                stt(xc[LBS, g, :], oa[LBS, :, :], 1.0, xc[LBS, g, :], ALU.add, ALU.mult)\
                    .then_inc(VR.sem, VR.one(f"u{i}"))
            for i in range(4):
                g = slice(4 * i, 4 * i + 4)
                dve.wait_ge(AR.sem, AR.at(f"root{i}"))
                tt(xc[LBS, g, :], xc[LBS, g, :], ig[LBS, g, :], ALU.mult)
                dve.drain()
                for n in range(4 * i, 4 * i + 4):
                    nc.vector.tensor_tensor_scan(ig[LBS, n, :], rg[LBS, n, :], xc[LBS, n, :], 0.0,
                                                 ALU.mult, ALU.add)
                dve.drain()
                tt(gelu[LBS, g, :], gelu[LBS, g, :], ig[LBS, g, :], ALU.mult).then_inc(VR.sem, VR.one(f"y{i}"))

            def into_x(V, Pj, bank, g1):
                for i in range(4):
                    dve.wait_ge(Pj.sem, Pj.at(f"out{i}"))
                    for k in (2 * i, 2 * i + 1):
                        ins = stt(x_t[:, k, :], bank[f"out{i}"][:, T * (k % 2):T * (k % 2) + T],
                                  g1[:, k:k + 1], x_t[:, k, :], ALU.mult, ALU.add)
                    ins.then_inc(V.sem, V.one(f"out{i}"))

            into_x(VR, PR, r_bank, mod[:, 2 * KT:3 * KT])
            dve.wait_ge(AR.sem, AR.at("norm2"))
            modulated(x_t, amod[:, KT:2 * KT], mod[:, 3 * KT:4 * KT], rs[:, 0, :], VR, H2)
            stream_lo(VR, AR)

            def mlp_dve(layer):
                pe_steps, act_steps_, dve_steps_ = MLP[layer]
                dve.drain().then_inc(dve_steps_.sem, dve_steps_.first)
                with dve.Fori(0, MLP_TURNS // 2) as it:
                    for pair in range(2):
                        e = it * 2 + pair
                        slots = MLP_SLOTS[layer][2 * pair:2 * pair + 2]

                        def rest_of_part(j):
                            dve.wait_ge(act_steps_.sem, act_steps_.at(f"hi{j}", e))
                            tt(part_lo(j), mlp_raw(slots, j), as_f32(part_hi(j)), ALU.subtract)\
                                .then_inc(dve_steps_.sem, dve_steps_.one(f"lo{j}"))

                        for j in range(4):
                            rest_of_part(j)
                            if layer == 0 and j in (1, 3):
                                i = j // 2
                                dve.wait_ge(act_steps_.sem, act_steps_.at(f"mul{i}", e))
                                nc.vector.tensor_reduce(accs2[i], chunks2[i].rearrange("p k n -> p n k"), AX,
                                                        ALU.add)\
                                    .then_inc(dve_steps_.sem, dve_steps_.one(f"acc{i}"))
                        for m in range(4):
                            dve.wait_ge(act_steps_.sem, act_steps_.at(f"g{m}", e))
                            nc.vector.tensor_copy(he_hi[:, m, :], he[:, m, :])
                            dve.drain()
                            tt(he_lo[:, m, :], he[:, m, :], as_f32(he_hi[:, m, :]), ALU.subtract)\
                                .then_inc(dve_steps_.sem, dve_steps_.one(f"he{m}"))
                            rest_of_part(m + 4)
                        if layer == 0:
                            dve.wait_ge(pe_steps.sem, pe_steps.at("mods", e))
                            tt(modn[:, bass.ds(e * 6, 6)], banks[7][:, 0:6],
                               par[:, bass.ds(e * 6 + (COLS["ada_b"][0] + 3 * MODS), 6)], ALU.add)
                            tt(modn[:, bass.ds(e * 2 + MODS, 2)], banks[7][:, 6:8],
                               par[:, bass.ds(e * 2 + COLS["kv_ada_b"][0], 2)], ALU.add)\
                                .then_inc(dve_steps_.sem, dve_steps_.one("mods"))
                dve.wait_ge(pe_steps.sem, pe_steps.at("part7", MLP_TURNS - 1))
                for k in range(KT):
                    ins = stt(x_t[:, k, :], banks[k // 2][:, T * (k % 2):T * (k % 2) + T],
                              mod[:, 5 * KT + k:5 * KT + k + 1], x_t[:, k, :], ALU.mult, ALU.add)
                    if layer == 0 and k % 2:
                        ins.then_inc(VA.sem, VA.one(X2[k // 2]))
                return ins

            mlp_dve(0)
            dve.drain()
            modulation(col("n1g2", KT, KT), col("n2g2", KT, KT))
            stt(akv, modn[:, MODS + KT:MODS + 2 * KT], 1.0, col("kvng2", 0, KT), ALU.add, ALU.mult)
            dve.drain()
            dve.wait_ge(AA.sem, AA.at("norm"))
            modulated(x_t, akv, modn[:, MODS:MODS + KT], rs[:, 0, :], VA, ["h 0", "h 1"])
            tt(hq, x_t, heads(rs[:, 0, :], KT), ALU.mult)
            dve.drain()
            for k in range(KT):
                ins = ts(hq[:, k, :], hq[:, k, :], amod[:, k:k + 1], mod[:, k:k + 1], ALU.mult, ALU.add)
            ins.then_inc(VA.sem, VA.one("hq"))
            bias_a, bias_b = slot(A_SLOT[6], NH2, P), slot(A_SLOT[7], NH2, T)
            for u, ap in ((6, bias_a[0:64, :, 64:P]), (7, bias_b[0:64, :, T - 64:T])):
                dve.wait_ge(ring_full[A_SLOT[u]], 16 * (A_BASE[A_SLOT[u]] + 2))
                nc.vector.memset(ap, NEG)
            dve.drain().then_inc(VA.sem, VA.one("bias"))

            for rows, j in own:
                nc.vector.memset(q2_[rows, :, 1 - j, :], 0.0)
            dve.wait_ge(AA.sem, AA.at("kn rs"))
            stt(k2_, k2_, col("kng"), krs2, ALU.mult, ALU.mult).then_inc(VA.sem, VA.one("k"))
            dve.wait_ge(AA.sem, AA.at("qn rs"))
            for rows, j in own:
                ins = stt(q2_[rows, :, j, :], q2_[rows, :, j, :], col("qng")[rows, :], qrs2[rows, :, :],
                          ALU.mult, ALU.mult)
            ins.then_inc(VA.sem, VA.one("q"))

            def scores(half, g):
                scores_dve(nc, dve, lambda n: a_bank[n], PA, VA, 0, ("A ", "B ")[half], g, HD ** -0.5,
                           lambda h0, nh, n: (bias_a if n == P else bias_b)[:, 8 * half + h0:8 * half + h0 + nh, :],
                           p2_[half], nmax[half])

            for g in range(6):
                scores(0, g)
            for g in range(6):
                normed_dve(nc, dve, AA, VA, 0, "A ", g, p2_[0], sums[0])
                scores(1, g)
            for g in range(6):
                normed_dve(nc, dve, AA, VA, 0, "B ", g, p2_[1], sums[1])
            into_x(VA, PA, a_bank, mod[:, 2 * KT:3 * KT])
            dve.wait_ge(AA.sem, AA.at("norm2"))
            modulated(x_t, amod[:, KT:2 * KT], mod[:, 3 * KT:4 * KT], rs[:, 0, :], VA, H2)
            stream_lo(VA, AA)
            mlp_dve(1).then_inc(VA.sem, VA.one("x"))


def shape_constants():
    con = np.zeros((P, NCONST), np.float32)
    def put(name, v):
        con[:v.shape[0], CONST[name][0]:CONST[name][0] + v.shape[1]] = v

    put("ident", np.eye(P, dtype=np.float32))
    put("ones", np.ones((P, P), np.float32))
    put("heads", np.kron(np.eye(2, dtype=np.float32), np.ones((HD, HD), np.float32)))
    turn = np.zeros((P, DQK), np.float32)
    half = ROPE // 2
    for i in range(half):
        turn[NOPE + half + i, NOPE + i] = -1.0
        turn[NOPE + i, NOPE + half + i] = 1.0
    put("turn", turn)
    s, t = np.arange(P)[:, None], np.arange(P)[None, :]
    masks = [s == t] + [(s // (2 * n) == t // (2 * n)) & (s // n % 2 == 0) & (t // n % 2 == 1) for n in LEVELS]
    put("pair", np.concatenate([m.astype(np.float32) * np.float32(DK ** -0.5) for m in masks], 1))
    future = np.zeros((P, 2 * P), np.float32)
    future[:64, P + 64:] = NEG
    put("future", future)
    freq = (np.float32(10000.0) ** (-np.arange(half, dtype=np.float32) / np.float32(half))).astype(np.float32)
    put("freq", np.tile(freq, P // half)[:, None])
    return con


def columns(v):
    return v.reshape(-1, P).T


def kernel(**inputs):
    import concourse.bacc as bacc
    from concourse.bass_utils import run_bass_kernel_spmd

    a = {k: np.asarray(v) for k, v in inputs.items()}
    cols = np.zeros((P, NCOLS), np.float32)

    def put(name, v):
        cols[:v.shape[0], COLS[name][0]:COLS[name][0] + v.shape[1]] = v

    put("layer", np.concatenate([columns(a[n][l]) for l in range(2) for n in
                                 ("norm1_g", "hg_norm_g", "q_norm_g", "kv_norm_g", "norm2_g")], 1))
    put("lb", columns(a["hg_lb_logits"]))
    put("ada_b", np.concatenate([columns(a["ada_b"]), columns(a["ada_b_2"])], 1))
    put("kv_ada_b", columns(a["kv_ada_b_2"]))
    put("c", np.concatenate([columns(a["c"]), columns(a["c_2"])], 1))
    put("final_g", columns(a["final_g"]))
    put("n1g2", columns(a["norm1_g_2"]))
    put("n2g2", columns(a["norm2_g_2"]))
    put("kvng2", columns(a["kv_norm_g_2"]))
    put("kng", columns(np.tile(a["k_norm_g_2"], 2)))
    put("qng", columns(np.tile(a["q_norm_g_2"][0], 2)))
    put("conv_w", a["lru_conv_w_2"][0].reshape(4 * LN, LB).T)
    for name, v in (("conv_b", "lru_conv_b_2"), ("ba", "lru_gate_a_b_2"), ("bx", "lru_gate_x_b_2"), ("lam", "lru_lambda_2")):
        put(name, a[v][0].reshape(LN, LB).T)
    rb = a["rel_bias_2"][0]
    ext = np.concatenate([np.repeat(rb[:, 256:257], 127, 1), rb[:, ::-1], np.repeat(rb[:, 0:1], 128, 1)], 1)
    arrays = {
        "x": np.ascontiguousarray(a["x"][0].T.reshape(KT, P, T).transpose(1, 0, 2)),
        "positions": a["positions"],
        "cols": cols,
        "consts": shape_constants(),
        "ext": np.ascontiguousarray(ext),
        "ada": np.concatenate([a["ada_w"], a["ada_w_2"]], 0),
        "w_router": a["w_router"], "router_bias": a["router_bias"],
    }
    for n in ("w_in", "w_q_up", "w_kv_up", "w_br_a", "w_br_b", "w_out", "w_gate", "w_up", "w_down",
              "mlp_w1_2", "mlp_w2_2", "lru_w_in_2", "lru_gate_a_w_2", "lru_gate_x_w_2", "lru_w_out_2",
              "kv_ada_w_2", "kv_w_2", "attn_w_q_2", "attn_w_o_2"):
        arrays[n] = np.ascontiguousarray(a[n])
    nc = bacc.Bacc("TRN2", target_bir_lowering=False, num_devices=1)
    w = {n: nc.dram_tensor("in_" + n, v.shape, mybir.dt.from_np(v.dtype), kind="ExternalInput").ap()
         for n, v in arrays.items()}
    w["out"] = nc.dram_tensor("out", (P, KT, T), F32, kind="ExternalOutput").ap()
    program(nc, w["x"], w["positions"], w["cols"], w["consts"], w["ext"], w)
    r = run_bass_kernel_spmd(nc, [{"in_" + n: v for n, v in arrays.items()}], core_ids=[0])
    out = np.asarray(r.results[0]["out"])
    return out.transpose(2, 1, 0).reshape(1, T, D)
```
